# Optimizing a Trainium2 kernel written in Bass

```python
import math
import jax, jax.numpy as jnp
from jax import lax
import numpy as np

D_MODEL = 1024
BATCH = 1
SEQ = 256
DEPTH = 2

N_HEADS = 16
HEAD_DIM = D_MODEL // N_HEADS
MOBA_BLOCK = 256
MOBA_TOPK = 3
Q_CHUNK = 32
ROPE_THETA = 10000.0
RWKV_HEAD = 64
RWKV_HEADS = D_MODEL // RWKV_HEAD
DECAY_LORA = 64
AAA_LORA = 64
GATE_LORA = 128
LNX_EPS = 64e-5
D_FF = ((8 * D_MODEL // 3 + 127) // 128) * 128
CONV_WIDTH = 3
N_MIXERS = 2
N_ATTN_LAYERS = (DEPTH + N_MIXERS - 1) // N_MIXERS
N_RWKV_LAYERS = DEPTH // N_MIXERS
RMS_EPS = 1e-6


def rms_norm(x, g):
    xf = x.astype(jnp.float32)
    y = xf * lax.rsqrt(jnp.mean(xf * xf, axis=-1, keepdims=True) + RMS_EPS)
    return (y * g.astype(jnp.float32)).astype(x.dtype)

def rope_tables(seq):
    inv = 1.0 / (ROPE_THETA ** (jnp.arange(0, HEAD_DIM, 2, dtype=jnp.float32) / HEAD_DIM))
    ang = jnp.arange(seq, dtype=jnp.float32)[:, None] * inv[None, :]
    ang = jnp.concatenate([ang, ang], axis=-1)
    return jnp.cos(ang), jnp.sin(ang)

def apply_rope(t, cos, sin):
    half = HEAD_DIM // 2
    rot = jnp.concatenate([-t[..., half:], t[..., :half]], axis=-1)
    return t * cos.astype(t.dtype) + rot * sin.astype(t.dtype)

def moba_attention(x, w_qkv, w_o, cos, sin):
    B, S, D = x.shape
    H, Dh = N_HEADS, HEAD_DIM
    qkv = x @ w_qkv
    q, k, v = jnp.split(qkv, 3, axis=-1)
    to_heads = lambda t: t.reshape(B, S, H, Dh).transpose(0, 2, 1, 3)
    q = apply_rope(to_heads(q), cos, sin)
    k = apply_rope(to_heads(k), cos, sin)
    v = to_heads(v)
    scale = 1.0 / math.sqrt(Dh)

    nb = -(-S // MOBA_BLOCK)
    pad = nb * MOBA_BLOCK - S
    kb = jnp.pad(k, ((0, 0), (0, 0), (0, pad), (0, 0))).reshape(B, H, nb, MOBA_BLOCK, Dh)
    vb = jnp.pad(v, ((0, 0), (0, 0), (0, pad), (0, 0))).reshape(B, H, nb, MOBA_BLOCK, Dh)

    kmean = jnp.mean(kb.astype(jnp.float32), axis=3)
    gate = jnp.einsum('bhsd,bhnd->bhsn', q.astype(jnp.float32), kmean)
    qblk = jnp.arange(S) // MOBA_BLOCK
    past = jnp.arange(nb)[None, :] < qblk[:, None]
    gate = jnp.where(past, gate, -jnp.inf)
    k_sel = min(MOBA_TOPK, nb)
    _, gidx = lax.top_k(gate, k_sel)
    gvalid = gidx < qblk[:, None]

    bi = jnp.arange(B)[:, None, None, None]
    hi = jnp.arange(H)[None, :, None, None]

    def chunk(c):
        s0 = c * Q_CHUNK
        qc = lax.dynamic_slice_in_dim(q, s0, Q_CHUNK, axis=2)
        idc = lax.dynamic_slice_in_dim(gidx, s0, Q_CHUNK, axis=2)
        vdc = lax.dynamic_slice_in_dim(gvalid, s0, Q_CHUNK, axis=2)
        kg = kb[bi, hi, idc]
        vg = vb[bi, hi, idc]
        s_sel = jnp.einsum('bhqd,bhqjtd->bhqjt', qc, kg) * scale
        s_sel = jnp.where(vdc[..., None], s_sel, -jnp.inf)
        s_sel = s_sel.reshape(B, H, Q_CHUNK, k_sel * MOBA_BLOCK)
        own = s0 // MOBA_BLOCK
        ko = lax.dynamic_index_in_dim(kb, own, axis=2, keepdims=False)
        vo = lax.dynamic_index_in_dim(vb, own, axis=2, keepdims=False)
        s_own = jnp.einsum('bhqd,bhtd->bhqt', qc, ko) * scale
        qpos = s0 + jnp.arange(Q_CHUNK)
        kpos = own * MOBA_BLOCK + jnp.arange(MOBA_BLOCK)
        s_own = jnp.where(kpos[None, :] <= qpos[:, None], s_own, -jnp.inf)
        s_all = jnp.concatenate([s_sel, s_own], axis=-1).astype(jnp.float32)
        p = jax.nn.softmax(s_all, axis=-1).astype(v.dtype)
        p_sel = p[..., :k_sel * MOBA_BLOCK].reshape(B, H, Q_CHUNK, k_sel, MOBA_BLOCK)
        p_own = p[..., k_sel * MOBA_BLOCK:]
        return (jnp.einsum('bhqjt,bhqjtd->bhqd', p_sel, vg)
                + jnp.einsum('bhqt,bhtd->bhqd', p_own, vo))

    out = lax.map(chunk, jnp.arange(S // Q_CHUNK))
    out = out.transpose(1, 0, 3, 2, 4).reshape(B, S, D)
    return out @ w_o

def rwkv7_time_mix(x, mu, w_rkv, w0, w1, w2, a0, a1, a2, g1, g2, k_k, k_a, r_k,
                   lnx_w, lnx_b, w_o):
    B, S, D = x.shape
    H, N = RWKV_HEADS, RWKV_HEAD
    f32 = jnp.float32
    x_prev = jnp.pad(x[:, :-1], ((0, 0), (1, 0), (0, 0)))
    xx = x_prev - x
    xr, xw, xk, xv, xa, xg = [x + xx * mu[n] for n in range(6)]
    rkv = jnp.einsum('nbsd,nde->nbse', jnp.stack([xr, xk, xv]), w_rkv)
    r, k, v = rkv[0], rkv[1], rkv[2]
    w = -jax.nn.softplus(-(w0 + jnp.tanh(xw @ w1) @ w2).astype(f32)) - 0.5
    decay = jnp.exp(-jnp.exp(w))
    a = jax.nn.sigmoid((a0 + (xa @ a1) @ a2).astype(f32))
    g = jax.nn.sigmoid(xg @ g1) @ g2

    heads = lambda t: t.astype(f32).reshape(B, S, H, N)
    r, k, v, decay, a = heads(r), heads(k), heads(v), heads(decay), heads(a)
    kk = k * k_k.astype(f32).reshape(H, N)
    kk = kk / jnp.maximum(jnp.sqrt(jnp.sum(kk * kk, axis=-1, keepdims=True)), 1e-12)
    k = k * (1.0 + (a - 1.0) * k_a.astype(f32).reshape(H, N))

    def step(state, inp):
        r_t, w_t, k_t, v_t, kk_t, a_t = inp
        sa = jnp.einsum('bhvk,bhk->bhv', state, -kk_t)
        state = (state * w_t[:, :, None, :]
                 + sa[..., None] * (kk_t * a_t)[:, :, None, :]
                 + v_t[..., None] * k_t[:, :, None, :])
        y = jnp.einsum('bhvk,bhk->bhv', state, r_t)
        return state, y

    tm = lambda t: jnp.swapaxes(t, 0, 1)
    _, y = lax.scan(step, jnp.zeros((B, H, N, N), f32),
                    (tm(r), tm(decay), tm(k), tm(v), tm(kk), tm(a)))
    y = jnp.swapaxes(y, 0, 1)
    mean = jnp.mean(y, axis=-1, keepdims=True)
    var = jnp.mean(jnp.square(y - mean), axis=-1, keepdims=True)
    yn = ((y - mean) * lax.rsqrt(var + LNX_EPS)).reshape(B, S, D)
    yn = yn * lnx_w.astype(f32) + lnx_b.astype(f32)
    bonus = (jnp.sum(r * k * r_k.astype(f32), axis=-1, keepdims=True) * v).reshape(B, S, D)
    return ((yn + bonus).astype(x.dtype) * g) @ w_o

def conv_ffn(x, w_gate, w_up, conv_w, conv_b, w_down):
    gt = x @ w_gate
    gt = lax.conv_general_dilated(
        gt, conv_w[:, None, :].astype(gt.dtype), window_strides=(1,),
        padding=[(CONV_WIDTH - 1, 0)], dimension_numbers=('NWC', 'WIO', 'NWC'),
        feature_group_count=gt.shape[-1]) + conv_b
    return (jax.nn.silu(gt) * (x @ w_up)) @ w_down

def first_inputs(seed: int = 0) -> dict:
    key = jax.random.key(seed)
    ks = iter(jax.random.split(key, 40))
    nrm = lambda shape, s: jax.random.normal(next(ks), shape, jnp.float32) * s
    D, F, H, N = D_MODEL, D_FF, RWKV_HEADS, RWKV_HEAD
    NA, NR = N_ATTN_LAYERS, N_RWKV_LAYERS
    return {
        'x': nrm((BATCH, SEQ, D), 1.0),
        'norm_mix': 1.0 + nrm((DEPTH, D), 0.02),
        'norm_ffn': 1.0 + nrm((DEPTH, D), 0.02),
        'norm_final': 1.0 + nrm((D,), 0.02),
        'attn_w_qkv': nrm((NA, D, 3 * D), D ** -0.5),
        'attn_w_o': nrm((NA, D, D), D ** -0.5),
        'rwkv_mu': jax.random.uniform(next(ks), (NR, 6, D), jnp.float32),
        'rwkv_w_rkv': nrm((NR, 3, D, D), D ** -0.5),
        'rwkv_w0': -1.0 + nrm((NR, D), 0.5),
        'rwkv_w1': nrm((NR, D, DECAY_LORA), D ** -0.5),
        'rwkv_w2': nrm((NR, DECAY_LORA, D), 0.5 * DECAY_LORA ** -0.5),
        'rwkv_a0': nrm((NR, D), 0.1),
        'rwkv_a1': nrm((NR, D, AAA_LORA), D ** -0.5),
        'rwkv_a2': nrm((NR, AAA_LORA, D), 0.5 * AAA_LORA ** -0.5),
        'rwkv_g1': nrm((NR, D, GATE_LORA), D ** -0.5),
        'rwkv_g2': nrm((NR, GATE_LORA, D), GATE_LORA ** -0.5),
        'rwkv_k_k': 0.85 + nrm((NR, D), 0.05),
        'rwkv_k_a': 1.0 + nrm((NR, D), 0.05),
        'rwkv_r_k': nrm((NR, H, N), 0.1),
        'rwkv_lnx_w': 1.0 + nrm((NR, D), 0.02),
        'rwkv_lnx_b': nrm((NR, D), 0.02),
        'rwkv_w_o': nrm((NR, D, D), D ** -0.5),
        'ffn_w_gate': nrm((DEPTH, D, F), D ** -0.5),
        'ffn_w_up': nrm((DEPTH, D, F), D ** -0.5),
        'ffn_conv_w': nrm((DEPTH, CONV_WIDTH, F), CONV_WIDTH ** -0.5),
        'ffn_conv_b': nrm((DEPTH, F), 0.02),
        'ffn_w_down': nrm((DEPTH, F, D), F ** -0.5),
    }

def first_block(x, norm_mix, norm_ffn, norm_final, attn_w_qkv, attn_w_o,
              rwkv_mu, rwkv_w_rkv, rwkv_w0, rwkv_w1, rwkv_w2, rwkv_a0, rwkv_a1,
              rwkv_a2, rwkv_g1, rwkv_g2, rwkv_k_k, rwkv_k_a, rwkv_r_k,
              rwkv_lnx_w, rwkv_lnx_b, rwkv_w_o,
              ffn_w_gate, ffn_w_up, ffn_conv_w, ffn_conv_b, ffn_w_down):
    S = x.shape[1]
    cos, sin = rope_tables(S)
    h = x
    for i in range(DEPTH):
        xn = rms_norm(h, norm_mix[i])
        j = i // N_MIXERS
        if i % N_MIXERS == 0:
            h = h + moba_attention(xn, attn_w_qkv[j], attn_w_o[j], cos, sin)
        else:
            h = h + rwkv7_time_mix(
                xn, rwkv_mu[j], rwkv_w_rkv[j], rwkv_w0[j], rwkv_w1[j], rwkv_w2[j],
                rwkv_a0[j], rwkv_a1[j], rwkv_a2[j], rwkv_g1[j], rwkv_g2[j],
                rwkv_k_k[j], rwkv_k_a[j], rwkv_r_k[j], rwkv_lnx_w[j], rwkv_lnx_b[j],
                rwkv_w_o[j])
        h = h + conv_ffn(rms_norm(h, norm_ffn[i]), ffn_w_gate[i], ffn_w_up[i],
                         ffn_conv_w[i], ffn_conv_b[i], ffn_w_down[i])
    return rms_norm(h, norm_final)


_first_inputs = first_inputs


def first_inputs(seed=0):
    import zlib

    import numpy as np

    out = dict(_first_inputs(seed))
    spreads = {}
    factors = {'norm_mix': 2.684,
     'norm_final': 9.023,
     'rwkv_k_k': 37.85,
     'rwkv_lnx_w': 25.426,
     'rwkv_lnx_b': 25.843,
     'ffn_conv_b': 3.569,
     'norm_ffn': 4.052}
    for name, (base, spread) in spreads.items():
        noise = np.random.default_rng([zlib.crc32(name.encode()), seed]).standard_normal(out[name].shape)
        drawn = base * np.exp(spread * noise) if base else spread * noise
        out[name] = __import__('jax').numpy.asarray(drawn.astype(out[name].dtype))
    for name, factor in factors.items():
        out[name] = (out[name] * factor).astype(out[name].dtype)
    return out


_narrow_inputs = first_inputs


def first_inputs(seed=0):

    out = dict(_narrow_inputs(seed))
    wider = {'norm_final': 3.38, 'rwkv_k_k': 4.82, 'rwkv_lnx_w': 3.63, 'rwkv_lnx_b': 3.68}
    for name, times in wider.items():
        mean = out[name].mean()
        out[name] = (mean + times * (out[name] - mean)).astype(out[name].dtype)
    return out


CHUNK = 64
Q_BLOCK = 128
D_MIX = D_MODEL
LRU_WIDTH = D_MIX // 2
LRU_BLOCKS = 8
LRU_BLOCK_W = LRU_WIDTH // LRU_BLOCKS
CONV_W = 4
RG_C = 8.0
ATTN_WIDTH = D_MIX - LRU_WIDTH
DIFF_HEADS = 4
DIFF_VDIM = ATTN_WIDTH // DIFF_HEADS
DIFF_DH = DIFF_VDIM // 2
D_IN = 2 * LRU_WIDTH + 3 * ATTN_WIDTH
D_FF_2 = 3 * D_MODEL
N_EXPERTS = 8
TOP_K = 2
N_DENSE = (DEPTH + 1) // 2
N_MOE = DEPTH // 2
EPS = 1e-6
MAX_OFFSET_CHUNKS = 64


def rmsnorm(x, g):
    x32 = x.astype(jnp.float32)
    y = x32 * lax.rsqrt(jnp.mean(x32 * x32, axis=-1, keepdims=True) + EPS)
    return y.astype(x.dtype) * g

def rope5(x, pos):
    inv = ROPE_THETA ** (-jnp.arange(0, DIFF_DH, 2, dtype=jnp.float32) / DIFF_DH)
    ang = pos.astype(jnp.float32)[..., None] * inv
    ang = jnp.concatenate([ang, ang], axis=-1)[:, :, None, None, :]
    cos, sin = jnp.cos(ang), jnp.sin(ang)
    x1, x2 = jnp.split(x, 2, axis=-1)
    rot = jnp.concatenate([-x2, x1], axis=-1)
    return (x * cos + rot * sin).astype(x.dtype)

def causal_conv(x, w, b):
    rhs = w[:, None, :]
    y = lax.conv_general_dilated(x, rhs, window_strides=(1,), padding=[(CONV_W - 1, 0)],
                                 dimension_numbers=('NWC', 'WIO', 'NWC'),
                                 feature_group_count=x.shape[-1])
    return y + b

def _lin_rec(e1, e2):
    a1, b1 = e1
    a2, b2 = e2
    return a1 * a2, a2 * b1 + b2

def rg_lru(x, wa, ba, wx, bx, lam):
    B, S, W = x.shape
    xb = x.reshape(B, S, LRU_BLOCKS, LRU_BLOCK_W)
    r = jax.nn.sigmoid(jnp.einsum('bsnh,nhk->bsnk', xb, wa).reshape(B, S, W) + ba)
    i = jax.nn.sigmoid(jnp.einsum('bsnh,nhk->bsnk', xb, wx).reshape(B, S, W) + bx)
    log_a = -RG_C * r.astype(jnp.float32) * jax.nn.softplus(-lam.astype(jnp.float32))
    a = jnp.exp(log_a)
    mult = jnp.sqrt(-jnp.expm1(2.0 * log_a))
    bt = mult * (i * x).astype(jnp.float32)
    _, h = lax.associative_scan(_lin_rec, (a, bt), axis=1)
    return h.astype(x.dtype)

def diff_attention(q, k, v, pos, lq1, lk1, lq2, lk2, subln_g, lambda_init):
    B, S, _ = q.shape
    q = rope5(q.reshape(B, S, DIFF_HEADS, 2, DIFF_DH), pos)
    k = rope5(k.reshape(B, S, DIFF_HEADS, 2, DIFF_DH), pos)
    v = v.reshape(B, S, DIFF_HEADS, DIFF_VDIM)
    lam = (jnp.exp(jnp.sum(lq1.astype(jnp.float32) * lk1.astype(jnp.float32)))
           - jnp.exp(jnp.sum(lq2.astype(jnp.float32) * lk2.astype(jnp.float32)))
           + lambda_init)
    chunk = pos // CHUNK
    nqb = S // Q_BLOCK
    qs = q.reshape(B, nqb, Q_BLOCK, DIFF_HEADS, 2, DIFF_DH).transpose(1, 0, 3, 4, 2, 5)
    qc = chunk.reshape(B, nqb, Q_BLOCK).transpose(1, 0, 2)
    kt = k.transpose(0, 2, 3, 1, 4)
    vt = v.transpose(0, 2, 1, 3)
    scale = DIFF_DH ** -0.5
    neg = jnp.finfo(jnp.float32).min

    def attend(args):
        qb, qcb = args
        s = jnp.einsum('bhcqd,bhckd->bhcqk', qb, kt).astype(jnp.float32) * scale
        mask = (chunk[:, None, :] <= qcb[:, :, None])[:, None, None]
        p = jax.nn.softmax(jnp.where(mask, s, neg), axis=-1)
        pd = p[:, :, 0] - lam * p[:, :, 1]
        return jnp.einsum('bhqk,bhkd->bhqd', pd.astype(vt.dtype), vt)

    o = lax.map(attend, (qs, qc))
    o = o.transpose(1, 0, 3, 2, 4).reshape(B, S, DIFF_HEADS, DIFF_VDIM)
    o = rmsnorm(o, subln_g) * (1.0 - lambda_init)
    return o.reshape(B, S, ATTN_WIDTH)

def swiglu(h, wg, wu, wd):
    return (jax.nn.silu(h @ wg) * (h @ wu)) @ wd

def moe(h, router, wg, wu, wd):
    logits = (h @ router).astype(jnp.float32)
    vals, idx = lax.top_k(logits, TOP_K)
    w = jax.nn.softmax(vals, axis=-1)
    gates = jnp.sum(jax.nn.one_hot(idx, N_EXPERTS, dtype=jnp.float32) * w[..., None], axis=-2)
    y = jnp.zeros_like(h)
    for e in range(N_EXPERTS):
        y = y + gates[..., e:e + 1].astype(h.dtype) * swiglu(h, wg[e], wu[e], wd[e])
    return y

def second_inputs(seed: int = 0) -> dict:
    key = jax.random.key(seed)
    ks = iter(jax.random.split(key, 40))
    f32 = jnp.float32

    def nrm(shape, scale):
        return jax.random.normal(next(ks), shape, f32) * scale

    a0 = jax.random.uniform(next(ks), (DEPTH, LRU_WIDTH), f32, 0.9, 0.999)
    s0 = a0 ** (1.0 / RG_C)
    lru_lambda = jnp.log(s0) - jnp.log1p(-s0)
    offsets = jax.random.randint(next(ks), (BATCH, 1), 0, MAX_OFFSET_CHUNKS) * CHUNK
    positions = (offsets + jnp.arange(SEQ, dtype=jnp.int32)[None, :]).astype(jnp.int32)
    return {
        'x': nrm((BATCH, SEQ, D_MODEL), 1.0),
        'c': nrm((BATCH, D_MODEL), 1.0),
        'positions': positions,
        'ada_w': nrm((DEPTH, D_MODEL, 6 * D_MODEL), 0.5 * D_MODEL ** -0.5),
        'ada_b': nrm((DEPTH, 6 * D_MODEL), 0.02),
        'ln1_g': 1.0 + nrm((DEPTH, D_MODEL), 0.02),
        'ln2_g': 1.0 + nrm((DEPTH, D_MODEL), 0.02),
        'w_in': nrm((DEPTH, D_MODEL, D_IN), D_MODEL ** -0.5),
        'conv_w': nrm((DEPTH, CONV_W, LRU_WIDTH), CONV_W ** -0.5),
        'conv_b': nrm((DEPTH, LRU_WIDTH), 0.02),
        'gate_a_w': nrm((DEPTH, LRU_BLOCKS, LRU_BLOCK_W, LRU_BLOCK_W), LRU_BLOCK_W ** -0.5),
        'gate_a_b': nrm((DEPTH, LRU_WIDTH), 0.02),
        'gate_x_w': nrm((DEPTH, LRU_BLOCKS, LRU_BLOCK_W, LRU_BLOCK_W), LRU_BLOCK_W ** -0.5),
        'gate_x_b': nrm((DEPTH, LRU_WIDTH), 0.02),
        'lru_lambda': lru_lambda,
        'lam_q1': nrm((DEPTH, DIFF_DH), 0.1),
        'lam_k1': nrm((DEPTH, DIFF_DH), 0.1),
        'lam_q2': nrm((DEPTH, DIFF_DH), 0.1),
        'lam_k2': nrm((DEPTH, DIFF_DH), 0.1),
        'subln_g': 1.0 + nrm((DEPTH, DIFF_VDIM), 0.02),
        'w_out': nrm((DEPTH, D_MIX, D_MODEL), D_MIX ** -0.5),
        'ffn_w_gate': nrm((N_DENSE, D_MODEL, D_FF_2), D_MODEL ** -0.5),
        'ffn_w_up': nrm((N_DENSE, D_MODEL, D_FF_2), D_MODEL ** -0.5),
        'ffn_w_down': nrm((N_DENSE, D_FF_2, D_MODEL), D_FF_2 ** -0.5),
        'moe_router': nrm((N_MOE, D_MODEL, N_EXPERTS), D_MODEL ** -0.5),
        'moe_w_gate': nrm((N_MOE, N_EXPERTS, D_MODEL, D_FF_2), D_MODEL ** -0.5),
        'moe_w_up': nrm((N_MOE, N_EXPERTS, D_MODEL, D_FF_2), D_MODEL ** -0.5),
        'moe_w_down': nrm((N_MOE, N_EXPERTS, D_FF_2, D_MODEL), D_FF_2 ** -0.5),
        'final_g': 1.0 + nrm((D_MODEL,), 0.02),
    }

def second_block(x, c, positions, ada_w, ada_b, ln1_g, ln2_g, w_in, conv_w, conv_b,
              gate_a_w, gate_a_b, gate_x_w, gate_x_b, lru_lambda, lam_q1, lam_k1,
              lam_q2, lam_k2, subln_g, w_out, ffn_w_gate, ffn_w_up, ffn_w_down,
              moe_router, moe_w_gate, moe_w_up, moe_w_down, final_g):
    splits = [LRU_WIDTH, 2 * LRU_WIDTH, 2 * LRU_WIDTH + ATTN_WIDTH, 2 * LRU_WIDTH + 2 * ATTN_WIDTH]
    for l in range(DEPTH):
        lambda_init = 0.8 - 0.6 * math.exp(-0.3 * l)
        mod = jax.nn.silu(c) @ ada_w[l] + ada_b[l]
        sh1, sc1, g1, sh2, sc2, g2 = jnp.split(mod[:, None, :], 6, axis=-1)
        h = rmsnorm(x, ln1_g[l]) * (1.0 + sc1) + sh1
        z = h @ w_in[l]
        xr, yr, q, k, v = jnp.split(z, splits, axis=-1)
        lru = rg_lru(causal_conv(xr, conv_w[l], conv_b[l]), gate_a_w[l], gate_a_b[l],
                     gate_x_w[l], gate_x_b[l], lru_lambda[l]) * jax.nn.gelu(yr)
        att = diff_attention(q, k, v, positions, lam_q1[l], lam_k1[l], lam_q2[l], lam_k2[l],
                             subln_g[l], lambda_init)
        x = x + g1 * (jnp.concatenate([lru, att], axis=-1) @ w_out[l])
        h = rmsnorm(x, ln2_g[l]) * (1.0 + sc2) + sh2
        if l % 2 == 0:
            j = l // 2
            f = swiglu(h, ffn_w_gate[j], ffn_w_up[j], ffn_w_down[j])
        else:
            j = l // 2
            f = moe(h, moe_router[j], moe_w_gate[j], moe_w_up[j], moe_w_down[j])
        x = x + g2 * f
    return rmsnorm(x, final_g)


def setup_inputs(seed=0):
    out = dict(first_inputs(seed))
    for name, value in second_inputs(seed + 1).items():
        if name != "x":
            out[name + "_2"] = value
    return out


def reference(
    x, norm_mix, norm_ffn, norm_final, attn_w_qkv, attn_w_o, rwkv_mu, rwkv_w_rkv, rwkv_w0,
    rwkv_w1, rwkv_w2, rwkv_a0, rwkv_a1, rwkv_a2, rwkv_g1, rwkv_g2, rwkv_k_k, rwkv_k_a, rwkv_r_k,
    rwkv_lnx_w, rwkv_lnx_b, rwkv_w_o, ffn_w_gate, ffn_w_up, ffn_conv_w, ffn_conv_b, ffn_w_down,
    c_2, positions_2, ada_w_2, ada_b_2, ln1_g_2, ln2_g_2, w_in_2, conv_w_2, conv_b_2,
    gate_a_w_2, gate_a_b_2, gate_x_w_2, gate_x_b_2, lru_lambda_2, lam_q1_2, lam_k1_2, lam_q2_2,
    lam_k2_2, subln_g_2, w_out_2, ffn_w_gate_2, ffn_w_up_2, ffn_w_down_2, moe_router_2,
    moe_w_gate_2, moe_w_up_2, moe_w_down_2, final_g_2,
):
    x = first_block(
        x, norm_mix, norm_ffn, norm_final, attn_w_qkv, attn_w_o, rwkv_mu, rwkv_w_rkv, rwkv_w0,
        rwkv_w1, rwkv_w2, rwkv_a0, rwkv_a1, rwkv_a2, rwkv_g1, rwkv_g2, rwkv_k_k, rwkv_k_a,
        rwkv_r_k, rwkv_lnx_w, rwkv_lnx_b, rwkv_w_o, ffn_w_gate, ffn_w_up, ffn_conv_w,
        ffn_conv_b, ffn_w_down,
    )
    return second_block(
        x, c_2, positions_2, ada_w_2, ada_b_2, ln1_g_2, ln2_g_2, w_in_2, conv_w_2, conv_b_2,
        gate_a_w_2, gate_a_b_2, gate_x_w_2, gate_x_b_2, lru_lambda_2, lam_q1_2, lam_k1_2,
        lam_q2_2, lam_k2_2, subln_g_2, w_out_2, ffn_w_gate_2, ffn_w_up_2, ffn_w_down_2,
        moe_router_2, moe_w_gate_2, moe_w_up_2, moe_w_down_2, final_g_2,
    )


_drawn_inputs = setup_inputs


def setup_inputs(seed=0):
    import zlib

    import numpy as np

    out = dict(_drawn_inputs(seed))
    spreads = {}
    factors = {'ada_b_2': 8.0,
     'ln1_g_2': 8.0,
     'ln2_g_2': 8.0,
     'conv_b_2': 64.0,
     'gate_a_w_2': 64.0,
     'gate_a_b_2': 64.0,
     'gate_x_w_2': 48.984,
     'gate_x_b_2': 64.0,
     'lru_lambda_2': 63.072,
     'lam_q1_2': 8.0,
     'lam_k1_2': 8.0,
     'lam_q2_2': 8.0,
     'lam_k2_2': 8.0,
     'subln_g_2': 8.0,
     'moe_router_2': 3.509,
     'moe_w_gate_2': 3.381,
     'moe_w_up_2': 3.159,
     'moe_w_down_2': 3.151,
     'final_g_2': 8.39,
     'conv_w_2': 8.0}
    for name, (base, spread) in spreads.items():
        noise = np.random.default_rng([zlib.crc32(name.encode()), seed]).standard_normal(out[name].shape)
        drawn = base * np.exp(spread * noise) if base else spread * noise
        out[name] = __import__('jax').numpy.asarray(drawn.astype(out[name].dtype))
    for name, factor in factors.items():
        out[name] = (out[name] * factor).astype(out[name].dtype)
    return out
```

```python
from contextlib import ExitStack
import math

import numpy as np

import concourse.bass as bass
from concourse import mybir

F32 = mybir.dt.float32
F32R = mybir.dt.float32r
I32 = mybir.dt.int32
ALU = mybir.AluOpType
ACT = mybir.ActivationFunctionType
AX = mybir.AxisListType.X

P = 128
T = 256
TT = T // P
D = 1024
KT = D // P
F1 = 2816
F2 = 3072
EXPERTS = 8
RING = 4
SPLITS = 3
BLK = 2048
BIG = 1.0e30
RMS_EPS = 1e-6
LNX_EPS = 64e-5
HEADS = 16
DH = 64
CHUNKS = F2 // 512
EXPERT_BLOCKS = 6 * CHUNKS

CONST = {}


def const_table():
    cols, at = [], 0

    def add(name, a):
        nonlocal at
        CONST[name] = (at, a.shape[1])
        cols.append(a.astype(np.float32))
        at += a.shape[1]

    i = np.arange(P)
    row, col = i[:, None], i[None, :]
    add("ident", np.eye(P))
    add("ones", np.ones((P, P)))
    rot = np.zeros((P, P))
    for d in range(P):
        base, r = d // DH * DH, d % DH
        rot[base + (r + 32) % DH, d] = -1.0 if r < 32 else 1.0
    add("rot", rot)
    inv = (1.0 / (np.float32(10000.0) ** (np.arange(0, DH, 2, dtype=np.float32) / np.float32(DH)))).astype(np.float32)
    ang = (np.arange(T, dtype=np.float32)[:, None] * inv[None, :]).astype(np.float32)
    ang = np.tile(ang.T, (4, 1))
    add("cos", np.cos(ang))
    add("sin", np.sin(ang))
    inv2 = np.float32(10000.0) ** (-np.arange(0, DH, 2, dtype=np.float32) / np.float32(DH))
    add("inv", np.tile(inv2.astype(np.float32)[:, None], (4, 1)))
    tri = np.where(col <= row, 0.0, -BIG)
    add("causal", np.concatenate([tri, np.zeros((P, P)), tri], 1))
    add("before", (row < col) * 1.0)
    add("iota", np.tile(col, (P, 1)))
    strict, incl = (row < col) * 1.0, (row <= col) * 1.0
    add("pairmask", np.concatenate([strict, incl, strict, incl], 1))
    for lv in range(7):
        half = 1 << lv
        same = (row // (2 * half)) == (col // (2 * half))
        add(f"level{lv}", (same & (row % (2 * half) < half) & (col % (2 * half) >= half)) * 1.0)
    add("headones", (row // DH == col // DH) * 1.0)
    add("headsel", np.stack([i < DH, i >= DH], 1) * 1.0)
    add("rms_eps", np.full((P, 1), RMS_EPS))
    add("lnx_eps", np.full((P, 1), LNX_EPS))
    add("iota8", np.tile(np.arange(8)[None], (P, 2)))
    return np.ascontiguousarray(np.concatenate(cols, 1))


CONSTS = const_table()

VECTORS = [
    ("norm_mix", 16), ("norm_ffn", 16), ("rwkv_mu", 48), ("rwkv_w0", 8), ("rwkv_a0", 8), ("rwkv_k_k", 8),
    ("rwkv_k_a", 8), ("rwkv_r_k", 8), ("ffn_conv_w", 132), ("ffn_conv_b", 44), ("ln1_g_2", 16), ("ln2_g_2", 16),
    ("conv_w_2", 32), ("conv_b_2", 8), ("gate_a_b_2", 8), ("gate_x_b_2", 8), ("lru_lambda_2", 8),
    ("subln_g_2", 2), ("ada_b_2", 96), ("c_2", 8),
]
VROW = {}
_at = 0
for _name, _n in VECTORS:
    VROW[_name] = _at
    _at += _n
VTILES = -(-_at // P)
assert _at <= VTILES * P


class Steps:

    def __init__(self, sem):
        self.sem, self.n = sem, 0

    def mark(self, ins):
        ins.then_inc(self.sem, 1)
        self.n += 1

    def link(self, eng, ins):
        self.mark(ins)
        eng.wait_ge(self.sem, self.n)

    def wait(self, eng):
        eng.wait_ge(self.sem, self.n)


def build(nc, a, out, upto=99):
    with ExitStack() as ctx:
        names = {}

        def sb(name, shape, dt=F32, stage=ctx):
            names[name] = names.get(name, 0) + 1
            if names[name] > 1:
                name = f"{name}_{names[name]}"
            return stage.enter_context(nc.sbuf_tensor(name, shape, dt))

        def sem(name):
            return ctx.enter_context(nc.semaphore(name))

        pb = [ctx.enter_context(nc.psum_tensor(f"bank{i}", [P, 512], F32)) for i in range(8)]
        ring = sb("ring", [P, RING, BLK])
        split = [sb(n, [P, SPLITS, BLK], F32R) for n in ("weights_hi", "weights_lo")]
        mods = sb("mods", [P, 2, 48])
        gain2 = sb("gain2", [P, 2, 2, KT])
        silu_c = sb("silu_c", [P, KT])
        cst = sb("cst", [P, CONSTS.shape[1]])
        vec = sb("vec", [P, VTILES * P])
        resid = sb("resid", [P, TT, D])
        xn = sb("xn", [P, TT, D])
        AT = sb("AT", [P, KT, T])
        stat = sb("stat", [P, 64])

        def const(name, lo=0, n=None):
            at, width = CONST[name]
            return cst[:, at + lo:at + lo + (width if n is None else n)]

        def v(name, i=0, n=1):
            return vec[:, VROW[name] + i:VROW[name] + i + n]

        arrived = [sem(f"arrived{i}") for i in range(RING)]
        hi_ready = sem("hi_ready")
        taken = sem("taken")
        used = sem("used")
        at_ready = [sem(f"at_ready{i}") for i in range(4)]
        at_hi = sem("at_hi")
        at_lo = sem("at_lo")
        setup_in = sem("setup_in")
        setup_rows = sem("setup_rows")
        rows_turned = sem("rows_turned")
        squares = sem("squares")
        gain_in = sem("gain_in")
        rooted = sem("rooted")
        normed = sem("normed")
        turned = sem("turned")
        dve_step = Steps(sem("dve_step"))
        act_step = Steps(sem("act_step"))
        pool_step = Steps(sem("pool_step"))
        ident = const("ident")

        def cols_block(w, c):
            return w.rearrange("(k p) n -> p k n", p=P)[:, :, 256 * c:256 * c + 256]

        def rows_block(w, c):
            return w[256 * c:256 * c + 256, :].rearrange("(f p) n -> p f n", p=P)

        stream, weight_no, first = [], [], {}
        counted = [0]
        ffn_plan = {}

        def plan_one(src, weight=True):
            stream.append(src)
            weight_no.append(counted[0] if weight else None)
            counted[0] += weight
            return counted[0] - 1

        def plan(name, blocks):
            first[name] = counted[0]
            for src in blocks:
                plan_one(src)

        def plan_ffn(name, gate, up, down, extra):
            pairs = gate.shape[1] // 256
            at = {"places": {}}
            extra = list(extra)
            gap = max(1, (2 * pairs - 1) // len(extra))

            def place(q):
                if extra and q % gap == 0 and q <= 2 * pairs - 2:
                    l, i = extra.pop(0)
                    at["places"][q] = (l, i, len(stream))
                    plan_one(cols_block(a["ada_w_2"][l], i), False)

            for j in range(pairs + 1):
                if j < pairs:
                    at["gate", j] = plan_one(cols_block(gate, j))
                    at["up", j] = plan_one(cols_block(up, j))
                place(2 * j)
                if j:
                    at["down", j - 1] = plan_one(rows_block(down, j - 1))
                place(2 * j + 1)
            assert not extra
            ffn_plan[name] = at

        plan("qkv", [cols_block(a["attn_w_qkv"][0], c) for c in range(12)])
        plan("wo", [rows_block(a["attn_w_o"][0], c) for c in range(4)])
        early = [(0, i) for i in (*range(8), *range(12, 16))]
        late = [(0, i) for i in (*range(8, 12), *range(16, 24))] + [(1, 0), (1, 1)]
        plan_ffn(0, a["ffn_w_gate"][0], a["ffn_w_up"][0], a["ffn_w_down"][0], early)
        for m in (1, 0, 2):
            plan(f"rkv{m}", [cols_block(a["rwkv_w_rkv"][0, m], c) for c in range(4)])
        plan("rwkv_wo", [rows_block(a["rwkv_w_o"][0], c) for c in range(4)])
        plan_ffn(1, a["ffn_w_gate"][1], a["ffn_w_up"][1], a["ffn_w_down"][1], late)
        for l in range(2):
            plan(f"win{l}", [cols_block(a["w_in_2"][l], c) for c in range(10)])
            plan(f"wout{l}", [rows_block(a["w_out_2"][l], c) for c in range(4)])
            if l == 0:
                plan_ffn(2, a["ffn_w_gate_2"][0], a["ffn_w_up_2"][0], a["ffn_w_down_2"][0], [(1, i) for i in range(2, 24)])
        moe_first, moe_weight = len(stream), counted[0]
        position = {m: n for n, m in enumerate(weight_no) if m is not None}

        order = []
        for c in range(CHUNKS + 1):
            if c < CHUNKS:
                order += [("gate", c, 0), ("gate", c, 1), ("up", c, 0), ("up", c, 1)]
            if c:
                order += [("down", c - 1, 0), ("down", c - 1, 1)]
        assert len(order) == EXPERT_BLOCKS and EXPERT_BLOCKS % RING == 0 and EXPERT_BLOCKS % SPLITS == 0
        slot_of = {key: (moe_weight + j) % SPLITS for j, key in enumerate(order)}
        moe_dram = {k: a[f"moe_w_{k}_2"][0] for k in ("gate", "up", "down")}

        def expert_block(e, j):
            kind, c, half = order[j]
            w = moe_dram[kind][bass.ds(e, 1)] if not type(e) is int else moe_dram[kind][e:e + 1]
            if kind == "down":
                at = 512 * c + 256 * half
                return w[:, at:at + 256, :].rearrange("e (f p) n -> p (e f) n", p=P)
            rows = moe_dram[kind].rearrange("e k n -> (e k) n")
            return rows[bass.ds(e * D + 512 * half, 512), 512 * c:512 * c + 512].rearrange("(k p) n -> p k n", p=P)

        def slot_view(slot, src):
            return ring[:, slot, :].rearrange("p (k n) -> p k n", n=src.shape[-1])

        def issue(eng, n):
            src = stream[n] if n < moe_first else expert_block(0, n - moe_first)
            if n >= RING:
                eng.wait_ge(taken, n - RING + 1)
            eng.dma_start(slot_view(n % RING, src), src).then_inc(arrived[n % RING], 16)

        issued, rounded, rested = [0], [0], [0]

        def feed(sp):
            while issued[0] < min(goal[0] + RING, moe_first + RING):
                issue(sp, issued[0])
                issued[0] += 1

        goal = [0]

        def ahead(m):
            goal[0] = position[m - 1] + 1 if m else 0
            assert m <= moe_weight

        def hi_part(act, n):
            m = weight_no[n]
            act.wait_ge(arrived[n % RING], 16 * (n // RING + 1))
            if m >= SPLITS:
                act.wait_ge(used, m - SPLITS + 1)
            nc.scalar.copy(split[0][:, m % SPLITS, :], ring[:, n % RING, :]).then_inc(hi_ready, 1)

        def lo_part(dve, n):
            m = weight_no[n]
            dve.wait_ge(hi_ready, m + 1)
            nc.vector.tensor_tensor(split[1][:, m % SPLITS, :], ring[:, n % RING, :],
                                    split[0][:, m % SPLITS, :].bitcast(F32), ALU.subtract).then_inc(taken, 1)

        def round_to(act, m):
            while rounded[0] < goal[0] and (weight_no[rounded[0]] is None or weight_no[rounded[0]] < m):
                if weight_no[rounded[0]] is not None:
                    hi_part(act, rounded[0])
                rounded[0] += 1

        def rest_to(dve, m, other=None):
            while rested[0] < goal[0] and (weight_no[rested[0]] is None or weight_no[rested[0]] < m):
                if weight_no[rested[0]] is None:
                    other(rested[0])
                else:
                    lo_part(dve, rested[0])
                rested[0] += 1

        def landed(pe, m):
            pe.wait_ge(taken, position[m] + 1)

        splitting, skipped = [0], [0]

        def new_split():
            splitting[0] += 1
            return splitting[0] - 1

        def at_round(act, k, c, src=None):
            act.wait_ge(at_ready[c], k + 1 - skipped[0])
            src = AT if src is None else src
            nc.scalar.copy(acts[0][:, 2 * c:2 * c + 2, :], src[:, 2 * c:2 * c + 2, :]).then_inc(at_hi, 1)

        def at_rest(dve, k, c, src=None):
            dve.wait_ge(at_hi, 4 * k + c + 1)
            src = AT if src is None else src
            w = slice(2 * c, 2 * c + 2)
            nc.vector.tensor_tensor(acts[1][:, w, :], src[:, w, :], acts[0][:, w, :].bitcast(F32), ALU.subtract).then_inc(at_lo, 1)

        acts = [None, None]

        def open_acts(stage):
            acts[:] = [sb(n, [P, KT, T], F32R, stage) for n in ("acts_hi", "acts_lo")]

        PARTS = ((0, 0), (0, 1), (1, 0))

        with ExitStack() as stage:
            rows = sb("rows", [P, VTILES, P], stage=stage)
            pieces = []
            for name, n in VECTORS:
                src = a[name]
                letters = " ".join("abcdef"[:len(src.shape)])
                flat = src.rearrange(f"{letters} -> ({letters})").rearrange("(r x) -> r x", x=P)
                done = 0
                while done < n:
                    at = VROW[name] + done
                    m = min(n - done, P - at % P)
                    pieces.append((rows[at % P:at % P + m, at // P, :], flat[done:done + m]))
                    done += m
            tail = VROW["c_2"] + 8
            with nc.Block() as block:
                @block.sync
                def _(sp):
                    sp.dma_start(cst[:], a["consts"]).then_inc(setup_in, 16)
                    sp.dma_start(resid[:], a["x"][0].rearrange("(t p) d -> p t d", p=P)).then_inc(setup_in, 16)
                    feed(sp)

                @block.gpsimd
                def _(pool):
                    pool.memset(rows[:], 0.0).then_inc(setup_rows, 1)

                @block.scalar
                def _(act):
                    act.wait_ge(setup_rows, 1)
                    for dst, src in pieces:
                        act.dma_start(dst, src).then_inc(setup_in, 16)

                @block.tensor
                def _(pe):
                    pe.wait_ge(setup_in, 16 * (2 + len(pieces)))
                    for i in range(VTILES):
                        ins = nc.tensor.transpose(pb[0][:, i * P:(i + 1) * P], rows[:, i, :], ident)
                    ins.then_inc(rows_turned, 1)

                @block.vector
                def _(dve):
                    dve.wait_ge(rows_turned, 1)
                    nc.vector.tensor_copy(vec[:], pb[0][:]).then_inc(rows_turned, 1)

                @block.scalar
                def _(act):
                    act.wait_ge(rows_turned, 2)
                    nc.scalar.activation(silu_c[:], v("c_2", 0, KT), ACT.Silu)

        def norm_rows(k, row):
            with ExitStack() as stage:
                gain = sb(f"gain{k}", [P, D], stage=stage)
                with nc.Block() as block:
                    @block.sync
                    def _(sp):
                        sp.dma_start(gain[:], row.broadcast_to([P, D])).then_inc(gain_in, 16)

                    @block.scalar
                    def _(act):
                        for t in range(TT):
                            nc.scalar.activation(xn[:, t, :], resid[:, t, :], ACT.Square,
                                                 accum_out=stat[:, t:t + 1]).then_inc(squares, 1)
                        for t in range(TT):
                            act.wait_ge(squares, TT * k + t + 1)
                            nc.scalar.activation(stat[:, t:t + 1], stat[:, t:t + 1], ACT.Sqrt, scale=1.0 / D,
                                                 bias=const("rms_eps")).then_inc(rooted, 1)

                    @block.vector
                    def _(dve):
                        dve.wait_ge(gain_in, 16 * (1 if k < 5 else 2))
                        for t in range(TT):
                            dve.wait_ge(rooted, TT * k + t + 1)
                            dve_step.link(dve, nc.vector.reciprocal(stat[:, t:t + 1], stat[:, t:t + 1]))
                            nc.vector.scalar_tensor_tensor(resid[:, t, :], resid[:, t, :], stat[:, t:t + 1], gain[:],
                                                           ALU.mult, ALU.mult).then_inc(normed, 1)

        def norm_turn(k, gain, bias=None, turns=None, then=None, look=SPLITS, parts=True):
            no = new_split() if parts else None
            if then is not None:
                ahead(then + look)
            turns = k if turns is None else turns
            with nc.Block() as block:
                @block.scalar
                def _(act):
                    for t in range(TT):
                        nc.scalar.activation(xn[:, t, :], resid[:, t, :], ACT.Square,
                                             accum_out=stat[:, t:t + 1]).then_inc(squares, 1)
                    for t in range(TT):
                        act.wait_ge(squares, TT * k + t + 1)
                        nc.scalar.activation(stat[:, t:t + 1], stat[:, t:t + 1], ACT.Sqrt, scale=1.0 / D,
                                             bias=const("rms_eps")).then_inc(rooted, 1)
                    if then is not None:
                        round_to(act, then + look)
                    for b in range(2):
                        act.wait_ge(turned, 4 * turns + b + 1)
                        for i in range(2):
                            f = 2 * b + i
                            ins = nc.scalar.activation(AT[:, f, :], pb[b][:, i * T:(i + 1) * T], ACT.Identity,
                                                       scale=gain(f), bias=bias(f) if bias else 0.0)
                        if parts:
                            ins.then_inc(at_ready[b], 1)
                    if parts:
                        for c in range(4):
                            at_round(act, no, c)

                @block.sync
                def _(sp):
                    feed(sp)

                @block.vector
                def _(dve):
                    for t in range(TT):
                        dve.wait_ge(rooted, TT * k + t + 1)
                        dve_step.link(dve, nc.vector.reciprocal(stat[:, t:t + 1], stat[:, t:t + 1]))
                        nc.vector.tensor_scalar(xn[:, t, :], resid[:, t, :], stat[:, t:t + 1], None,
                                                ALU.mult).then_inc(normed, 1)
                    for b in range(2, 4):
                        dve.wait_ge(turned, 4 * turns + b + 1)
                        for i in range(2):
                            f = 2 * b + i
                            ins = nc.vector.tensor_scalar(AT[:, f, :], pb[b][:, i * T:(i + 1) * T], gain(f),
                                                          bias(f) if bias else 0.0, ALU.mult, ALU.add)
                        if parts:
                            ins.then_inc(at_ready[b], 1)
                    if then is not None:
                        rest_to(dve, then + 1)
                    if parts:
                        for c in range(4):
                            at_rest(dve, no, c)
                    if then is not None:
                        rest_to(dve, then + look)

                @block.tensor
                def _(pe):
                    pe.wait_ge(normed, TT * (k + 1))
                    for b in range(4):
                        for i in range(2):
                            for t in range(TT):
                                f = 2 * b + i
                                ins = nc.tensor.transpose(pb[b][:, i * T + t * P:i * T + (t + 1) * P],
                                                          xn[:, t, f * P:(f + 1) * P], ident)
                        ins.then_inc(turned, 1)
            return no

        def to_features(pe, m, bank):
            landed(pe, m)
            for f in range(2):
                for k in range(KT):
                    for w, x in PARTS:
                        ins = nc.tensor.matmul(bank[:, f * T:(f + 1) * T],
                                               split[w][:, m % SPLITS, k * 256 + f * P:k * 256 + (f + 1) * P],
                                               acts[x][:, k, :], start=(k == 0 and w + x == 0), stop=(k == KT - 1 and w == 1))
            ins.then_inc(used, 1)

        def to_tokens(pe, m, bank):
            landed(pe, m)
            for t in range(TT):
                for k in range(KT):
                    for x, w in PARTS:
                        ins = nc.tensor.matmul(bank[:, t * 256:(t + 1) * 256], acts[x][:, k, t * P:(t + 1) * P],
                                               split[w][:, m % SPLITS, k * 256:(k + 1) * 256],
                                               start=(k == 0 and w + x == 0), stop=(k == KT - 1 and x == 1))
            ins.then_inc(used, 1)

        def project(pe, m, c, count, src, tile=None):
            landed(pe, m)
            tile = 2 * c if tile is None else tile
            for f in range(2):
                for t in range(TT):
                    for x, w in PARTS:
                        for h in range(2):
                            ins = nc.tensor.matmul(pb[4 + 2 * t + h][:], src[x][:, tile + f, t * P:(t + 1) * P],
                                                   split[w][:, m % SPLITS, f * D + h * 512:f * D + (h + 1) * 512],
                                                   start=(c == 0 and f == 0 and w + x == 0),
                                                   stop=(c == count - 1 and f == 1 and x == 1))
            ins.then_inc(used, 1)

        def add_projected(dve, end, scale=None, scratch=None):
            dve.wait_ge(used, end)
            for t in range(TT):
                for h in range(2):
                    y = pb[4 + 2 * t + h][:]
                    if scale is not None:
                        y = scratch[:, h, :]
                        dve_step.mark(nc.vector.tensor_tensor(y, pb[4 + 2 * t + h][:], scale[:, h * 512:(h + 1) * 512], ALU.mult))
                if scale is not None:
                    dve_step.wait(dve)
                for h in range(2):
                    r = resid[:, t, h * 512:(h + 1) * 512]
                    y = pb[4 + 2 * t + h][:] if scale is None else scratch[:, h, :]
                    dve_step.mark(nc.vector.tensor_tensor(r, r, y, ALU.add))
                if scale is not None:
                    dve_step.wait(dve)

        def finish():
            stored = sem("stored")
            with nc.Block() as block:
                @block.sync
                def _(sp):
                    sp.dma_start(out[0].rearrange("(t p) d -> p t d", p=P), resid[:]).then_inc(stored, 16)
                    sp.wait_ge(stored, 16)
        region = ExitStack()
        ctx.callback(region.close)
        open_acts(region)
        no = norm_turn(0, lambda f: v("norm_mix", f), then=0)
        heads_stage = ExitStack()
        QK = sb("QK", [P, 16, T], stage=heads_stage)
        V = sb("V", [P, TT, D], stage=heads_stage)

        raw_ready = sem("raw_ready")
        rot_done = sem("rot_done")
        qk_done = sem("qk_done")
        v_done = sem("v_done")
        with ExitStack() as stage:
            raw = sb("raw", [P, 2, 2 * T], stage=stage)
            rc = sb("rc", [P, 2, 2 * T], stage=stage)
            rs = sb("rs", [P, 2, 2 * T], stage=stage)
            n0 = first["qkv"]
            ahead(n0 + 12)
            with nc.Block() as block:
                @block.sync
                def _(sp):
                    feed(sp)

                @block.tensor
                def _(pe):
                    pe.wait_ge(at_lo, 4 * no + 4)
                    for i in range(12):
                        bank = pb[i % 3]
                        if i >= 3:
                            if i - 3 < 8:
                                pe.wait_ge(raw_ready, i - 2)
                            else:
                                pe.wait_ge(v_done, i - 3 - 8 + 1)
                        (to_features if i < 8 else to_tokens)(pe, n0 + i, bank)
                        if 1 <= i <= 8:
                            b = i - 1
                            pe.wait_ge(raw_ready, b + 1)
                            if b >= 2:
                                pe.wait_ge(qk_done, b - 1)
                            nc.tensor.matmul(pb[4 + b % 2][:], const("rot"), raw[:, b % 2, :], start=True,
                                             stop=True).then_inc(rot_done, 1)

                @block.scalar
                def _(act):
                    for b in range(8):
                        round_to(act, n0 + b + 3)
                        act.wait_ge(used, n0 + b + 1)
                        if b >= 2:
                            act.wait_ge(qk_done, b - 1)
                        nc.scalar.copy(raw[:, b % 2, :], pb[b % 3][:]).then_inc(raw_ready, 1)
                    for b in range(4):
                        round_to(act, n0 + 8 + b + 3)
                        act.wait_ge(used, n0 + 8 + b + 1)
                        nc.scalar.copy(V[:, :, b * 256:(b + 1) * 256],
                                       pb[(8 + b) % 3][:].rearrange("p (t n) -> p t n", t=2)).then_inc(v_done, 1)

                @block.vector
                def _(dve):
                    cos = const("cos").rearrange("p (a t) -> p a t", a=1).broadcast_to([P, 2, T])
                    sin = const("sin").rearrange("p (a t) -> p a t", a=1).broadcast_to([P, 2, T])
                    for b in range(8):
                        three = lambda z: z.rearrange("p (f t) -> p f t", f=2)
                        rest_to(dve, n0 + b + 3)
                        dve.wait_ge(raw_ready, b + 1)
                        dve_step.mark(nc.vector.tensor_tensor(three(rc[:, b % 2, :]), three(raw[:, b % 2, :]), cos, ALU.mult))
                        dve.wait_ge(rot_done, b + 1)
                        dve_step.link(dve, nc.vector.tensor_tensor(three(rs[:, b % 2, :]), three(pb[4 + b % 2][:]), sin, ALU.mult))
                        nc.vector.tensor_tensor(QK[:, 2 * b:2 * b + 2, :].rearrange("p f t -> p (f t)"), rc[:, b % 2, :],
                                                rs[:, b % 2, :], ALU.add).then_inc(qk_done, 1)
                    rest_to(dve, n0 + 12)

        scored = sem("scored")
        masked = sem("masked")
        maxed = sem("maxed")
        exped = sem("exped")
        weighted = sem("weighted")
        p_turned = sem("p_turned")
        p_copied = sem("p_copied")
        head_out = sem("head_out")
        out_copied = sem("out_copied")
        with ExitStack() as stage:
            S = sb("S", [P, 2, 384], stage=stage)
            Pr = sb("Pr", [P, 2, 384], stage=stage)
            PT = sb("PT", [P, 2, 384], stage=stage)
            st = sb("st", [P, HEADS, 6], stage=stage)
            sc = DH ** -0.5
            n0 = first["wo"]
            ahead(n0 + 3)
            no = new_split()
            skipped[0] += 1
            with nc.Block() as block:
                @block.sync
                def _(sp):
                    feed(sp)

                @block.tensor
                def _(pe):
                    def score(h):
                        if h >= 2:
                            pe.wait_ge(masked, h - 1)
                        lo, f = DH * (h % 2), h // 2
                        q, kk = QK[lo:lo + DH, f, :], QK[lo:lo + DH, 8 + f, :]
                        bank = pb[h % 2]
                        nc.tensor.matmul(bank[:, 0:P], q[:, 0:P], kk[:, 0:P], start=True, stop=True)
                        nc.tensor.matmul(bank[:, P:384], q[:, P:T], kk[:, :], start=True, stop=True).then_inc(scored, 1)

                    def turn(h):
                        pe.wait_ge(weighted, h + 1)
                        if h >= 2:
                            pe.wait_ge(p_copied, h - 1)
                        bank = pb[2 + h % 2]
                        for i in range(3):
                            at = [0, P, 2 * P][i]
                            ins = nc.tensor.transpose(bank[:, at:at + P], Pr[:, h % 2, [0, P, 2 * P][i]:[0, P, 2 * P][i] + P], ident)
                        ins.then_inc(p_turned, 1)

                    def mix(h):
                        pe.wait_ge(p_copied, h + 1)
                        if h >= 4 and h % 2 == 0:
                            pe.wait_ge(out_copied, h // 2 - 1)
                        lo, pt = DH * (h % 2), PT[:, h % 2, :]
                        o = pb[4 + h // 2 % 2][lo:lo + DH, 0:T]
                        nc.tensor.matmul(o, V[:, 0, h * DH:(h + 1) * DH], pt[:, 0:T], start=True, stop=False)
                        nc.tensor.matmul(o[:, P:T], V[:, 1, h * DH:(h + 1) * DH], pt[:, T:T + P], start=False,
                                         stop=True).then_inc(head_out, 1)

                    for i in range(HEADS + 2):
                        if i < HEADS:
                            score(i)
                        if 1 <= i <= HEADS:
                            turn(i - 1)
                        if i >= 2:
                            mix(i - 2)

                @block.vector
                def _(dve):
                    def first_half(h):
                        dve.wait_ge(scored, h + 1)
                        if h >= 2:
                            dve.wait_ge(exped, 2 * (h - 1))
                        nc.vector.tensor_tensor(S[:, h % 2, :], pb[h % 2][:, 0:384], const("causal"), ALU.add).then_inc(masked, 1)
                        dve.wait_ge(masked, h + 1)
                        dve_step.mark(nc.vector.reduce_max(st[:, h, 0:1], S[:, h % 2, 0:P], AX))
                        dve_step.link(dve, nc.vector.reduce_max(st[:, h, 1:2], S[:, h % 2, P:384], AX))
                        nc.vector.tensor_scalar(st[:, h, 0:2], st[:, h, 0:2], -sc, None, ALU.mult).then_inc(maxed, 1)

                    def second_half(h):
                        dve.wait_ge(exped, 2 * (h + 1))
                        dve_step.link(dve, nc.vector.reciprocal(st[:, h, 4:6], st[:, h, 2:4]))
                        if h >= 2:
                            dve.wait_ge(p_turned, h - 1)
                        dve_step.mark(nc.vector.tensor_scalar(Pr[:, h % 2, 0:P], S[:, h % 2, 0:P], st[:, h, 4:5], None, ALU.mult))
                        nc.vector.tensor_scalar(Pr[:, h % 2, P:384], S[:, h % 2, P:384], st[:, h, 5:6], None,
                                                ALU.mult).then_inc(weighted, 1)

                    for h in range(HEADS + 1):
                        if h in (2, 4, 6):
                            rest_to(dve, n0 + h // 2)
                        if h >= 1:
                            second_half(h - 1)
                        if h < HEADS:
                            if h >= 2:
                                dve.wait_ge(weighted, h - 1)
                            first_half(h)

                @block.scalar
                def _(act):
                    def copies(h):
                        act.wait_ge(p_turned, h + 1)
                        if h >= 2:
                            act.wait_ge(head_out, h - 1)
                        nc.scalar.copy(PT[:, h % 2, :], pb[2 + h % 2][:, 0:384]).then_inc(p_copied, 1)

                    def outs(f):
                        act.wait_ge(head_out, 2 * f + 2)
                        nc.scalar.copy(AT[:, f, :], pb[4 + f % 2][:, 0:T]).then_inc(out_copied, 1)
                        if f % 2:
                            act.wait_ge(out_copied, f + 1)
                            nc.scalar.copy(acts[0][:, f - 1:f + 1, :], AT[:, f - 1:f + 1, :]).then_inc(at_hi, 1)

                    for i in range(HEADS + 3):
                        if i in (0, 2, 4):
                            round_to(act, n0 + i // 2 + 1)
                        if i < HEADS:
                            act.wait_ge(maxed, i + 1)
                            for t, (lo, hi) in enumerate(((0, P), (P, 384))):
                                nc.scalar.activation(S[:, i % 2, lo:hi], S[:, i % 2, lo:hi], ACT.Exp, scale=sc,
                                                     bias=st[:, i, t:t + 1], accum_out=st[:, i, 2 + t:3 + t]).then_inc(exped, 1)
                        if 1 <= i <= HEADS:
                            copies(i - 1)
                        if i >= 3 and i % 2 == 1:
                            outs((i - 3) // 2)
            after = ffn_plan[0]["gate", 0]
            ahead(after + 2)
            with nc.Block() as block:
                @block.sync
                def _(sp):
                    feed(sp)

                @block.scalar
                def _(act):
                    round_to(act, after + 2)

                @block.tensor
                def _(pe):
                    for c in range(4):
                        pe.wait_ge(at_lo, 4 * no + c + 1)
                        project(pe, n0 + c, c, 4, acts)

                @block.vector
                def _(dve):
                    for c in range(4):
                        at_rest(dve, no, c)
                    rest_to(dve, after + 2)
                    add_projected(dve, n0 + 4)
        heads_stage.close()

        if upto <= 1:
            return finish()

        gate_copied = sem("gate_copied")
        gate_pads = sem("gate_pads")
        convolved = sem("convolved")
        silued = sem("silued")
        hidden = sem("hidden")
        hid_hi = sem("hid_hi")
        hid_lo = sem("hid_lo")
        ada_done = sem("ada_done")
        ada_read = sem("ada_read")
        gates = [None, None]
        gates_in = sem("gates_in")
        ada_before, pairs_done_before, conv_before = [0], [0], [0]

        def make_gates(l):
            gates[l] = sb(f"gates{l}", [P, 2, D])
            return gates[l]

        def ffn(name, no, then, conv=None, scale=None, gate_rows=None, finished=None):
            at = ffn_plan[name]
            places = at["places"]
            pairs = sum(1 for k in at if k[0] == "gate")
            hb, cb, ab = pairs_done_before[0], conv_before[0], ada_before[0]
            number = {q: ab + i for i, q in enumerate(sorted(places))}
            last = at["down", pairs - 1] + 1
            ahead(min(then + 2, last + 2) if then is not None else last)
            with ExitStack() as stage:
                hf = sb("hf", [P, 2, 2 * T], stage=stage)
                hp = [sb(n, [P, 4, T], F32R, stage=stage) for n in ("hid_hi_part", "hid_lo_part")]
                sg = sb("sg", [P, 2, 2 * T], stage=stage)
                asum = sb("asum", [P, 4, 256], stage=stage)
                if conv is not None:
                    gp = sb("gp", [P, 2, 2, T + 2], stage=stage)
                    cv = sb("cv", [P, 2, 2 * T], stage=stage)
                zz = sb("zz", [P, 2, 512], stage=stage) if scale is not None else None
                with nc.Block() as block:
                    @block.sync
                    def _(sp):
                        if gate_rows is not None:
                            for i in range(2):
                                sp.dma_start(gates[gate_rows][:, i, :],
                                             a["ada_b_2"][gate_rows:gate_rows + 1, (3 * i + 2) * D:(3 * i + 3) * D]
                                             .broadcast_to([P, D])).then_inc(gates_in, 16)
                        feed(sp)

                    @block.tensor
                    def _(pe):
                        def modulation(q):
                            if q - 2 not in places:
                                return
                            (l, i, place), n = places[q - 2], number[q - 2]
                            pe.wait_ge(taken, place + 1)
                            if n:
                                pe.wait_ge(ada_read, n)
                            if i // 4 in (2, 5):
                                ins = nc.tensor.matmul(pb[3][:, 0:256], const("ones"), asum[:, n % 4, :],
                                                       start=True, stop=True)
                            else:
                                for f in range(2):
                                    ins = nc.tensor.matmul(pb[3][:, f:f + 1], asum[:, n % 4, f * P:(f + 1) * P],
                                                           const("ones", 0, 1), start=True, stop=True)
                            ins.then_inc(ada_done, 1)

                        pe.wait_ge(at_lo, 4 * no + 4)
                        for j in range(pairs + 1):
                            if j < pairs:
                                if j >= 2:
                                    pe.wait_ge(gate_copied, hb + j - 1)
                                to_features(pe, at["gate", j], pb[j % 2])
                                if j:
                                    pe.wait_ge(hidden, hb + j)
                                to_features(pe, at["up", j], pb[2])
                            modulation(2 * j)
                            if j:
                                pe.wait_ge(hid_lo, hb + j)
                                project(pe, at["down", j - 1], j - 1, pairs, hp, 2 * ((j - 1) % 2))
                            modulation(2 * j + 1)

                    @block.scalar
                    def _(act):
                        for j in range(pairs + 1):
                            if j:
                                act.wait_ge(hidden, hb + j)
                                if j >= 3:
                                    act.wait_ge(used, at["down", j - 3] + 1)
                                h = 2 * ((j - 1) % 2)
                                nc.scalar.copy(hp[0][:, h:h + 2, :].rearrange("p f t -> p (f t)"), hf[:, (j - 1) % 2, :]).then_inc(hid_hi, 1)
                            if j < pairs:
                                round_to(act, at["gate", j] + 3)
                                round_to(act, at["up", j] + 3)
                                act.wait_ge(used, at["gate", j] + 1)
                                if conv is None:
                                    if j >= 2:
                                        act.wait_ge(hidden, hb + j - 1)
                                    nc.scalar.activation(sg[:, j % 2, :], pb[j % 2][:], ACT.Silu).then_inc(gate_copied, 1)
                                else:
                                    if j >= 2:
                                        act.wait_ge(convolved, cb + j - 1)
                                    else:
                                        act.wait_ge(gate_pads, 2 * conv + 2)
                                    nc.scalar.copy(gp[:, j % 2, :, 2:], pb[j % 2][:].rearrange("p (f t) -> p f t", f=2)).then_inc(gate_copied, 1)
                                    act.wait_ge(convolved, cb + j + 1)
                                    if j >= 2:
                                        act.wait_ge(hidden, hb + j - 1)
                                    nc.scalar.activation(sg[:, j % 2, :], cv[:, j % 2, :], ACT.Silu).then_inc(silued, 1)
                            if j:
                                round_to(act, at["down", j - 1] + 3)

                    @block.vector
                    def _(dve):
                        if conv is not None:
                            for b in range(2):
                                nc.vector.memset(gp[:, b, :, 0:2], 0.0).then_inc(gate_pads, 1)
                        def convolve(j):
                            dve.wait_ge(gate_copied, hb + j + 1)
                            if j >= 2:
                                dve.wait_ge(silued, cb + j - 1)
                            for i in range(3):
                                for f in range(2):
                                    ft = 2 * j + f
                                    w = v("ffn_conv_w", (conv * 3 + 2 - i) * (F1 // P) + ft)
                                    src, dst = gp[:, j % 2, f, 2 - i:2 - i + T], cv[:, j % 2, f * T:(f + 1) * T]
                                    if i == 0:
                                        ins = nc.vector.tensor_scalar(dst, src, w, v("ffn_conv_b", conv * (F1 // P) + ft), ALU.mult, ALU.add)
                                    else:
                                        ins = nc.vector.scalar_tensor_tensor(dst, src, w, dst, ALU.mult, ALU.add)
                                    if i == 2 and f == 1:
                                        ins.then_inc(convolved, 1)
                                    else:
                                        dve_step.mark(ins)
                                if i < 2:
                                    dve_step.wait(dve)

                        def multiply(j):
                            dve.wait_ge(gate_copied if conv is None else silued, (hb if conv is None else cb) + j + 1)
                            dve.wait_ge(used, at["up", j] + 1)
                            if j >= 2:
                                dve.wait_ge(hid_lo, hb + j - 1)
                            nc.vector.tensor_tensor(hf[:, j % 2, :], sg[:, j % 2, :], pb[2][:], ALU.mult).then_inc(hidden, 1)

                        def rest(j):
                            dve.wait_ge(hid_hi, hb + j + 1)
                            h = 2 * (j % 2)
                            hi, lo = (z[:, h:h + 2, :].rearrange("p f t -> p (f t)") for z in hp)
                            nc.vector.tensor_tensor(lo, hf[:, j % 2, :], hi.bitcast(F32), ALU.subtract).then_inc(hid_lo, 1)

                        def modulation_read(q):
                            if q - 3 not in places:
                                return
                            (l, i, _), n = places[q - 3], number[q - 3]
                            dve.wait_ge(ada_done, n + 1)
                            seg, c = i // 4, i % 4
                            if seg in (2, 5):
                                dve.wait_ge(gates_in, 32 * (l + 1))
                                g = gates[l][:, seg // 3, c * 256:(c + 1) * 256]
                                ins = nc.vector.tensor_tensor(g, g, pb[3][:, 0:256], ALU.add)
                            else:
                                k = seg * KT + 2 * c
                                ins = nc.vector.tensor_tensor(mods[:, l, k:k + 2], pb[3][:, 0:2],
                                                              v("ada_b_2", l * 48 + k, 2), ALU.add)
                            ins.then_inc(ada_read, 1)

                        summed = [ab]

                        def modulation_sum(n):
                            i = summed[0]
                            summed[0] += 1
                            dve.wait_ge(arrived[n % RING], 16 * (n // RING + 1))
                            if i >= 4:
                                dve.wait_ge(ada_done, i - 3)
                            x = ring[:, n % RING, :]
                            z = asum[:, i % 4, :]
                            dve_step.link(dve, nc.vector.tensor_scalar(z, x[:, 0:256], silu_c[:, 0:1], None, ALU.mult))
                            for r in range(1, KT):
                                ins = nc.vector.scalar_tensor_tensor(z, x[:, r * 256:(r + 1) * 256],
                                                                     silu_c[:, r:r + 1], z, ALU.mult, ALU.add)
                                if r < KT - 1:
                                    dve_step.link(dve, ins)
                            ins.then_inc(taken, 1)

                        for j in range(pairs + 1):
                            if j:
                                multiply(j - 1)
                            if j < pairs:
                                rest_to(dve, at["gate", j] + 3, modulation_sum)
                            if j:
                                rest(j - 1)
                            modulation_read(2 * j)
                            if j < pairs:
                                rest_to(dve, at["up", j] + 3, modulation_sum)
                            if j < pairs and conv is not None:
                                convolve(j)
                            if j:
                                rest_to(dve, at["down", j - 1] + 3, modulation_sum)
                            modulation_read(2 * j + 1)
                        if finished is not None:
                            dve.wait_ge(ada_read, ab + len(places))
                            for i, gname in enumerate(("ln1_g_2", "ln2_g_2")):
                                seg = 3 * i + 1
                                nc.vector.scalar_tensor_tensor(gain2[:, finished, i, :], mods[:, finished, seg * KT:(seg + 1) * KT],
                                                               1.0, v(gname, finished * KT, KT), ALU.add, ALU.mult)
                        add_projected(dve, last, scale, zz)
            ada_before[0] += len(places)
            pairs_done_before[0] += pairs
            if conv is not None:
                conv_before[0] += pairs

        no = norm_turn(1, lambda f: v("norm_ffn", f), then=ffn_plan[0]["gate", 0], look=2)
        ffn(0, no, first["rkv1"], conv=0)
        if upto <= 2:
            return finish()

        region.close()
        nk = first["rkv1"]
        norm_turn(2, lambda f: v("norm_mix", KT + f), then=nk, look=3, parts=False)
        C = P
        rwkv = ExitStack()
        KR = sb("KR", [P, 16, 2, C], stage=rwkv)
        bet = sb("bet", [P, 16, C], stage=rwkv)
        G = sb("G", [P, KT, T], stage=rwkv)
        bonus = sb("bonus", [P, TT, HEADS], stage=rwkv)
        S0 = sb("S0", [P, KT, DH], stage=rwkv)
        fac = sb("fac", [P, KT], stage=rwkv)
        fc = lambda z: z.rearrange("p f (c t) -> p (f c) t", c=2)

        mix_ready = sem("mix_ready")
        lora_in = sem("lora_in")
        lora_first = sem("lora_first")
        lora_act = sem("lora_act")
        lora_out = sem("lora_out")
        lora_read = sem("lora_read")
        rkv_read = sem("rkv_read")
        with ExitStack() as stage:
            xx = xn[:].rearrange("p a b -> p (a b)").rearrange("p (k t) -> p k t", k=KT)
            mix = sb("mix", [P, 2, KT, T], stage=stage)
            w1, a1, g1 = (sb(n, [P, KT, m], stage=stage) for n, m in (("w1", 64), ("a1", 64), ("g1", 128)))
            second = sb("second", [P, 3, D], stage=stage)
            la = sb("la", [P, 3, T], stage=stage)
            with nc.Block() as block:
                @block.sync
                def _(sp):
                    for dst, name in ((w1, "rwkv_w1"), (a1, "rwkv_a1"), (g1, "rwkv_g1")):
                        sp.dma_start(dst[:], a[name][0].rearrange("(k p) n -> p k n", p=P)).then_inc(lora_in, 16)
                    for i, name in enumerate(("rwkv_w2", "rwkv_a2", "rwkv_g2")):
                        m = 64 if i < 2 else P
                        sp.dma_start(second[0:m, i, :], a[name][0]).then_inc(lora_in, 16)

                @block.vector
                def _(dve):
                    dve_step.mark(nc.vector.tensor_tensor(xx[:, :, 1:T], AT[:, :, 0:T - 1], AT[:, :, 1:T], ALU.subtract))
                    dve_step.link(dve, nc.vector.tensor_scalar(xx[:, :, 0:1], AT[:, :, 0:1], -1.0, None, ALU.mult))
                    for i, m in enumerate((1, 4, 5)):
                        if i == 2:
                            dve.wait_ge(lora_first, 1)
                        for k in range(KT):
                            ins = nc.vector.scalar_tensor_tensor(mix[:, i % 2, k, :], xx[:, k, :], v("rwkv_mu", m * KT + k),
                                                                 AT[:, k, :], ALU.mult, ALU.add)
                        ins.then_inc(mix_ready, 1)

                @block.tensor
                def _(pe):
                    pe.wait_ge(lora_in, 96)
                    for i, (w, m) in enumerate(((w1, 64), (a1, 64), (g1, P))):
                        pe.wait_ge(mix_ready, i + 1)
                        for k in range(KT):
                            ins = nc.tensor.matmul(pb[i][0:m, 0:T], w[:, k, :], mix[:, i % 2, k, :],
                                                   start=(k == 0), stop=(k == KT - 1))
                        ins.then_inc(lora_first, 1)
                    for q in range(12):
                        i, m = q // 4, (64, 64, P)[q // 4]
                        if q % 4 == 0:
                            pe.wait_ge(lora_act, i + 1)
                        if q >= 4:
                            pe.wait_ge(lora_read, q - 3)
                        for f in range(2):
                            ft = 2 * (q % 4) + f
                            ins = nc.tensor.matmul(pb[3 + q % 4][:, f * T:(f + 1) * T], second[0:m, i, ft * P:(ft + 1) * P],
                                                   la[0:m, i, :], start=True, stop=True)
                        ins.then_inc(lora_out, 1)

                @block.scalar
                def _(act):
                    for i, func in enumerate((ACT.Tanh, ACT.Copy, ACT.Sigmoid)):
                        m = (64, 64, P)[i]
                        act.wait_ge(lora_first, i + 1)
                        nc.scalar.activation(la[0:m, i, :], pb[i][0:m, 0:T], func).then_inc(lora_act, 1)
                    for q in range(12):
                        act.wait_ge(lora_out, q + 1)
                        bank = pb[3 + q % 4]
                        if q >= 8:
                            nc.scalar.copy(G[:, 2 * (q % 4):2 * (q % 4) + 2, :].rearrange("p f t -> p (f t)"),
                                           bank[:]).then_inc(lora_read, 1)
                            continue
                        for f in range(2):
                            ft = 2 * (q % 4) + f
                            dst = KR[:, 2 * ft:2 * ft + 2, 0, :] if q < 4 else bet[:, 2 * ft:2 * ft + 2, :]
                            ins = nc.scalar.activation(dst, bank[:, f * T:(f + 1) * T].rearrange("p (c t) -> p c t", c=2),
                                                       ACT.Sigmoid, bias=v("rwkv_w0" if q < 4 else "rwkv_a0", ft))
                        ins.then_inc(lora_read, 1)

        kh = sb("kh", [P, 16, C], stage=rwkv)
        V = sb("Vr", [P, TT, D], stage=rwkv)
        with ExitStack() as stage:
            mix = sb("mix", [P, 2, KT, T], stage=stage)
            open_acts(stage)
            numbers = [new_split() for _ in range(3)]
            n0 = first["rwkv_wo"]
            ahead(n0 + 3)
            with nc.Block() as block:
                @block.sync
                def _(sp):
                    feed(sp)

                @block.tensor
                def _(pe):
                    for q in range(12):
                        pe.wait_ge(at_lo, 4 * numbers[q // 4] + 4)
                        if q >= 4:
                            pe.wait_ge(rkv_read, q - 3)
                        (to_tokens if q >= 8 else to_features)(pe, nk + q, pb[q % 4])

                @block.vector
                def _(dve):
                    def interpolate(i):
                        if i == 2:
                            dve.wait_ge(at_lo, 4 * numbers[1])
                        for k in range(KT):
                            ins = nc.vector.scalar_tensor_tensor(mix[:, i % 2, k, :], xx[:, k, :], v("rwkv_mu", (2, 0, 3)[i] * KT + k),
                                                                 AT[:, k, :], ALU.mult, ALU.add)
                            if k % 2:
                                ins.then_inc(at_ready[k // 2], 1)

                    def rests(i):
                        for c in range(4):
                            at_rest(dve, numbers[i], c, mix[:, i % 2])

                    interpolate(0)
                    rests(0)
                    interpolate(1)
                    for q in range(12):
                        rest_to(dve, nk + q + 3)
                        if q in (3, 7):
                            rests(q // 4 + 1)
                        if q == 4:
                            interpolate(2)
                    rest_to(dve, n0 + 3)

                @block.scalar
                def _(act):
                    for c in range(4):
                        at_round(act, numbers[0], c, mix[:, 0])
                    for q in range(12):
                        round_to(act, nk + q + 3)
                        act.wait_ge(used, nk + q + 1)
                        if q in (3, 7):
                            for c in range(4):
                                at_round(act, numbers[q // 4 + 1], c, mix[:, (q // 4 + 1) % 2])
                        bank, b = pb[q % 4], q % 4
                        if q >= 8:
                            dst, src = V[:, :, b * 256:(b + 1) * 256], bank[:].rearrange("p (t n) -> p t n", t=2)
                        else:
                            dst = (kh[:, 4 * b:4 * b + 4, :] if q < 4 else KR[:, 4 * b:4 * b + 4, 1, :])
                            src = bank[:].rearrange("p (f t) -> p f t", f=4)
                        nc.scalar.copy(dst, src).then_inc(rkv_read, 1)
                    round_to(act, n0 + 3)

        CD = -math.exp(-0.5)
        keyed = sem("keyed")
        key_sq = sem("key_sq")
        key_sum = sem("key_sum")
        key_max = sem("key_max")
        key_root = sem("key_root")
        decays = sem("decays")
        exps = sem("exps")
        bonus_in = sem("bonus_in")
        bonus_done = sem("bonus_done")
        with ExitStack() as stage:
            Ls = xn[:].rearrange("p a b -> p (a b)").rearrange("p (f t) -> p f t", f=16)
            Lp = sb("Lp", [P, 16, C], stage=stage)
            E1 = AT[:].rearrange("p k t -> p (k t)").rearrange("p (f t) -> p f t", f=16)
            E2 = sb("E2", [P, 16, C], stage=stage)
            rn = sb("rn", [P, 16, C], stage=stage)
            rksel = sb("rksel", [P, KT, 2], stage=stage)
            flat = lambda z: z[:].rearrange("p a b -> p (a b)")
            kap, rho = KR[:, :, 0, :], KR[:, :, 1, :]
            with nc.Block() as block:
                @block.scalar
                def _(act):
                    for f in range(KT):
                        ins = nc.scalar.activation(rn[:, 2 * f:2 * f + 2, :], kh[:, 2 * f:2 * f + 2, :], ACT.Square,
                                                   scale=v("rwkv_k_k", f))
                    ins.then_inc(key_sq, 1)
                    act.wait_ge(key_max, 4)
                    nc.scalar.activation(rn[:], rn[:], ACT.Sqrt).then_inc(key_root, 1)
                    act.wait_ge(decays, 1)
                    nc.scalar.activation(E1, Ls[:], ACT.Exp, scale=CD).then_inc(exps, 1)
                    nc.scalar.activation(E2[:], Ls[:], ACT.Exp, scale=-CD).then_inc(exps, 1)
                    act.wait_ge(decays, 2)
                    nc.scalar.activation(Lp[:], Lp[:], ACT.Exp, scale=CD).then_inc(exps, 1)
                    act.wait_ge(decays, 3)
                    nc.scalar.activation(fac[:], fac[:], ACT.Exp, scale=CD)

                @block.tensor
                def _(pe):
                    pe.wait_ge(key_sq, 1)
                    for b in range(4):
                        nc.tensor.matmul(pb[b][:], const("headones"), flat(rn)[:, b * 512:(b + 1) * 512],
                                         start=True, stop=True).then_inc(key_sum, 1)
                    pe.wait_ge(bonus_in, 1)
                    for f in range(KT):
                        for t in range(TT):
                            ins = nc.tensor.matmul(pb[4][:, t * HEADS + 2 * f:t * HEADS + 2 * f + 2], rn[:, 2 * f + t, :],
                                                   rksel[:, f, :], start=True, stop=True)
                    ins.then_inc(bonus_done, 1)

                @block.vector
                def _(dve):
                    for i in range(16):
                        ins = nc.vector.tensor_tensor_scan(Lp[:, i, :], const("ones"), kap[:, i, :], 0.0, ALU.mult, ALU.add)
                    dve_step.link(dve, ins)
                    mid = Lp[:, :, C // 2 - 1:C // 2]
                    dve_step.link(dve, nc.vector.tensor_tensor(Ls[:], Lp[:], mid.broadcast_to([P, 16, C]), ALU.subtract))
                    four = lambda z: z.rearrange("p (f c) t -> p f c t", c=2)
                    dve_step.link(dve, nc.vector.tensor_tensor(
                        fac[:].rearrange("p (f a) -> p f a", a=1), four(Ls)[:, :, 0, C - 1:C],
                        four(Lp[:])[:, :, 1, C // 2 - 1:C // 2], ALU.add))
                    ins = nc.vector.tensor_tensor(Lp[:], Ls[:], kap, ALU.subtract)
                    dve_step.link(dve, ins)
                    nc.vector.tensor_copy(stat[:, 4:5], stat[:, 0:1]).then_inc(decays, 3)
                    for b in range(4):
                        dve.wait_ge(key_sum, b + 1)
                        nc.vector.tensor_scalar(flat(rn)[:, b * 512:(b + 1) * 512], pb[b][:], 1e-24, None,
                                                ALU.max).then_inc(key_max, 1)
                    dve.wait_ge(key_root, 1)
                    dve_step.link(dve, nc.vector.reciprocal(rn[:], rn[:]))
                    for f in range(KT):
                        w = slice(2 * f, 2 * f + 2)
                        ins = nc.vector.scalar_tensor_tensor(kap[:, w, :], kh[:, w, :], v("rwkv_k_k", f), rn[:, w, :],
                                                             ALU.mult, ALU.mult)
                    dve_step.link(dve, ins)
                    for f in range(KT):
                        w = slice(2 * f, 2 * f + 2)
                        ins = nc.vector.tensor_scalar(rn[:, w, :], bet[:, w, :], 1.0, v("rwkv_k_a", f), ALU.subtract, ALU.mult)
                    dve_step.link(dve, ins)
                    dve_step.link(dve, nc.vector.scalar_tensor_tensor(kh[:], rn[:], 1.0, kh[:], ALU.add, ALU.mult))
                    dve_step.mark(nc.vector.tensor_tensor(bet[:], bet[:], kap, ALU.mult))
                    for f in range(KT):
                        ins = nc.vector.tensor_scalar(rksel[:, f, :], const("headsel"), v("rwkv_r_k", f), None, ALU.mult)
                    dve_step.mark(ins)
                    nc.vector.tensor_tensor(rn[:], rho, kh[:], ALU.mult).then_inc(bonus_in, 1)
                    dve_step.wait(dve)
                    dve.wait_ge(bonus_in, 1)
                    dve.wait_ge(exps, 3)
                    nc.vector.tensor_tensor(bet[:], bet[:], E2[:], ALU.mult)
                    nc.vector.tensor_tensor(kh[:], kh[:], E2[:], ALU.mult)
                    nc.vector.tensor_tensor(kap, kap, Lp[:], ALU.mult)
                    nc.vector.tensor_tensor(rho, rho, E1, ALU.mult)
                    dve.wait_ge(bonus_done, 1)
                    nc.vector.tensor_copy(bonus[:].rearrange("p t h -> p (t h)"), pb[4][:, 0:2 * HEADS])

        pairs_done = sem("pairs_done")
        pairs_read = sem("pairs_read")
        level_in = sem("level_in")
        y_done = sem("y_done")
        y_copied = sem("y_copied")
        x_done = sem("x_done")
        x_new = sem("x_new")
        w_done, w_copied, u_done, u_copied, o_done, o_copied = (sem(n) for n in (
            "w_done", "w_copied", "u_done", "u_copied", "o_done", "o_copied"))
        tok_done, tok_copied, s_done, s_copied = (sem(n) for n in ("tok_done", "tok_copied", "s_done", "s_copied"))
        Y = xn
        with ExitStack() as stage:
            AD = sb("AD", [P, 2, 4, 256], stage=stage)
            BE = sb("BE", [P, 2, 4, 256], stage=stage)
            N = sb("N", [P, 2, 2, 4, C], stage=stage)
            X, XT = (AT[:, 4 * i:4 * i + 4, :].rearrange("p k t -> p (k t)").rearrange("p (g h c) -> p g h c", g=2, h=4)
                     for i in range(2))
            YS = sb("YS", [P, 2, 4, C], stage=stage)
            W = sb("W", [P, 2, 4, DH], stage=stage)
            U = sb("U", [P, 2, 4, DH], stage=stage)
            BT = sb("BT", [P, 2, 4, C], stage=stage)
            four = lambda z: z.rearrange("p (h n) -> p h n", h=4)
            rounds = [(c, d) for c in range(2) for d in range(2)]
            with nc.Block() as block:
                def heads(d, g):
                    return [(par, i, 4 * d + 2 * g + i) for par in range(2) for i in range(2)]

                @block.tensor
                def _(pe):
                    for r, (c, d) in enumerate(rounds):
                        for g in range(2):
                            if r:
                                pe.wait_ge(o_copied, 2 * (r - 1) + 2)
                                if c == 0 or r == 2:
                                    pe.wait_ge(s_copied, 2 * min(r, 2))
                            for j, (par, i, f) in enumerate(heads(d, g)):
                                rows = slice(DH * par, DH * par + DH)
                                both = KR[rows, 2 * f + c, :, :].rearrange("p a t -> p (a t)")
                                nc.tensor.matmul(pb[4 * g + par][:, i * 256:(i + 1) * 256], bet[rows, 2 * f + c, :], both,
                                                 start=True, stop=True)
                                ins = nc.tensor.matmul(pb[4 * g + 2 + par][:, i * 256:(i + 1) * 256], kh[rows, 2 * f + c, :],
                                                       both, start=True, stop=True)
                            ins.then_inc(pairs_done, 1)
                        for lv in range(7):
                            at = 7 * r + lv
                            for g in range(2):
                                pe.wait_ge(level_in, 2 * at + g + 1)
                                if lv == 0:
                                    pe.wait_ge(pairs_read, 2 * r + 2)
                                else:
                                    pe.wait_ge(x_new, 2 * (at - 1) + g + 1)
                                for j in range(4):
                                    ins = nc.tensor.matmul(pb[g][:, j * C:(j + 1) * C], N[:, at % 2, g, j, :],
                                                           X[:, g, j, :] if lv else ident, start=True, stop=True)
                                ins.then_inc(y_done, 1)
                            if lv:
                                for g in range(2):
                                    pe.wait_ge(y_copied, 2 * (6 * r + lv - 1) + g + 1)
                                    for j in range(4):
                                        if lv < 6:
                                            nc.tensor.matmul(pb[2 + g][:, j * C:(j + 1) * C], XT[:, g, j, :], YS[:, g, j, :],
                                                             start=True, stop=True)
                                        ins = nc.tensor.matmul(pb[4 + g][:, j * C:(j + 1) * C], YS[:, g, j, :], XT[:, g, j, :],
                                                               start=True, stop=True)
                                    ins.then_inc(x_done, 1)
                        for g in range(2):
                            pe.wait_ge(x_new, 2 * (7 * r + 6) + g + 1)
                            for par, i, f in heads(d, g):
                                h = 2 * f + par
                                o = pb[2 * g + par][:, i * DH:(i + 1) * DH]
                                rows = slice(DH * par, DH * par + DH)
                                ins = nc.tensor.matmul(o, BE[:, g, 2 * par + i, 0:C], V[:, c, h * DH:(h + 1) * DH],
                                                       start=True, stop=(c == 0))
                                if c:
                                    ins = nc.tensor.matmul(o, KR[rows, 2 * f + c, 0, :], S0[rows, f, :], start=False, stop=True)
                            ins.then_inc(w_done, 1)
                        for g in range(2):
                            pe.wait_ge(w_copied, 2 * r + g + 1)
                            for j in range(4):
                                ins = nc.tensor.matmul(pb[4 + g][:, j * DH:(j + 1) * DH], XT[:, g, j, :], W[:, g, j, :],
                                                       start=True, stop=True)
                            ins.then_inc(u_done, 1)
                        if c == 0:
                            for g in range(2):
                                for z, src in enumerate((bet, kh)):
                                    for i in range(2):
                                        f = 4 * d + 2 * g + i
                                        ins = nc.tensor.transpose(pb[6 + g][:, (2 * z + i) * C:(2 * z + i + 1) * C],
                                                                  src[:, 2 * f + c, :], ident)
                                ins.then_inc(tok_done, 1)
                        for g in range(2):
                            pe.wait_ge(u_copied, 2 * r + g + 1)
                            for par, i, f in heads(d, g):
                                h, j = 2 * f + par, 2 * par + i
                                o = pb[2 * g + par][:, i * DH:(i + 1) * DH]
                                rows = slice(DH * par, DH * par + DH)
                                nc.tensor.matmul(o, AD[:, g, j, C:2 * C], U[:, g, j, :], start=True, stop=False)
                                ins = nc.tensor.matmul(o, BE[:, g, j, C:2 * C], V[:, c, h * DH:(h + 1) * DH],
                                                       start=False, stop=(c == 0))
                                if c:
                                    ins = nc.tensor.matmul(o, KR[rows, 2 * f + c, 1, :], S0[rows, f, :], start=False, stop=True)
                            ins.then_inc(o_done, 1)
                        if c == 0:
                            for g in range(2):
                                pe.wait_ge(tok_copied, 2 * r + g + 1)
                                for par, i, f in heads(d, g):
                                    h, j = 2 * f + par, 2 * par + i
                                    o = pb[4 + g][DH * par:DH * par + DH, i * DH:(i + 1) * DH]
                                    nc.tensor.matmul(o, BT[:, g, i, DH * par:DH * par + DH], U[:, g, j, :], start=True, stop=False)
                                    ins = nc.tensor.matmul(o, BT[:, g, 2 + i, DH * par:DH * par + DH],
                                                           V[:, c, h * DH:(h + 1) * DH], start=False, stop=True)
                                ins.then_inc(s_done, 1)

                @block.gpsimd
                def _(pool):
                    for r in range(4):
                        for lv in range(7):
                            for g in range(2):
                                at = 7 * r + lv
                                if lv == 0:
                                    pool.wait_ge(pairs_read, 2 * r + g + 1)
                                if at >= 2:
                                    pool.wait_ge(y_done, 2 * (at - 2) + g + 1)
                                if lv == 2:
                                    pool.wait_ge(x_new, 2 * (at - 2) + g + 1)
                                mask = const(f"level{lv}").rearrange("p (a t) -> p a t", a=1).broadcast_to([P, 4, C])
                                pool.tensor_tensor(N[:, at % 2, g, :, :], AD[:, g, :, 0:C], mask, ALU.mult).then_inc(level_in, 1)

                @block.vector
                def _(dve):
                    idb = ident.rearrange("p (a t) -> p a t", a=1).broadcast_to([P, 4, C])
                    for r, (c, d) in enumerate(rounds):
                        for g in range(2):
                            dve.wait_ge(pairs_done, 2 * r + g + 1)
                            for par in range(2):
                                for z, dst in enumerate((AD, BE)):
                                    ins = nc.vector.tensor_tensor(
                                        dst[:, g, 2 * par:2 * par + 2, :].rearrange("p h n -> p (h n)"),
                                        pb[4 * g + 2 * z + par][:], const("pairmask"), ALU.mult)
                            ins.then_inc(pairs_read, 1)
                        for lv in range(7):
                            at = 7 * r + lv
                            for g in range(2):
                                if lv == 0:
                                    dve.wait_ge(y_done, 2 * at + g + 1)
                                    nc.vector.tensor_tensor(X[:, g, :, :], idb, four(pb[g][:]), ALU.subtract)
                                    nc.vector.tensor_tensor(XT[:, g, :, :], idb, N[:, at % 2, g, :, :], ALU.subtract).then_inc(x_new, 1)
                                    continue
                                dve.wait_ge(x_done, 2 * (6 * r + lv - 1) + g + 1)
                                dve.wait_ge(x_new, 2 * at - 2 + g + 1)
                                if lv < 6:
                                    nc.vector.tensor_tensor(X[:, g, :, :], X[:, g, :, :], four(pb[2 + g][:]), ALU.subtract)
                                nc.vector.tensor_tensor(XT[:, g, :, :], XT[:, g, :, :], four(pb[4 + g][:]),
                                                        ALU.subtract).then_inc(x_new, 1)
                        if c == 0:
                            for g in range(2):
                                dve.wait_ge(tok_done, 2 * r + g + 1)
                                nc.vector.tensor_copy(BT[:, g, :, :], four(pb[6 + g][:])).then_inc(tok_copied, 1)
                            for g in range(2):
                                dve.wait_ge(s_done, 2 * r + g + 1)
                                for i in range(2):
                                    f = 4 * d + 2 * g + i
                                    ins = nc.vector.tensor_scalar(S0[:, f, :], pb[4 + g][:, i * DH:(i + 1) * DH],
                                                                  fac[:, f:f + 1], None, ALU.mult)
                                ins.then_inc(s_copied, 1)

                @block.scalar
                def _(act):
                    for r, (c, d) in enumerate(rounds):
                        for lv in range(1, 7):
                            for g in range(2):
                                act.wait_ge(y_done, 2 * (7 * r + lv) + g + 1)
                                nc.scalar.copy(YS[:, g, :, :], four(pb[g][:])).then_inc(y_copied, 1)
                        for g in range(2):
                            act.wait_ge(w_done, 2 * r + g + 1)
                            for par in range(2):
                                ins = nc.scalar.copy(W[:, g, 2 * par:2 * par + 2, :],
                                                     pb[2 * g + par][:, 0:2 * DH].rearrange("p (h n) -> p h n", h=2))
                            ins.then_inc(w_copied, 1)
                        for g in range(2):
                            act.wait_ge(u_done, 2 * r + g + 1)
                            nc.scalar.mul(U[:, g, :, :], four(pb[4 + g][:, 0:4 * DH]), -1.0).then_inc(u_copied, 1)
                        for g in range(2):
                            act.wait_ge(o_done, 2 * r + g + 1)
                            for par in range(2):
                                f = 4 * d + 2 * g
                                dst = Y[:, c, :].rearrange("p (f a n) -> p f a n", a=2, n=DH)[:, f:f + 2, par, :]
                                ins = nc.scalar.copy(dst, pb[2 * g + par][:, 0:2 * DH].rearrange("p (h n) -> p h n", h=2))
                            ins.then_inc(o_copied, 1)

        lnx_in = sem("lnx_in")
        y_sq = sem("y_sq")
        y_centred = sem("y_centred")
        y_var = sem("y_var")
        y_root = sem("y_root")
        y_ready = sem("y_ready")
        y_turned = sem("y_turned")
        with ExitStack() as stage:
            lw = sb("lw", [P, D], stage=stage)
            lb = sb("lb", [P, D], stage=stage)
            sq = sb("sq", [P, TT, D], stage=stage)
            hs = sb("hs", [P, 2, TT * HEADS], stage=stage)
            open_acts(stage)
            no = new_split()
            after = ffn_plan[1]["gate", 0]
            ahead(after + 2)
            hv = lambda z: z.rearrange("p t (h n) -> p (t h) n", n=DH)
            one = lambda z: z.rearrange("p (h a) -> p h a", a=1).broadcast_to([P, TT * HEADS, DH])
            with nc.Block() as block:
                @block.sync
                def _(sp):
                    sp.dma_start(lw[:], a["rwkv_lnx_w"][0:1, :].broadcast_to([P, D])).then_inc(lnx_in, 16)
                    sp.dma_start(lb[:], a["rwkv_lnx_b"][0:1, :].broadcast_to([P, D])).then_inc(lnx_in, 16)
                    feed(sp)

                @block.vector
                def _(dve):
                    L = lambda ins: dve_step.link(dve, ins)
                    L(nc.vector.reduce_sum(hs[:, 0, :], hv(Y[:]), AX))
                    L(nc.vector.tensor_scalar(hs[:, 0, :], hs[:, 0, :], 1.0 / DH, None, ALU.mult))
                    nc.vector.tensor_tensor(hv(Y[:]), hv(Y[:]), one(hs[:, 0, :]), ALU.subtract).then_inc(y_centred, 1)
                    dve.wait_ge(y_sq, 1)
                    nc.vector.reduce_sum(hs[:, 1, :], hv(sq[:]), AX).then_inc(y_var, 1)
                    dve.wait_ge(y_root, 1)
                    L(nc.vector.reciprocal(hs[:, 1, :], hs[:, 1, :]))
                    L(nc.vector.tensor_tensor(hv(Y[:]), hv(Y[:]), one(hs[:, 1, :]), ALU.mult))
                    dve.wait_ge(lnx_in, 32)
                    rowb = lambda z: z.rearrange("p (a n) -> p a n", a=1).broadcast_to([P, TT, D])
                    L(nc.vector.tensor_tensor(Y[:], Y[:], rowb(lw[:]), ALU.mult))
                    dve_step.mark(nc.vector.tensor_tensor(Y[:], Y[:], rowb(lb[:]), ALU.add))
                    L(nc.vector.tensor_tensor(hv(sq[:]), hv(V[:]), one(bonus[:].rearrange("p t h -> p (t h)")), ALU.mult))
                    nc.vector.tensor_tensor(Y[:], Y[:], sq[:], ALU.add).then_inc(y_ready, 1)
                    for b in range(4):
                        dve.wait_ge(y_turned, b + 1)
                        w = slice(2 * b, 2 * b + 2)
                        ins = nc.vector.tensor_tensor(AT[:, w, :].rearrange("p f t -> p (f t)"), pb[b][:],
                                                      G[:, w, :].rearrange("p f t -> p (f t)"), ALU.mult)
                        ins.then_inc(at_ready[b], 1)
                    for c in range(4):
                        at_rest(dve, no, c)
                    rest_to(dve, after + 2)
                    add_projected(dve, n0 + 4)

                @block.scalar
                def _(act):
                    act.wait_ge(y_centred, 1)
                    nc.scalar.activation(sq[:], Y[:], ACT.Square).then_inc(y_sq, 1)
                    act.wait_ge(y_var, 1)
                    nc.scalar.activation(hs[:, 1, :], hs[:, 1, :], ACT.Sqrt, scale=1.0 / DH,
                                         bias=const("lnx_eps")).then_inc(y_root, 1)
                    for c in range(4):
                        at_round(act, no, c)
                    round_to(act, after + 2)

                @block.tensor
                def _(pe):
                    pe.wait_ge(y_ready, 1)
                    for b in range(4):
                        for i in range(2):
                            for t in range(TT):
                                f = 2 * b + i
                                ins = nc.tensor.transpose(pb[b][:, i * T + t * P:i * T + (t + 1) * P],
                                                          Y[:, t, f * P:(f + 1) * P], ident)
                        ins.then_inc(y_turned, 1)
                    for c in range(4):
                        pe.wait_ge(at_lo, 4 * no + c + 1)
                        project(pe, n0 + c, c, 4, acts)
        rwkv.close()
        if upto <= 3:
            return finish()

        cos2, sin2 = sb("cos2", [P, T]), sb("sin2", [P, T])
        seen = sb("seen", [P, TT, T])
        nlam = sb("nlam", [P, 2])
        decay8 = sb("decay8", [P, 8])
        two_in = sem("two_in")
        two_exp = sem("two_exp")
        two_ready = sem("two_ready")
        lam0 = [0.8 - 0.6 * math.exp(-0.3 * l) for l in range(2)]
        TWO_PI = 2.0 * math.pi
        C1 = 6.28125
        C2 = float(np.round((TWO_PI - C1) * 2 ** 21) / 2 ** 21)
        C3 = TWO_PI - C1 - C2
        MAGIC = 1.5 * 2.0 ** 23
        with ExitStack() as stage:
            posb = sb("posb", [P, T], I32, stage=stage)
            posq = sb("posq", [P, TT], I32, stage=stage)
            fl = sb("fl", [P, 4, T], stage=stage)
            cq = sb("cq", [P, TT], stage=stage)
            lams = sb("lams", [P, 4, 2, DH], stage=stage)
            dots = sb("dots", [P, 2, 2], stage=stage)
            sp8 = sb("sp8", [P, 6, 8], stage=stage)
            with nc.Block() as block:
                @block.sync
                def _(sp):
                    sp.dma_start(posb[:], a["positions_2"][0:1, :].broadcast_to([P, T])).then_inc(two_in, 16)
                    sp.dma_start(posq[:], a["positions_2"][0].rearrange("(t p) -> p t", p=P), allow_slow_non_contiguous=True).then_inc(two_in, 16)
                    for i, n in enumerate(("lam_q1_2", "lam_k1_2", "lam_q2_2", "lam_k2_2")):
                        sp.dma_start(lams[:, i, :, :].rearrange("p l d -> p (l d)"),
                                     a[n].rearrange("(a l) d -> a (l d)", a=1).broadcast_to([P, 2 * DH])).then_inc(two_in, 16)

                @block.vector
                def _(dve):
                    L = lambda ins: dve_step.link(dve, ins)
                    ts, tt = nc.vector.tensor_scalar, nc.vector.tensor_tensor
                    dve.wait_ge(two_in, 96)
                    L(nc.vector.tensor_copy(fl[:, 0, :], posb[:]))
                    L(ts(fl[:, 0, :], fl[:, 0, :], const("inv"), None, ALU.mult))
                    L(ts(fl[:, 1, :], fl[:, 0, :], 1.0 / TWO_PI, MAGIC, ALU.mult, ALU.add))
                    L(ts(fl[:, 1, :], fl[:, 1, :], MAGIC, None, ALU.subtract))
                    for part in (C1, C2, C3):
                        L(nc.vector.scalar_tensor_tensor(fl[:, 0, :], fl[:, 1, :], -part, fl[:, 0, :], ALU.mult, ALU.add))
                    L(ts(fl[:, 2, :], fl[:, 0, :], math.pi / 2, None, ALU.add))
                    L(ts(fl[:, 3, :], fl[:, 2, :], math.pi, -TWO_PI, ALU.is_gt, ALU.mult))
                    L(tt(fl[:, 2, :], fl[:, 2, :], fl[:, 3, :], ALU.add))
                    PI = 3.1415925
                    L(ts(fl[:, 2, :], fl[:, 2, :], PI, -PI, ALU.min, ALU.max))
                    ts(fl[:, 0, :], fl[:, 0, :], PI, -PI, ALU.min, ALU.max).then_inc(two_ready, 1)
                    dve_step.mark(nc.vector.tensor_scalar(posq[:], posq[:], 6, None, ALU.arith_shift_right))
                    L(nc.vector.tensor_scalar(posb[:], posb[:], 6, None, ALU.arith_shift_right))
                    dve_step.mark(nc.vector.tensor_copy(cq[:], posq[:]))
                    L(nc.vector.tensor_copy(fl[:, 3, :], posb[:]))
                    for t in range(TT):
                        dve_step.mark(ts(seen[:, t, :], fl[:, 3, :], cq[:, t:t + 1], 1.0, ALU.is_le, ALU.subtract))
                    dve_step.wait(dve)
                    dve_step.mark(ts(seen[:], seen[:], BIG, None, ALU.mult))
                    for i in range(2):
                        dve_step.mark(tt(lams[:, 2 * i, :, :], lams[:, 2 * i, :, :], lams[:, 2 * i + 1, :, :], ALU.mult))
                    dve_step.wait(dve)
                    for i in range(2):
                        ins = nc.vector.reduce_sum(dots[:, i, :], lams[:, 2 * i, :, :], AX)
                    ins.then_inc(two_ready, 1)
                    lam = v("lru_lambda_2", 0, 8)
                    L(ts(sp8[:, 0, :], lam, -1.0, None, ALU.mult))
                    L(tt(sp8[:, 1, :], sp8[:, 0, :], lam, ALU.min))
                    ts(sp8[:, 0, :], sp8[:, 0, :], 0.0, None, ALU.max).then_inc(two_ready, 1)
                    dve.wait_ge(two_exp, 1)
                    ts(sp8[:, 2, :], sp8[:, 1, :], 1.0, None, ALU.add).then_inc(two_ready, 1)
                    dve.wait_ge(two_ready, 4)
                    L(ts(sp8[:, 3, :], sp8[:, 2, :], 1.0, None, ALU.subtract))
                    L(ts(sp8[:, 4, :], sp8[:, 3, :], 0.0, None, ALU.is_equal))
                    L(tt(sp8[:, 3, :], sp8[:, 3, :], sp8[:, 4, :], ALU.add))
                    L(nc.vector.reciprocal(sp8[:, 3, :], sp8[:, 3, :]))
                    dve.wait_ge(two_exp, 2)
                    L(tt(sp8[:, 5, :], sp8[:, 5, :], sp8[:, 3, :], ALU.mult))
                    L(tt(sp8[:, 5, :], sp8[:, 5, :], sp8[:, 4, :], ALU.add))
                    L(tt(sp8[:, 5, :], sp8[:, 5, :], sp8[:, 1, :], ALU.mult))
                    L(tt(sp8[:, 5, :], sp8[:, 5, :], sp8[:, 0, :], ALU.add))
                    dve_step.mark(ts(decay8[:], sp8[:, 5, :], -8.0, None, ALU.mult))
                    dve.wait_ge(two_exp, 3)
                    for l in range(2):
                        L(tt(nlam[:, l:l + 1], dots[:, 1, l:l + 1], dots[:, 0, l:l + 1], ALU.subtract))
                        L(ts(nlam[:, l:l + 1], nlam[:, l:l + 1], -lam0[l], None, ALU.add))

                @block.scalar
                def _(act):
                    act.wait_ge(two_ready, 1)
                    nc.scalar.activation(sin2[:], fl[:, 0, :], ACT.Sin)
                    nc.scalar.activation(cos2[:], fl[:, 2, :], ACT.Sin)
                    act.wait_ge(two_ready, 3)
                    nc.scalar.activation(sp8[:, 1, :], sp8[:, 1, :], ACT.Exp).then_inc(two_exp, 1)
                    act.wait_ge(two_ready, 4)
                    nc.scalar.activation(sp8[:, 5, :], sp8[:, 2, :], ACT.Ln).then_inc(two_exp, 1)
                    nc.scalar.activation(dots[:], dots[:], ACT.Exp).then_inc(two_exp, 1)

        make_gates(0)
        open_acts(ctx)
        no = norm_turn(3, lambda f: v("norm_ffn", KT + f), then=ffn_plan[1]["gate", 0], look=2)
        ffn(1, no, first["win0"], conv=1, gate_rows=0, finished=0)
        if upto <= 4:
            return finish()
        norm_rows(4, a["norm_final"].rearrange("(a d) -> a d", a=1))
        if upto <= 5:
            return finish()

        lru_in = sem("lru_in")
        pads_clear = sem("pads_clear")
        win_read = sem("win_read")
        rot2 = sem("rot2")
        rotated2 = sem("rotated2")
        lru_conv = sem("lru_conv")
        lru_gate = sem("lru_gate")
        lru_gate_read = sem("lru_gate_read")
        lru_log = sem("lru_log")
        lru_exp = sem("lru_exp")
        lru_mult = sem("lru_mult")
        d_scored, d_masked, d_maxed, d_exped, d_mixed = (sem("d_" + n) for n in ("scored", "masked", "maxed", "exped", "mixed"))
        d_turned, d_copied, d_out, d_read = (sem("d_" + n) for n in ("turned", "copied", "out", "read"))
        o_sq, o_var, o_root, o_norm, o_turned = (sem("o_" + n) for n in ("sq", "var", "root", "norm", "turned"))

        def mixer(l, no, then):
            n0, n1 = first[f"win{l}"], first[f"wout{l}"]
            ahead(n1 + 3)
            own = new_split()
            with ExitStack() as stage:
                QK = sb(f"QK{l}", [P, 8, T], stage=stage)
                V = sb(f"V{l}", [P, TT, 512], stage=stage)
                lru = ExitStack()
                xp = sb(f"xp{l}", [P, 4, T + 3], stage=lru)
                xc = sb(f"xc{l}", [P, 4, T], stage=lru)
                yr = sb(f"yr{l}", [P, 4, T], stage=lru)
                rg = sb(f"rg{l}", [P, 4, T], stage=lru)
                ig = sb(f"ig{l}", [P, 4, T], stage=lru)
                e2, th = (xn[:, i, :].rearrange("p (f t) -> p f t", f=4) for i in range(2))
                raw = sb(f"raw{l}", [P, 2, 2 * T], stage=lru)
                rc = sb(f"rc{l}", [P, 2, 2 * T], stage=lru)
                rs = sb(f"rs{l}", [P, 2, 2 * T], stage=lru)
                bd = [sb(f"bd{i}{l}", [P, 4, P], stage=lru) for i in range(2)]
                with nc.Block() as block:
                    @block.sync
                    def _(sp):
                        feed(sp)

                    @block.gpsimd
                    def _(pool):
                        for b in bd:
                            ins = pool.memset(b[:], 0.0)
                            ins.then_inc(pads_clear, 1)
                        pool.memset(xp[:, :, 0:3], 0.0).then_inc(pads_clear, 1)
                        pool.wait_ge(pads_clear, 3 * l + 3)
                        for b, name in zip(bd, ("gate_a_w_2", "gate_x_w_2")):
                            for par in range(2):
                                pool.dma_start(b[DH * par:DH * par + DH, :, DH * par:DH * par + DH],
                                               a[name][l, par::2].rearrange("n h k -> h n k")).then_inc(lru_in, 16)

                    @block.tensor
                    def _(pe):
                        pe.wait_ge(at_lo, 4 * no + 4)
                        for i in range(10):
                            if i >= 3:
                                pe.wait_ge(win_read, 10 * l + i - 2)
                            (to_tokens if i >= 8 else to_features)(pe, n0 + i, pb[i % 3])
                            if 5 <= i <= 8:
                                b = i - 5
                                pe.wait_ge(win_read, 10 * l + i)
                                if b >= 2:
                                    pe.wait_ge(rotated2, 4 * l + b - 1)
                                nc.tensor.matmul(pb[4 + b % 2][:], const("rot"), raw[:, b % 2, :], start=True,
                                                 stop=True).then_inc(rot2, 1)
                            if i == 4:
                                pe.wait_ge(lru_in, 64 * (l + 1))
                                pe.wait_ge(lru_conv, l + 1)
                                for q in range(4):
                                    if q == 3:
                                        pe.wait_ge(lru_gate_read, 4 * l + 1)
                                    for f in range(2):
                                        ft = 2 * (q % 2) + f
                                        ins = nc.tensor.matmul(pb[(6, 7, 3, 6)[q]][:, f * T:(f + 1) * T], bd[q // 2][:, ft, :],
                                                               xc[:, ft, :], start=True, stop=True)
                                    ins.then_inc(lru_gate, 1)

                    @block.scalar
                    def _(act):
                        def read(i):
                            round_to(act, n0 + i + 3)
                            act.wait_ge(used, n0 + i + 1)
                            two = pb[i % 3][:].rearrange("p (f t) -> p f t", f=2)
                            if i < 2:
                                dst = xp[:, 2 * i:2 * i + 2, 3:]
                            elif i < 4:
                                dst = yr[:, 2 * i - 4:2 * i - 2, :]
                            elif i < 8:
                                if i >= 6:
                                    act.wait_ge(rotated2, 4 * l + i - 5)
                                dst = raw[:, i % 2, :].rearrange("p (f t) -> p f t", f=2)
                            else:
                                dst = V[:, :, (i - 8) * 256:(i - 7) * 256]
                            nc.scalar.copy(dst, two).then_inc(win_read, 1)

                        for i in range(5):
                            read(i)
                        for q in range(4):
                            act.wait_ge(lru_gate, 4 * l + q + 1)
                            for f in range(2):
                                ft = 2 * (q % 2) + f
                                ins = nc.scalar.activation((rg, ig)[q // 2][:, ft, :], pb[(6, 7, 3, 6)[q]][:, f * T:(f + 1) * T],
                                                           ACT.Sigmoid, bias=v(("gate_a_b_2", "gate_x_b_2")[q // 2], 4 * l + ft))
                            ins.then_inc(lru_gate_read, 1)
                        read(5)
                        read(6)
                        act.wait_ge(lru_log, l + 1)
                        nc.scalar.activation(e2, rg[:], ACT.Exp, scale=2.0)
                        nc.scalar.activation(th, rg[:], ACT.Tanh, scale=-1.0).then_inc(act_step.sem, 1)
                        act_step.n += 1
                        act_step.wait(act)
                        nc.scalar.activation(rg[:], rg[:], ACT.Exp).then_inc(lru_exp, 1)
                        read(7)
                        act.wait_ge(lru_mult, l + 1)
                        nc.scalar.activation(th, th, ACT.Sqrt).then_inc(lru_exp, 1)
                        nc.scalar.activation(yr[:], yr[:], ACT.Gelu_apprx_tanh).then_inc(lru_exp, 1)
                        read(8)
                        read(9)
                        round_to(act, n1 + 3)

                    @block.vector
                    def _(dve):
                        L = lambda ins: dve_step.link(dve, ins)

                        def rotate(b):
                            three = lambda z: z.rearrange("p (f t) -> p f t", f=2)
                            cos = cos2[:].rearrange("p (a t) -> p a t", a=1).broadcast_to([P, 2, T])
                            sin = sin2[:].rearrange("p (a t) -> p a t", a=1).broadcast_to([P, 2, T])
                            rest_to(dve, n0 + 4 + b + 3)
                            dve.wait_ge(win_read, 10 * l + 5 + b)
                            dve_step.mark(nc.vector.tensor_tensor(three(rc[:, b % 2, :]), three(raw[:, b % 2, :]), cos, ALU.mult))
                            dve.wait_ge(rot2, 4 * l + b + 1)
                            L(nc.vector.tensor_tensor(three(rs[:, b % 2, :]), three(pb[4 + b % 2][:]), sin, ALU.mult))
                            nc.vector.tensor_tensor(QK[:, 2 * b:2 * b + 2, :].rearrange("p f t -> p (f t)"), rc[:, b % 2, :],
                                                    rs[:, b % 2, :], ALU.add).then_inc(rotated2, 1)

                        rest_to(dve, n0 + 4)
                        dve.wait_ge(pads_clear, 3 * l + 3)
                        dve.wait_ge(win_read, 10 * l + 2)
                        for i in range(4):
                            for ft in range(4):
                                w = v("conv_w_2", (l * 4 + 3 - i) * 4 + ft)
                                src, dst = xp[:, ft, 3 - i:3 - i + T], xc[:, ft, :]
                                if i == 0:
                                    ins = nc.vector.tensor_scalar(dst, src, w, v("conv_b_2", 4 * l + ft), ALU.mult, ALU.add)
                                else:
                                    ins = nc.vector.scalar_tensor_tensor(dst, src, w, dst, ALU.mult, ALU.add)
                                if i == 3 and ft == 3:
                                    ins.then_inc(lru_conv, 1)
                                else:
                                    dve_step.mark(ins)
                            if i < 3:
                                dve_step.wait(dve)
                            if i == 0:
                                rest_to(dve, n0 + 5)
                            if i == 2:
                                rest_to(dve, n0 + 6)
                        rest_to(dve, n0 + 7)
                        dve.wait_ge(lru_gate_read, 4 * l + 4)
                        for ft in range(4):
                            ins = nc.vector.tensor_scalar(rg[:, ft, :], rg[:, ft, :], decay8[:, 4 * l + ft:4 * l + ft + 1], None, ALU.mult)
                        ins.then_inc(lru_log, 1)
                        dve.wait_ge(lru_conv, l + 1)
                        L(nc.vector.tensor_tensor(ig[:], ig[:], xc[:], ALU.mult))
                        rotate(0)
                        rotate(1)
                        dve.wait_ge(lru_exp, 3 * l + 1)
                        nc.vector.scalar_tensor_tensor(th, e2, 1.0, th, ALU.add, ALU.mult).then_inc(lru_mult, 1)
                        rotate(2)
                        dve.wait_ge(lru_exp, 3 * l + 2)
                        L(nc.vector.tensor_tensor(ig[:], ig[:], th, ALU.mult))
                        for ft in range(4):
                            ins = nc.vector.tensor_tensor_scan(xc[:, ft, :], rg[:, ft, :], ig[:, ft, :], 0.0, ALU.mult, ALU.add)
                        L(ins)
                        rotate(3)
                        rest_to(dve, n0 + 12)
                        dve.wait_ge(lru_exp, 3 * l + 3)
                        for c in range(2):
                            w = slice(2 * c, 2 * c + 2)
                            nc.vector.tensor_tensor(AT[:, w, :], xc[:, w, :], yr[:, w, :], ALU.mult).then_inc(at_ready[c], 1)
                        rest_to(dve, n1 + 3)
                lru.close()

                S = sb(f"S{l}", [P, 2, 2, 2 * T], stage=stage)
                st = sb(f"st{l}", [P, 4, 2, 3, TT], stage=stage)
                Pd = sb(f"Pd{l}", [P, 2, 2 * T], stage=stage)
                PT = sb(f"PT{l}", [P, 2, 2 * T], stage=stage)
                O = sb(f"O{l}", [P, TT, 4, P], stage=stage)
                osq = sb(f"osq{l}", [P, TT, 4, P], stage=stage)
                ov = sb(f"ov{l}", [P, 8], stage=stage)
                zz = sb(f"zz{l}", [P, 2, 512], stage=stage)
                sc = DH ** -0.5
                ahead(then + 2)
                with nc.Block() as block:
                    @block.tensor
                    def _(pe):
                        def score(h):
                            if h >= 2:
                                pe.wait_ge(d_masked, 8 * l + 2 * (h - 1))
                            for c in range(2):
                                rows = slice(DH * c, DH * c + DH)
                                for t in range(TT):
                                    ins = nc.tensor.matmul(pb[2 * (h % 2) + c][:, t * T:(t + 1) * T],
                                                           QK[rows, h, t * P:(t + 1) * P], QK[rows, 4 + h, :], start=True, stop=True)
                                ins.then_inc(d_scored, 1)

                        def turn(h):
                            pe.wait_ge(d_mixed, 4 * l + h + 1)
                            if h >= 2:
                                pe.wait_ge(d_copied, 4 * l + h - 1)
                            for t in range(TT):
                                for kt in range(2):
                                    ins = nc.tensor.transpose(pb[4 + h % 2][:, kt * T + t * P:kt * T + (t + 1) * P],
                                                              Pd[:, h % 2, t * T + kt * P:t * T + (kt + 1) * P], ident)
                            ins.then_inc(d_turned, 1)

                        def out(h):
                            pe.wait_ge(d_copied, 4 * l + h + 1)
                            if h >= 2:
                                pe.wait_ge(d_read, 4 * l + h - 1)
                            for t in range(TT):
                                for kt in range(2):
                                    ins = nc.tensor.matmul(pb[6 + h % 2][:, t * P:(t + 1) * P],
                                                           PT[:, h % 2, kt * T + t * P:kt * T + (t + 1) * P],
                                                           V[:, kt, h * P:(h + 1) * P], start=(kt == 0), stop=(kt == 1))
                            ins.then_inc(d_out, 1)

                        for i in range(6):
                            if i < 4:
                                score(i)
                            if 1 <= i <= 4:
                                turn(i - 1)
                            if i >= 2:
                                out(i - 2)
                        pe.wait_ge(o_norm, l + 1)
                        for h in range(4):
                            for t in range(TT):
                                ins = nc.tensor.transpose(pb[h // 2][:, (h % 2) * T + t * P:(h % 2) * T + (t + 1) * P], O[:, t, h, :], ident)
                        ins.then_inc(o_turned, 1)
                        pe.wait_ge(d_read, 4 * l + 4)
                        for c in range(4):
                            pe.wait_ge(at_lo, 4 * own + c + 1)
                            project(pe, n1 + c, c, 4, acts)

                    @block.sync
                    def _(sp):
                        feed(sp)

                    @block.vector
                    def _(dve):
                        def first_half(h):
                            for c in range(2):
                                dve.wait_ge(d_scored, 8 * l + 2 * h + c + 1)
                                nc.vector.tensor_tensor(S[:, h % 2, c, :], pb[2 * (h % 2) + c][:], seen[:].rearrange("p t k -> p (t k)"),
                                                        ALU.add).then_inc(d_masked, 1)
                            for c in range(2):
                                dve.wait_ge(d_masked, 8 * l + 2 * h + c + 1)
                                dve_step.mark(nc.vector.reduce_max(st[:, h, c, 0, :], S[:, h % 2, c, :].rearrange("p (t k) -> p t k", t=2), AX))
                            dve_step.wait(dve)
                            nc.vector.tensor_scalar(st[:, h, :, 0, :], st[:, h, :, 0, :], -sc, None, ALU.mult).then_inc(d_maxed, 1)

                        def second_half(h):
                            dve.wait_ge(d_exped, 16 * l + 4 * (h + 1))
                            dve_step.link(dve, nc.vector.reciprocal(st[:, h, :, 2, :], st[:, h, :, 1, :]))
                            dve_step.link(dve, nc.vector.tensor_scalar(st[:, h, 1, 2, :], st[:, h, 1, 2, :], nlam[:, l:l + 1], None, ALU.mult))
                            if h >= 2:
                                dve.wait_ge(d_turned, 4 * l + h - 1)
                            for t in range(TT):
                                w = slice(t * T, (t + 1) * T)
                                dve_step.mark(nc.vector.tensor_scalar(Pd[:, h % 2, w], S[:, h % 2, 0, w], st[:, h, 0, 2, t:t + 1], None, ALU.mult))
                            dve_step.wait(dve)
                            for t in range(TT):
                                w = slice(t * T, (t + 1) * T)
                                ins = nc.vector.scalar_tensor_tensor(Pd[:, h % 2, w], S[:, h % 2, 1, w], st[:, h, 1, 2, t:t + 1],
                                                                     Pd[:, h % 2, w], ALU.mult, ALU.add)
                            ins.then_inc(d_mixed, 1)

                        for h in range(5):
                            if h == 2:
                                for c in range(2):
                                    at_rest(dve, own, c)
                            if h >= 1:
                                second_half(h - 1)
                            if h < 4:
                                if h >= 2:
                                    dve.wait_ge(d_mixed, 4 * l + h - 1)
                                first_half(h)
                        dve.wait_ge(o_sq, l + 1)
                        nc.vector.reduce_sum(ov[:], osq[:].rearrange("p t h n -> p (t h) n"), AX).then_inc(o_var, 1)
                        dve.wait_ge(o_root, l + 1)
                        dve_step.link(dve, nc.vector.reciprocal(ov[:], ov[:]))
                        nc.vector.tensor_tensor(O[:].rearrange("p t h n -> p (t h) n"), O[:].rearrange("p t h n -> p (t h) n"),
                                                ov[:].rearrange("p (h a) -> p h a", a=1).broadcast_to([P, 8, P]), ALU.mult).then_inc(o_norm, 1)
                        dve.wait_ge(o_turned, l + 1)
                        for b in range(2):
                            nc.vector.tensor_scalar(AT[:, 4 + 2 * b:6 + 2 * b, :].rearrange("p f t -> p (f t)"), pb[b][:],
                                                    v("subln_g_2", l), 1.0 - lam0[l], ALU.mult, ALU.mult).then_inc(at_ready[2 + b], 1)
                        for c in range(2, 4):
                            at_rest(dve, own, c)
                        rest_to(dve, then + 2)
                        add_projected(dve, n1 + 4, gates[l][:, 0, :], zz)

                    @block.scalar
                    def _(act):
                        for c in range(2):
                            at_round(act, own, c)
                        for i in range(6):
                            if i < 4:
                                act.wait_ge(d_maxed, 4 * l + i + 1)
                                for c in range(2):
                                    for t in range(TT):
                                        w = slice(t * T, (t + 1) * T)
                                        nc.scalar.activation(S[:, i % 2, c, w], S[:, i % 2, c, w], ACT.Exp, scale=sc,
                                                             bias=st[:, i, c, 0, t:t + 1],
                                                             accum_out=st[:, i, c, 1, t:t + 1]).then_inc(d_exped, 1)
                            if 1 <= i <= 4:
                                h = i - 1
                                act.wait_ge(d_turned, 4 * l + h + 1)
                                if h >= 2:
                                    act.wait_ge(d_out, 4 * l + h - 1)
                                nc.scalar.copy(PT[:, h % 2, :], pb[4 + h % 2][:]).then_inc(d_copied, 1)
                            if i >= 2:
                                h = i - 2
                                act.wait_ge(d_out, 4 * l + h + 1)
                                nc.scalar.copy(O[:, :, h, :], pb[6 + h % 2][:, 0:2 * P].rearrange("p (t n) -> p t n", t=2)).then_inc(d_read, 1)
                        act.wait_ge(d_read, 4 * l + 4)
                        nc.scalar.activation(osq[:], O[:], ACT.Square).then_inc(o_sq, 1)
                        act.wait_ge(o_var, l + 1)
                        nc.scalar.activation(ov[:], ov[:], ACT.Sqrt, scale=1.0 / P, bias=const("rms_eps")).then_inc(o_root, 1)
                        for c in range(2, 4):
                            at_round(act, own, c)
                        round_to(act, then + 2)

        def shift(l, i):
            return lambda f: mods[:, l, 3 * i * KT + f:3 * i * KT + f + 1]

        def gain_of(l, i):
            return lambda f: gain2[:, l, i, f:f + 1]

        no = norm_turn(5, gain_of(0, 0), shift(0, 0), turns=4, then=first["win0"])
        mixer(0, no, ffn_plan[2]["gate", 0])
        if upto <= 6:
            return finish()
        make_gates(1)
        no = norm_turn(6, gain_of(0, 1), shift(0, 1), turns=5, then=ffn_plan[2]["gate", 0], look=2)
        ffn(2, no, first["win1"], scale=gates[0][:, 1, :], gate_rows=1, finished=1)
        if upto <= 7:
            return finish()
        no = norm_turn(7, gain_of(1, 0), shift(1, 0), turns=6, then=first["win1"])
        mixer(1, no, moe_weight - 2)
        if upto <= 8:
            return finish()

        norm_turn(8, gain_of(1, 1), shift(1, 1), turns=7, parts=False)
        m_sel, m_gath, m_xg, m_gt, m_gtc, m_sg, m_h = (sem("m_" + n) for n in ("sel", "gath", "xg", "gt", "gtc", "sg", "h"))
        m_t, m_ht, m_oe, m_sc, m_y = (sem("m_" + n) for n in ("t", "ht", "oe", "sc", "y"))
        m_xhi, m_xlo, m_hlo = (sem("m_" + n) for n in ("xhi", "xlo", "hlo"))
        router_in = sem("router_in")
        routed = sem("routed")
        ranked = sem("ranked")
        r_exp = sem("r_exp")
        r_top = sem("r_top")
        slot_no = sb("slot_no", [P, 2, TT, EXPERTS])
        gate_w = sb("gate_w", [P, TT, EXPERTS])
        info = sb("info", [1, 3 * EXPERTS], I32)
        yacc = sb("yacc", [P, TT, D])
        E = EXPERTS
        with ExitStack() as stage:
            router = sb("router", [P, KT, E], stage=stage)
            lg = sb("lg", [P, TT, E], stage=stage)
            w3 = [sb(f"w3_{i}", [P, TT, E], stage=stage) for i in range(6)]
            m = sb("m", [P, 8, TT], stage=stage)
            cn = sb("cn", [P, 4, E], stage=stage)

            def moe_hi(act, n, j):
                slot = (moe_first + j) % RING
                act.wait_ge(arrived[slot], n * (16 * EXPERT_BLOCKS // RING) + 16 * ((moe_first + j) // RING + 1))
                act.wait_ge(used, n * EXPERT_BLOCKS + (moe_weight + j - SPLITS + 1))
                nc.scalar.copy(split[0][:, (moe_weight + j) % SPLITS, :], ring[:, slot, :]).then_inc(hi_ready, 1)

            def moe_lo(dve, n, j):
                at = (moe_weight + j) % SPLITS
                dve.wait_ge(hi_ready, n * EXPERT_BLOCKS + (moe_weight + j + 1))
                nc.vector.tensor_tensor(split[1][:, at, :], ring[:, (moe_first + j) % RING, :],
                                        split[0][:, at, :].bitcast(F32), ALU.subtract).then_inc(taken, 1)

            with nc.Block() as block:
                @block.sync
                def _(sp):
                    sp.dma_start(router[:], a["moe_router_2"][0].rearrange("(k p) n -> p k n", p=P)).then_inc(router_in, 16)

                @block.gpsimd
                def _(pool):
                    pool.memset(yacc[:], 0.0).then_inc(m_y, 4)

                @block.tensor
                def _(pe):
                    pe.wait_ge(router_in, 16)
                    for t in range(TT):
                        for k in range(KT):
                            ins = nc.tensor.matmul(pb[0][:, t * E:(t + 1) * E], AT[:, k, t * P:(t + 1) * P], router[:, k, :],
                                                   start=(k == 0), stop=(k == KT - 1))
                    ins.then_inc(routed, 1)
                    sel = w3[2]
                    pe.wait_ge(r_top, 2)
                    nc.tensor.matmul(pb[1][:, 0:E], const("before"), sel[:, 0, :], start=True, stop=True)
                    nc.tensor.matmul(pb[1][:, E:2 * E], const("before"), sel[:, 1, :], start=True, stop=False)
                    nc.tensor.matmul(pb[1][:, E:2 * E], const("ones"), sel[:, 0, :], start=False, stop=True)
                    nc.tensor.matmul(pb[1][:, 2 * E:3 * E], const("ones"), sel[:, 0, :], start=True, stop=False)
                    nc.tensor.matmul(pb[1][:, 2 * E:3 * E], const("ones"), sel[:, 1, :], start=False, stop=True).then_inc(ranked, 1)

                @block.scalar
                def _(act):
                    for j in range(SPLITS):
                        moe_hi(act, 0, j)
                    act.wait_ge(r_top, 1)
                    nc.scalar.activation(m[:, 4, :], m[:, 4, :], ACT.Exp).then_inc(r_exp, 1)

                @block.vector
                def _(dve):
                    L = lambda ins: dve_step.link(dve, ins)
                    ts, tt = nc.vector.tensor_scalar, nc.vector.tensor_tensor
                    wide = lambda z: z.rearrange("p (t a) -> p t a", a=1).broadcast_to([P, TT, E])
                    iota8 = const("iota8").rearrange("p (t e) -> p t e", t=TT)
                    dve.wait_ge(routed, 1)
                    L(nc.vector.tensor_copy(lg[:].rearrange("p t e -> p (t e)"), pb[0][:, 0:TT * E]))
                    for n in range(2):
                        s1, eq = w3[n], w3[3]
                        L(nc.vector.reduce_max(m[:, n, :], lg[:], AX))
                        L(tt(eq[:], lg[:], wide(m[:, n, :]), ALU.is_equal))
                        L(ts(eq[:], eq[:], -100.0, 100.0, ALU.mult, ALU.add))
                        L(tt(eq[:], eq[:], iota8, ALU.add))
                        L(nc.vector.tensor_reduce(m[:, 2 + n, :], eq[:], AX, ALU.min))
                        L(tt(s1[:], iota8, wide(m[:, 2 + n, :]), ALU.is_equal))
                        if n == 0:
                            L(nc.vector.scalar_tensor_tensor(lg[:], s1[:], -BIG, lg[:], ALU.mult, ALU.add))
                    tt(m[:, 4, :], m[:, 1, :], m[:, 0, :], ALU.subtract).then_inc(r_top, 1)
                    tt(w3[2][:], w3[0][:], w3[1][:], ALU.add).then_inc(r_top, 1)
                    for j in range(SPLITS):
                        moe_lo(dve, 0, j)
                    dve.wait_ge(r_exp, 1)
                    L(ts(m[:, 5, :], m[:, 4, :], 1.0, None, ALU.add))
                    L(nc.vector.reciprocal(m[:, 5, :], m[:, 5, :]))
                    L(tt(m[:, 6, :], m[:, 5, :], m[:, 4, :], ALU.mult))
                    dve_step.mark(tt(w3[0][:], w3[0][:], wide(m[:, 5, :]), ALU.mult))
                    L(tt(w3[1][:], w3[1][:], wide(m[:, 6, :]), ALU.mult))
                    L(tt(gate_w[:], w3[0][:], w3[1][:], ALU.add))
                    dve.wait_ge(ranked, 1)
                    L(ts(w3[4][:].rearrange("p t e -> p (t e)"), pb[1][:, 0:TT * E], 1.0, None, ALU.add))
                    L(tt(w3[4][:], w3[4][:], w3[2][:], ALU.mult))
                    for n in range(2):
                        dve_step.mark(ts(slot_no[:, n, :, :], w3[4][:], 1.0 + P * n, None, ALU.subtract))
                    L(ts(cn[:, 0, :], pb[1][:, 2 * E:3 * E], float(P), None, ALU.is_gt))
                    L(nc.vector.tensor_tensor_scan(cn[:, 1, :], const("ones", 0, E), cn[:, 0, :], 0.0, ALU.mult, ALU.add))
                    L(tt(cn[:, 2, :], cn[:, 1, :], cn[:, 0, :], ALU.subtract))
                    dve_step.mark(nc.vector.tensor_copy(info[0:1, 0:E], cn[0:1, 0, :]))
                    dve_step.mark(nc.vector.tensor_copy(info[0:1, E:2 * E], cn[0:1, 2, :]))
                    dve_step.mark(nc.vector.tensor_copy(info[0:1, 2 * E:3 * E], cn[0:1, 1, :]))

        with ExitStack() as stage:
            xg = sb("xg", [P, KT, P], stage=stage)
            Sel = sb("Sel", [P, TT, P], stage=stage)
            Gs = sb("Gs", [P, TT, P], stage=stage)
            GT = sb("GT", [P, T], stage=stage)
            sg = sb("msg", [P, 2, 512], stage=stage)
            hh = sb("mhh", [P, 2, 512], stage=stage)
            xp = [sb(z, [P, KT, P], F32R, stage) for z in ("xg_hi", "xg_lo")]
            hT = [sb(z, [P, 2, 512], F32R, stage) for z in ("hT_hi", "hT_lo")]
            oe = sb("moe", [P, D], stage=stage)
            first_use = {key: j for j, key in enumerate(order)}
            CH = CHUNKS

            def after(n, key):
                return n * EXPERT_BLOCKS + (moe_weight + first_use[key] + 1)

            def arrival(eng, n, key):
                eng.wait_ge(taken, n * EXPERT_BLOCKS + (moe_first + first_use[key] + 1))

            def load(sp, e, n, j):
                src = expert_block(e, j)
                slot = (moe_first + j) % RING
                sp.wait_ge(taken, n * EXPERT_BLOCKS + (moe_first + j - RING + 1))
                sp.dma_start(slot_view(slot, src), src).then_inc(arrived[slot], 16)

            def pe_pass(pe, e, n, second, span):
                pe.wait_ge(m_sel, n + 1)
                for b in range(2):
                    for k in range(4):
                        f = 4 * b + k
                        for t in range(TT):
                            ins = nc.tensor.matmul(pb[6 + b][:, k * P:(k + 1) * P], xn[:, t, f * P:(f + 1) * P], Sel[:, t, :],
                                                   start=(t == 0), stop=(t == 1))
                    ins.then_inc(m_gath, 1)
                for t in range(TT):
                    ins = nc.tensor.transpose(pb[5][:, t * P:(t + 1) * P], Gs[:, t, :], ident)
                ins.then_inc(m_gt, 1)
                pe.wait_ge(m_xlo, n + 1)

                def up(kind, c, bank):
                    for half in range(2):
                        arrival(pe, n, (kind, c, half))
                        slot = slot_of[kind, c, half]
                        for k in range(4):
                            for x, w in PARTS:
                                ins = nc.tensor.matmul(bank[:], xp[x][:, 4 * half + k, :], split[w][:, slot, k * 512:(k + 1) * 512],
                                                       start=(half == 0 and k == 0 and w + x == 0),
                                                       stop=(half == 1 and k == 3 and x == 1))
                        ins.then_inc(used, 1)

                for i in range(CH + 1):
                    if i < CH:
                        if i >= 2:
                            pe.wait_ge(m_sg, n * CH + (i - 1))
                        elif i == 0:
                            pe.wait_ge(m_y, n * 4 + 4)
                        up("gate", i, pb[i % 2])
                    if i:
                        c = i - 1
                        pe.wait_ge(m_h, n * CH + i)
                        if c == 1:
                            pe.wait_ge(m_gtc, n + 1)
                        for q in range(4):
                            ins = nc.tensor.transpose(pb[4 + c % 2][:, q * P:(q + 1) * P], hh[:, c % 2, q * P:(q + 1) * P], ident)
                        ins.then_inc(m_t, 1)
                    if i < CH:
                        if i >= 2:
                            pe.wait_ge(m_h, n * CH + (i - 1))
                        up("up", i, pb[2 + i % 2])
                    if i:
                        pe.wait_ge(m_hlo, n * CH + i)
                        for half in range(2):
                            arrival(pe, n, ("down", c, half))
                            slot = slot_of["down", c, half]
                            for f in range(2):
                                q = 2 * half + f
                                for x, w in PARTS:
                                    for b in range(2):
                                        ins = nc.tensor.matmul(pb[6 + b][:], hT[x][:, c % 2, q * P:(q + 1) * P],
                                                               split[w][:, slot, f * D + b * 512:f * D + (b + 1) * 512],
                                                               start=(c == 0 and q == 0 and w + x == 0),
                                                               stop=(c == CH - 1 and q == 3 and x == 1))
                            ins.then_inc(used, 1)
                pe.wait_ge(m_oe, n * 2 + 2)
                for t in range(TT):
                    for b in range(2):
                        nc.tensor.matmul(pb[2 * t + b][:], GT[:, t * P:(t + 1) * P], oe[:, b * 512:(b + 1) * 512],
                                         start=True, stop=True).then_inc(m_sc, 1)

            def up_to(part, eng, n, span):
                left = list(range(*span))

                def go(j):
                    while left and left[0] < j:
                        part(eng, n, left.pop(0))
                return go

            def act_pass(act, e, n, second, span):
                hi_to = up_to(moe_hi, act, n, span)
                hi_to(SPLITS)
                act.wait_ge(m_gath, n * 2 + 1)
                for k in range(4):
                    ins = nc.scalar.activation(xg[:, k, :], pb[6][:, k * P:(k + 1) * P], ACT.Identity,
                                               scale=gain_of(1, 1)(k), bias=shift(1, 1)(k))
                ins.then_inc(m_xg, 1)
                act.wait_ge(m_xg, n * 2 + 2)
                nc.scalar.copy(xp[0][:], xg[:]).then_inc(m_xhi, 1)
                act.wait_ge(m_gt, n + 1)
                nc.scalar.copy(GT[:], pb[5][:, 0:T]).then_inc(m_gtc, 1)
                for i in range(CH + 1):
                    if i < CH:
                        hi_to(first_use["gate", i, 1] + 3)
                        act.wait_ge(used, after(n, ("gate", i, 1)))
                        if i >= 2:
                            act.wait_ge(m_h, n * CH + (i - 1))
                        nc.scalar.activation(sg[:, i % 2, :], pb[i % 2][:], ACT.Silu).then_inc(m_sg, 1)
                    if i:
                        c = i - 1
                        act.wait_ge(m_t, n * CH + i)
                        if c >= 2:
                            act.wait_ge(used, after(n, ("down", c - 2, 1)))
                        nc.scalar.copy(hT[0][:, c % 2, :], pb[4 + c % 2][:]).then_inc(m_ht, 1)
                    if i < CH:
                        hi_to(first_use["up", i, 1] + 3)
                    if i:
                        hi_to(first_use["down", i - 1, 1] + (3 if i < CH else 2))
                act.wait_ge(used, after(n, ("down", CH - 1, 1)))
                nc.scalar.copy(oe[:, 0:512], pb[6][:]).then_inc(m_oe, 1)
                hi_to(span[1])

            def dve_pass(dve, e, n, second, span):
                lo_to = up_to(moe_lo, dve, n, span)
                for t in range(TT):
                    s = slot_no[:, int(second), t, bass.ds(e, 1)]
                    nc.vector.tensor_scalar(Sel[:, t, :], const("iota"), s, None, ALU.is_equal)
                    ins = nc.vector.tensor_scalar(Gs[:, t, :], const("iota"), s, gate_w[:, t, bass.ds(e, 1)],
                                                  ALU.is_equal, ALU.mult)
                ins.then_inc(m_sel, 1)
                lo_to(SPLITS)
                dve.wait_ge(m_gath, n * 2 + 2)
                for k in range(4):
                    ins = nc.vector.tensor_scalar(xg[:, 4 + k, :], pb[7][:, k * P:(k + 1) * P], gain_of(1, 1)(4 + k),
                                                  shift(1, 1)(4 + k), ALU.mult, ALU.add)
                ins.then_inc(m_xg, 1)
                dve.wait_ge(m_xhi, n + 1)
                nc.vector.tensor_tensor(xp[1][:], xg[:], xp[0][:].bitcast(F32), ALU.subtract).then_inc(m_xlo, 1)
                for i in range(CH + 1):
                    if i < CH:
                        lo_to(first_use["gate", i, 1] + 3)
                    if i:
                        c = i - 1
                        dve.wait_ge(m_ht, n * CH + i)
                        nc.vector.tensor_tensor(hT[1][:, c % 2, :], pb[4 + c % 2][:], hT[0][:, c % 2, :].bitcast(F32),
                                                ALU.subtract).then_inc(m_hlo, 1)
                    if i < CH:
                        lo_to(first_use["up", i, 1] + 3)
                        dve.wait_ge(m_sg, n * CH + (i + 1))
                        dve.wait_ge(used, after(n, ("up", i, 1)))
                        if i >= 2:
                            dve.wait_ge(m_t, n * CH + (i - 1))
                        nc.vector.tensor_tensor(hh[:, i % 2, :], sg[:, i % 2, :], pb[2 + i % 2][:], ALU.mult).then_inc(m_h, 1)
                    if i:
                        lo_to(first_use["down", i - 1, 1] + (3 if i < CH else 2))
                dve.wait_ge(used, after(n, ("down", CH - 1, 1)))
                nc.vector.tensor_copy(oe[:, 512:D], pb[7][:]).then_inc(m_oe, 1)
                dve.wait_ge(m_y, n * 4 + 4)
                lo_to(span[1])
                for t in range(TT):
                    for b in range(2):
                        dve.wait_ge(m_sc, n * 4 + (2 * t + b + 1))
                        y = yacc[:, t, b * 512:(b + 1) * 512]
                        nc.vector.tensor_tensor(y, y, pb[2 * t + b][:], ALU.add).then_inc(m_y, 1)

            def second_passes(eng, one_pass):
                total = eng.value_load(info[0:1, 3 * E - 1:3 * E], min_val=0, max_val=E)
                with eng.If(total > 0):
                    with eng.Fori(0, E) as e:
                        over = eng.value_load(info[0:1, bass.ds(e, 1)], min_val=0, max_val=1)
                        with eng.If(over > 0):
                            rank = eng.value_load(info[0:1, bass.ds(e + E, 1)], min_val=0, max_val=E - 1)
                            one_pass(eng, e, rank + E, True, (0, EXPERT_BLOCKS))

            def sp_second(sp, e, n, second, span):
                for j in range(EXPERT_BLOCKS):
                    load(sp, e, n, j)

            with nc.Block() as block:
                @block.sync
                def _(sp):
                    with sp.Fori(0, E - 1) as e:
                        for j in range(RING, EXPERT_BLOCKS):
                            load(sp, e, e, j)
                        for j in range(RING):
                            sp.wait_ge(taken, e * EXPERT_BLOCKS + (EXPERT_BLOCKS + moe_first + j - RING + 1))
                            src = expert_block(e + 1, j)
                            slot = (moe_first + j) % RING
                            sp.dma_start(slot_view(slot, src), src).then_inc(arrived[slot], 16)
                    for j in range(RING, EXPERT_BLOCKS):
                        load(sp, E - 1, E - 1, j)
                    second_passes(sp, sp_second)

                for declare, one_pass in ((block.tensor, pe_pass), (block.scalar, act_pass), (block.vector, dve_pass)):
                    @declare
                    def _(eng, one_pass=one_pass):
                        with eng.Fori(0, E - 1) as e:
                            one_pass(eng, e, e, False, (SPLITS, EXPERT_BLOCKS + SPLITS))
                        one_pass(eng, E - 1, E - 1, False, (SPLITS, EXPERT_BLOCKS))
                        second_passes(eng, one_pass)

            with nc.Block() as block:
                @block.vector
                def _(dve):
                    for t in range(TT):
                        dve_step.mark(nc.vector.tensor_tensor(yacc[:, t, :], yacc[:, t, :], gates[1][:, 1, :], ALU.mult))
                    dve_step.wait(dve)
                    nc.vector.tensor_tensor(resid[:], resid[:], yacc[:], ALU.add)
        if upto <= 9:
            return finish()
        norm_rows(9, a["final_g_2"].rearrange("(a d) -> a d", a=1))
        return finish()


_OUT = (1, T, D)


def kernel(upto=99, **inputs):
    from concourse import bacc
    from concourse.bass_utils import run_bass_kernel_spmd

    nc = bacc.Bacc("TRN2", target_bir_lowering=False, num_devices=1)
    arrays, args = {}, {}
    for name, x in {**inputs, "consts": CONSTS}.items():
        x = np.ascontiguousarray(x)
        arrays[f"in_{name}"] = x
        args[name] = nc.dram_tensor(f"in_{name}", x.shape, mybir.dt.from_np(x.dtype), kind="ExternalInput").ap()
    out = nc.dram_tensor("out", _OUT, F32, kind="ExternalOutput").ap()
    build(nc, args, out, upto)
    return run_bass_kernel_spmd(nc, [arrays], core_ids=[0]).results[0]["out"]
```

```python
from contextlib import ExitStack
import math

import numpy as np

import concourse.bass as bass
from concourse import mybir

F32 = mybir.dt.float32
F32R = mybir.dt.float32r
I32 = mybir.dt.int32
ALU = mybir.AluOpType
ACT = mybir.ActivationFunctionType
AX = mybir.AxisListType.X

P = 128
T = 256
TT = T // P
D = 1024
KT = D // P
F1 = 2816
F2 = 3072
EXPERTS = 8
RING = 4
SPLITS = 3
BLK = 2048
BIG = 1.0e30
RMS_EPS = 1e-6
LNX_EPS = 64e-5
HEADS = 16
DH = 64
CHUNKS = F2 // 512
EXPERT_BLOCKS = 6 * CHUNKS

CONST = {}


def const_table():
    cols, at = [], 0

    def add(name, a):
        nonlocal at
        CONST[name] = (at, a.shape[1])
        cols.append(a.astype(np.float32))
        at += a.shape[1]

    i = np.arange(P)
    row, col = i[:, None], i[None, :]
    add("ident", np.eye(P))
    add("ones", np.ones((P, P)))
    rot = np.zeros((P, P))
    for d in range(P):
        base, r = d // DH * DH, d % DH
        rot[base + (r + 32) % DH, d] = -1.0 if r < 32 else 1.0
    add("rot", rot)
    inv = (1.0 / (np.float32(10000.0) ** (np.arange(0, DH, 2, dtype=np.float32) / np.float32(DH)))).astype(np.float32)
    ang = (np.arange(T, dtype=np.float32)[:, None] * inv[None, :]).astype(np.float32)
    ang = np.tile(ang.T, (4, 1))
    add("cos", np.cos(ang))
    add("sin", np.sin(ang))
    inv2 = np.float32(10000.0) ** (-np.arange(0, DH, 2, dtype=np.float32) / np.float32(DH))
    add("inv", np.tile(inv2.astype(np.float32)[:, None], (4, 1)))
    tri = np.where(col <= row, 0.0, -BIG)
    add("causal", np.concatenate([tri, np.zeros((P, P)), tri], 1))
    add("before", (row < col) * 1.0)
    add("iota", np.tile(col, (P, 1)))
    strict, incl = (row < col) * 1.0, (row <= col) * 1.0
    add("pairmask", np.concatenate([strict, incl, strict, incl], 1))
    for lv in range(7):
        half = 1 << lv
        same = (row // (2 * half)) == (col // (2 * half))
        add(f"level{lv}", (same & (row % (2 * half) < half) & (col % (2 * half) >= half)) * 1.0)
    add("headones", (row // DH == col // DH) * 1.0)
    add("headsel", np.stack([i < DH, i >= DH], 1) * 1.0)
    add("rms_eps", np.full((P, 1), RMS_EPS))
    add("lnx_eps", np.full((P, 1), LNX_EPS))
    add("iota8", np.tile(np.arange(8)[None], (P, 2)))
    return np.ascontiguousarray(np.concatenate(cols, 1))


CONSTS = const_table()

VECTORS = [
    ("norm_mix", 16), ("norm_ffn", 16), ("rwkv_mu", 48), ("rwkv_w0", 8), ("rwkv_a0", 8), ("rwkv_k_k", 8),
    ("rwkv_k_a", 8), ("rwkv_r_k", 8), ("ffn_conv_w", 132), ("ffn_conv_b", 44), ("ln1_g_2", 16), ("ln2_g_2", 16),
    ("conv_w_2", 32), ("conv_b_2", 8), ("gate_a_b_2", 8), ("gate_x_b_2", 8), ("lru_lambda_2", 8),
    ("subln_g_2", 2), ("ada_b_2", 96), ("c_2", 8),
]
VROW = {}
_at = 0
for _name, _n in VECTORS:
    VROW[_name] = _at
    _at += _n
VTILES = -(-_at // P)
assert _at <= VTILES * P


class Steps:

    def __init__(self, sem):
        self.sem, self.n = sem, 0

    def mark(self, ins):
        ins.then_inc(self.sem, 1)
        self.n += 1

    def link(self, eng, ins):
        self.mark(ins)
        eng.wait_ge(self.sem, self.n)

    def wait(self, eng):
        eng.wait_ge(self.sem, self.n)


def build(nc, a, out):
    with ExitStack() as ctx:
        names = {}

        def sb(name, shape, dt=F32, stage=ctx):
            names[name] = names.get(name, 0) + 1
            if names[name] > 1:
                name = f"{name}_{names[name]}"
            return stage.enter_context(nc.sbuf_tensor(name, shape, dt))

        def sem(name):
            return ctx.enter_context(nc.semaphore(name))

        pb = [ctx.enter_context(nc.psum_tensor(f"bank{i}", [P, 512], F32)) for i in range(8)]
        ring = sb("ring", [P, RING, BLK])
        split = [sb(n, [P, SPLITS, BLK], F32R) for n in ("weights_hi", "weights_lo")]
        mods = sb("mods", [P, 2, 48])
        gain2 = sb("gain2", [P, 2, 2, KT])
        silu_c = sb("silu_c", [P, KT])
        cst = sb("cst", [P, CONSTS.shape[1]])
        vec = sb("vec", [P, VTILES * P])
        resid = sb("resid", [P, TT, D])
        xn = sb("xn", [P, TT, D])
        AT = sb("AT", [P, KT, T])
        stat = sb("stat", [P, 64])

        def const(name, lo=0, n=None):
            at, width = CONST[name]
            return cst[:, at + lo:at + lo + (width if n is None else n)]

        def v(name, i=0, n=1):
            return vec[:, VROW[name] + i:VROW[name] + i + n]

        arrived = [sem(f"arrived{i}") for i in range(RING)]
        hi_ready = sem("hi_ready")
        taken = sem("taken")
        used = sem("used")
        at_ready = [sem(f"at_ready{i}") for i in range(4)]
        at_hi = sem("at_hi")
        at_lo = sem("at_lo")
        setup_in = sem("setup_in")
        setup_rows = sem("setup_rows")
        rows_turned = sem("rows_turned")
        squares = sem("squares")
        gain_in = sem("gain_in")
        rooted = sem("rooted")
        normed = sem("normed")
        turned = sem("turned")
        dve_step = Steps(sem("dve_step"))
        act_step = Steps(sem("act_step"))
        pool_step = Steps(sem("pool_step"))
        ident = const("ident")

        def cols_block(w, c):
            return w.rearrange("(k p) n -> p k n", p=P)[:, :, 256 * c:256 * c + 256]

        def rows_block(w, c):
            return w[256 * c:256 * c + 256, :].rearrange("(f p) n -> p f n", p=P)

        stream, first = [], {}
        ffn_plan = {}

        def plan_one(src):
            stream.append(src)
            return len(stream) - 1

        def plan(name, blocks):
            first[name] = len(stream)
            for src in blocks:
                plan_one(src)

        def plan_ffn(name, gate, up, down, extra):
            pairs = gate.shape[1] // 256
            at = {"places": {}}
            extra = list(extra)
            chosen = [i * (2 * pairs - 1) // len(extra) for i in range(len(extra))]

            def place(q):
                if q in chosen:
                    at["places"][q] = extra.pop(0)

            for j in range(pairs + 1):
                if j < pairs:
                    at["gate", j] = plan_one(cols_block(gate, j))
                    at["up", j] = plan_one(cols_block(up, j))
                place(2 * j)
                if j:
                    at["down", j - 1] = plan_one(rows_block(down, j - 1))
                place(2 * j + 1)
            assert not extra
            ffn_plan[name] = at

        plan("qkv", [cols_block(a["attn_w_qkv"][0], c) for c in range(12)])
        plan("wo", [rows_block(a["attn_w_o"][0], c) for c in range(4)])
        early = [(0, i) for i in (*range(8), *range(12, 20))]
        late = [(0, i) for i in (*range(8, 12), *range(20, 24))] + [(1, i) for i in range(8)]
        plan_ffn(0, a["ffn_w_gate"][0], a["ffn_w_up"][0], a["ffn_w_down"][0], early)
        for m in (1, 0, 2):
            plan(f"rkv{m}", [cols_block(a["rwkv_w_rkv"][0, m], c) for c in range(4)])
        plan("rwkv_wo", [rows_block(a["rwkv_w_o"][0], c) for c in range(4)])
        plan_ffn(1, a["ffn_w_gate"][1], a["ffn_w_up"][1], a["ffn_w_down"][1], late)
        for l in range(2):
            plan(f"win{l}", [cols_block(a["w_in_2"][l], c) for c in range(10)])
            plan(f"wout{l}", [rows_block(a["w_out_2"][l], c) for c in range(4)])
            if l == 0:
                plan_ffn(2, a["ffn_w_gate_2"][0], a["ffn_w_up_2"][0], a["ffn_w_down_2"][0], [(1, i) for i in range(8, 24)])
        moe_first = len(stream)

        order = []
        for c in range(CHUNKS + 1):
            if c < CHUNKS:
                order += [("gate", c, 0), ("gate", c, 1), ("up", c, 0), ("up", c, 1)]
            if c:
                order += [("down", c - 1, 0), ("down", c - 1, 1)]
        assert len(order) == EXPERT_BLOCKS and EXPERT_BLOCKS % RING == 0 and EXPERT_BLOCKS % SPLITS == 0
        slot_of = {key: (moe_first + j) % SPLITS for j, key in enumerate(order)}
        moe_dram = {k: a[f"moe_w_{k}_2"][0] for k in ("gate", "up", "down")}

        def expert_block(e, j):
            kind, c, half = order[j]
            w = moe_dram[kind][bass.ds(e, 1)] if not type(e) is int else moe_dram[kind][e:e + 1]
            if kind == "down":
                at = 512 * c + 256 * half
                return w[:, at:at + 256, :].rearrange("e (f p) n -> p (e f) n", p=P)
            rows = moe_dram[kind].rearrange("e k n -> (e k) n")
            return rows[bass.ds(e * D + 512 * half, 512), 512 * c:512 * c + 512].rearrange("(k p) n -> p k n", p=P)

        def slot_view(slot, src):
            return ring[:, slot, :].rearrange("p (k n) -> p k n", n=src.shape[-1])

        def issue(eng, n):
            src = stream[n] if n < moe_first else expert_block(0, n - moe_first)
            if n >= RING:
                eng.wait_ge(taken, n - RING + 1)
            eng.dma_start(slot_view(n % RING, src), src).then_inc(arrived[n % RING], 16)

        issued, rounded, rested = [0], [0], [0]

        def feed(sp):
            while issued[0] < min(goal[0] + RING, moe_first + RING):
                issue(sp, issued[0])
                issued[0] += 1

        goal = [0]

        def ahead(m):
            goal[0] = m
            assert m <= moe_first

        def round_to(act, m):
            while rounded[0] < min(goal[0], m):
                n = rounded[0]
                rounded[0] += 1
                act.wait_ge(arrived[n % RING], 16 * (n // RING + 1))
                if n >= SPLITS:
                    act.wait_ge(used, n - SPLITS + 1)
                nc.scalar.copy(split[0][:, n % SPLITS, :], ring[:, n % RING, :]).then_inc(hi_ready, 1)

        def rest_to(dve, m):
            while rested[0] < min(goal[0], m):
                n = rested[0]
                rested[0] += 1
                dve.wait_ge(hi_ready, n + 1)
                nc.vector.tensor_tensor(split[1][:, n % SPLITS, :], ring[:, n % RING, :],
                                        split[0][:, n % SPLITS, :].bitcast(F32), ALU.subtract).then_inc(taken, 1)

        def landed(pe, m):
            pe.wait_ge(taken, m + 1)

        splitting, skipped = [0], [0]

        def new_split():
            splitting[0] += 1
            return splitting[0] - 1

        def at_round(act, k, c, src=None):
            act.wait_ge(at_ready[c], k + 1 - skipped[0])
            src = AT if src is None else src
            nc.scalar.copy(acts[0][:, 2 * c:2 * c + 2, :], src[:, 2 * c:2 * c + 2, :]).then_inc(at_hi, 1)

        def at_rest(dve, k, c, src=None):
            dve.wait_ge(at_hi, 4 * k + c + 1)
            src = AT if src is None else src
            w = slice(2 * c, 2 * c + 2)
            nc.vector.tensor_tensor(acts[1][:, w, :], src[:, w, :], acts[0][:, w, :].bitcast(F32), ALU.subtract).then_inc(at_lo, 1)

        acts = [None, None]

        def open_acts(stage):
            acts[:] = [sb(n, [P, KT, T], F32R, stage) for n in ("acts_hi", "acts_lo")]

        PARTS = ((0, 0), (0, 1), (1, 0))

        def norm_rows(k, row):
            with ExitStack() as stage:
                gain = sb(f"gain{k}", [P, D], stage=stage)
                with nc.Block() as block:
                    @block.sync
                    def _(sp):
                        sp.dma_start(gain[:], row.broadcast_to([P, D])).then_inc(gain_in, 16)

                    @block.scalar
                    def _(act):
                        for t in range(TT):
                            nc.scalar.activation(xn[:, t, :], resid[:, t, :], ACT.Square,
                                                 accum_out=stat[:, t:t + 1]).then_inc(squares, 1)
                        for t in range(TT):
                            act.wait_ge(squares, TT * k + t + 1)
                            nc.scalar.activation(stat[:, t:t + 1], stat[:, t:t + 1], ACT.Sqrt, scale=1.0 / D,
                                                 bias=const("rms_eps")).then_inc(rooted, 1)

                    @block.vector
                    def _(dve):
                        dve.wait_ge(gain_in, 16 * (1 if k < 5 else 2))
                        for t in range(TT):
                            dve.wait_ge(rooted, TT * k + t + 1)
                            dve_step.link(dve, nc.vector.reciprocal(stat[:, t:t + 1], stat[:, t:t + 1]))
                            nc.vector.scalar_tensor_tensor(resid[:, t, :], resid[:, t, :], stat[:, t:t + 1], gain[:],
                                                           ALU.mult, ALU.mult).then_inc(normed, 1)

        class Norm:

            def __init__(self, k, gain, bias=None, turns=None, then=None, look=SPLITS, parts=True, joined=False):
                self.k, self.gain, self.bias, self.then, self.look, self.parts = k, gain, bias, then, look, parts
                self.turns = k if turns is None else turns
                self.no = new_split() if parts else None
                self.joined = joined
                self.sums = sums[0]
                if joined:
                    sums[0] += TT

            def act(self, act):
                self.act_rows(act)
                self.act_columns(act)

            def act_rows(self, act):
                if self.joined:
                    nc.scalar.activation(stat[:, 8:9], const("rms_eps"), ACT.Sqrt)
                for t in range(TT):
                    if self.joined:
                        act.wait_ge(summed, self.sums + t + 1)
                    nc.scalar.activation(xn[:, t, :], resid[:, t, :], ACT.Square,
                                         accum_out=stat[:, t:t + 1]).then_inc(squares, 1)
                    act.wait_ge(squares, TT * self.k + t + 1)
                    nc.scalar.activation(stat[:, t:t + 1], stat[:, t:t + 1], ACT.Sqrt, scale=1.0 / D,
                                         bias=const("rms_eps")).then_inc(rooted, 1)
                if self.then is not None:
                    round_to(act, self.then + self.look)

            def act_columns(self, act):
                for b in range(2):
                    act.wait_ge(turned, 4 * self.turns + b + 1)
                    for i in range(2):
                        f = 2 * b + i
                        ins = nc.scalar.activation(AT[:, f, :], pb[b][:, i * T:(i + 1) * T], ACT.Identity,
                                                   scale=self.gain(f), bias=self.bias(f) if self.bias else 0.0)
                    if self.parts:
                        ins.then_inc(at_ready[b], 1)
                if self.parts:
                    for c in range(4):
                        at_round(act, self.no, c)

            def dve(self, dve):
                self.dve_rows(dve)
                self.dve_columns(dve)

            def dve_rows(self, dve):
                k = self.k
                for t in range(TT):
                    dve.wait_ge(rooted, TT * k + t + 1)
                    dve_step.link(dve, nc.vector.reciprocal(stat[:, t:t + 1], stat[:, t:t + 1]))
                    nc.vector.tensor_scalar(xn[:, t, :], resid[:, t, :], stat[:, t:t + 1], None,
                                            ALU.mult).then_inc(normed, 1)

            def dve_columns(self, dve):
                for b in range(2, 4):
                    dve.wait_ge(turned, 4 * self.turns + b + 1)
                    for i in range(2):
                        f = 2 * b + i
                        ins = nc.vector.tensor_scalar(AT[:, f, :], pb[b][:, i * T:(i + 1) * T], self.gain(f),
                                                      self.bias(f) if self.bias else 0.0, ALU.mult, ALU.add)
                    if self.parts:
                        ins.then_inc(at_ready[b], 1)
                if self.then is not None:
                    rest_to(dve, self.then + 1)
                if self.parts:
                    for c in range(4):
                        at_rest(dve, self.no, c)
                if self.then is not None:
                    rest_to(dve, self.then + self.look)

            def pe(self, pe):
                for t in range(TT):
                    pe.wait_ge(normed, TT * self.k + t + 1)
                    for b in range(4):
                        for i in range(2):
                            f = 2 * b + i
                            ins = nc.tensor.transpose(pb[b][:, i * T + t * P:i * T + (t + 1) * P],
                                                      xn[:, t, f * P:(f + 1) * P], ident)
                        if t == TT - 1:
                            ins.then_inc(turned, 1)

        sums = [0]
        summed = sem("summed")

        def norm_turn(*args, **kw):
            norm = Norm(*args, **kw)
            if norm.then is not None:
                ahead(norm.then + norm.look)
            with nc.Block() as block:
                @block.sync
                def _(sp):
                    feed(sp)

                @block.scalar
                def _(act):
                    norm.act(act)

                @block.vector
                def _(dve):
                    norm.dve(dve)

                @block.tensor
                def _(pe):
                    norm.pe(pe)
            return norm.no

        def to_features(pe, m, bank, no=None):
            landed(pe, m)
            for f in range(2):
                for k in range(KT):
                    if no is not None and f == 0 and k % 2 == 0:
                        pe.wait_ge(at_lo, 4 * no + k // 2 + 1)
                    for w, x in PARTS:
                        ins = nc.tensor.matmul(bank[:, f * T:(f + 1) * T],
                                               split[w][:, m % SPLITS, k * 256 + f * P:k * 256 + (f + 1) * P],
                                               acts[x][:, k, :], start=(k == 0 and w + x == 0), stop=(k == KT - 1 and w == 1))
            ins.then_inc(used, 1)

        def to_tokens(pe, m, bank):
            landed(pe, m)
            for t in range(TT):
                for k in range(KT):
                    for x, w in PARTS:
                        ins = nc.tensor.matmul(bank[:, t * 256:(t + 1) * 256], acts[x][:, k, t * P:(t + 1) * P],
                                               split[w][:, m % SPLITS, k * 256:(k + 1) * 256],
                                               start=(k == 0 and w + x == 0), stop=(k == KT - 1 and x == 1))
            ins.then_inc(used, 1)

        added = [0]
        halves = [0]
        half_done = sem("half_done")

        def project(pe, m, c, count, src, tile=None):
            landed(pe, m)
            tile = 2 * c if tile is None else tile
            last = c == count - 1
            steps = [(f, t) for t in range(TT) for f in range(2)] if last else [(f, t) for f in range(2) for t in range(TT)]
            for n, (f, t) in enumerate(steps):
                for x, w in PARTS:
                    for h in range(2):
                        ins = nc.tensor.matmul(pb[4 + 2 * t + h][:], src[x][:, tile + f, t * P:(t + 1) * P],
                                               split[w][:, m % SPLITS, f * D + h * 512:f * D + (h + 1) * 512],
                                               start=(c == 0 and f == 0 and w + x == 0),
                                               stop=(last and f == 1 and x == 1))
                if last and n == 1:
                    ins.then_inc(half_done, 1)
            ins.then_inc(used, 1)

        def add_projected(dve, end, scale=None, scratch=None, joined=False):
            halves[0] += 1
            if joined:
                added[0] += TT
            for t in range(TT):
                if t == 0:
                    dve.wait_ge(half_done, halves[0])
                else:
                    dve.wait_ge(used, end)
                for h in range(2):
                    y = pb[4 + 2 * t + h][:]
                    if scale is not None:
                        y = scratch[:, h, :]
                        dve_step.mark(nc.vector.tensor_tensor(y, pb[4 + 2 * t + h][:], scale[:, h * 512:(h + 1) * 512], ALU.mult))
                if scale is not None:
                    dve_step.wait(dve)
                for h in range(2):
                    r = resid[:, t, h * 512:(h + 1) * 512]
                    y = pb[4 + 2 * t + h][:] if scale is None else scratch[:, h, :]
                    ins = nc.vector.tensor_tensor(r, r, y, ALU.add)
                    if joined and h == 1:
                        ins.then_inc(summed, 1)
                    else:
                        dve_step.mark(ins)
                if scale is not None and joined:
                    dve.wait_ge(summed, added[0] - TT + t + 1)
                elif scale is not None:
                    dve_step.wait(dve)

        def finish():
            stored = sem("stored")
            with nc.Block() as block:
                @block.sync
                def _(sp):
                    sp.dma_start(out[0].rearrange("(t p) d -> p t d", p=P), resid[:]).then_inc(stored, 16)
                    sp.wait_ge(stored, 16)
        region = ExitStack()
        ctx.callback(region.close)
        open_acts(region)
        with ExitStack() as stage:
            rows = sb("rows", [P, VTILES, P], stage=stage)
            pieces = []
            for name, n in VECTORS:
                src = a[name]
                letters = " ".join("abcdef"[:len(src.shape)])
                flat = src.rearrange(f"{letters} -> ({letters})").rearrange("(r x) -> r x", x=P)
                done = 0
                while done < n:
                    at = VROW[name] + done
                    m = min(n - done, P - at % P)
                    pieces.append((rows[at % P:at % P + m, at // P, :], flat[done:done + m]))
                    done += m
            x_in = sem("x_in")
            norm = Norm(0, lambda f: v("norm_mix", f), then=0)
            no = norm.no
            ahead(SPLITS)
            with nc.Block() as block:
                @block.sync
                def _(sp):
                    sp.dma_start(resid[:], a["x"][0].rearrange("(t p) d -> p t d", p=P)).then_inc(x_in, 16)
                    sp.dma_start(cst[:], a["consts"]).then_inc(setup_in, 16)
                    sp.wait_ge(setup_rows, 1)
                    for dst, src in pieces[::2]:
                        sp.dma_start(dst, src).then_inc(setup_in, 16)
                    feed(sp)

                @block.gpsimd
                def _(pool):
                    pool.memset(rows[:], 0.0).then_inc(setup_rows, 1)

                @block.scalar
                def _(act):
                    act.wait_ge(setup_rows, 1)
                    for dst, src in pieces[1::2]:
                        act.dma_start(dst, src).then_inc(setup_in, 16)
                    act.wait_ge(x_in, 16)
                    act.wait_ge(setup_in, 16 * (1 + len(pieces)))
                    norm.act_rows(act)
                    act.wait_ge(rows_turned, 2)
                    norm.act_columns(act)
                    nc.scalar.activation(silu_c[:], v("c_2", 0, KT), ACT.Silu)

                @block.tensor
                def _(pe):
                    pe.wait_ge(setup_in, 16 * (1 + len(pieces)))
                    for i in range(VTILES):
                        ins = nc.tensor.transpose(pb[7][:, i * P:(i + 1) * P], rows[:, i, :], ident)
                    ins.then_inc(rows_turned, 1)
                    norm.pe(pe)

                @block.vector
                def _(dve):
                    dve.wait_ge(rows_turned, 1)
                    nc.vector.tensor_copy(vec[:], pb[7][:]).then_inc(rows_turned, 1)
                    norm.dve_rows(dve)
                    rest_to(dve, SPLITS)
                    dve.wait_ge(rows_turned, 2)
                    norm.dve_columns(dve)

        heads_stage = ExitStack()
        QK = sb("QK", [P, 16, T], stage=heads_stage)
        V = sb("V", [P, TT, D], stage=heads_stage)

        raw_ready = sem("raw_ready")
        rot_done = sem("rot_done")
        qk_done = sem("qk_done")
        v_done = sem("v_done")
        with ExitStack() as stage:
            raw = sb("raw", [P, 2, 2 * T], stage=stage)
            rc = sb("rc", [P, 2, 2 * T], stage=stage)
            rs = sb("rs", [P, 2, 2 * T], stage=stage)
            n0 = first["qkv"]
            ahead(n0 + 12)
            with nc.Block() as block:
                @block.sync
                def _(sp):
                    feed(sp)

                @block.tensor
                def _(pe):
                    for i in range(12):
                        bank = pb[i % 3]
                        if i >= 3:
                            if i - 3 < 8:
                                pe.wait_ge(raw_ready, i - 2)
                            else:
                                pe.wait_ge(v_done, i - 3 - 8 + 1)
                        if i < 8:
                            to_features(pe, n0 + i, bank, None if i else no)
                        else:
                            to_tokens(pe, n0 + i, bank)
                        if 1 <= i <= 8:
                            b = i - 1
                            pe.wait_ge(raw_ready, b + 1)
                            if b >= 2:
                                pe.wait_ge(qk_done, b - 1)
                            nc.tensor.matmul(pb[4 + b % 2][:], const("rot"), raw[:, b % 2, :], start=True,
                                             stop=True).then_inc(rot_done, 1)

                @block.scalar
                def _(act):
                    for b in range(8):
                        round_to(act, n0 + b + 3)
                        act.wait_ge(used, n0 + b + 1)
                        if b >= 2:
                            act.wait_ge(qk_done, b - 1)
                        nc.scalar.copy(raw[:, b % 2, :], pb[b % 3][:]).then_inc(raw_ready, 1)
                    for b in range(4):
                        round_to(act, n0 + 8 + b + 3)
                        act.wait_ge(used, n0 + 8 + b + 1)
                        nc.scalar.copy(V[:, :, b * 256:(b + 1) * 256],
                                       pb[(8 + b) % 3][:].rearrange("p (t n) -> p t n", t=2)).then_inc(v_done, 1)

                @block.vector
                def _(dve):
                    cos = const("cos").rearrange("p (a t) -> p a t", a=1).broadcast_to([P, 2, T])
                    sin = const("sin").rearrange("p (a t) -> p a t", a=1).broadcast_to([P, 2, T])
                    for b in range(8):
                        three = lambda z: z.rearrange("p (f t) -> p f t", f=2)
                        rest_to(dve, n0 + b + 3)
                        dve.wait_ge(raw_ready, b + 1)
                        dve_step.mark(nc.vector.tensor_tensor(three(rc[:, b % 2, :]), three(raw[:, b % 2, :]), cos, ALU.mult))
                        dve.wait_ge(rot_done, b + 1)
                        dve_step.link(dve, nc.vector.tensor_tensor(three(rs[:, b % 2, :]), three(pb[4 + b % 2][:]), sin, ALU.mult))
                        nc.vector.tensor_tensor(QK[:, 2 * b:2 * b + 2, :].rearrange("p f t -> p (f t)"), rc[:, b % 2, :],
                                                rs[:, b % 2, :], ALU.add).then_inc(qk_done, 1)
                    rest_to(dve, n0 + 12)

        scored = sem("scored")
        masked = sem("masked")
        maxed = sem("maxed")
        exped = sem("exped")
        weighted = sem("weighted")
        p_turned = sem("p_turned")
        p_copied = sem("p_copied")
        head_out = sem("head_out")
        out_copied = sem("out_copied")
        with ExitStack() as stage:
            S = sb("S", [P, 2, 384], stage=stage)
            Pr = sb("Pr", [P, 2, 384], stage=stage)
            PT = sb("PT", [P, 2, 384], stage=stage)
            st = sb("st", [P, HEADS, 6], stage=stage)
            sc = DH ** -0.5
            n0 = first["wo"]
            ahead(n0 + 3)
            no = new_split()
            skipped[0] += 1
            with nc.Block() as block:
                @block.sync
                def _(sp):
                    feed(sp)

                @block.tensor
                def _(pe):
                    def score(h):
                        if h >= 2:
                            pe.wait_ge(masked, h - 1)
                        lo, f = DH * (h % 2), h // 2
                        q, kk = QK[lo:lo + DH, f, :], QK[lo:lo + DH, 8 + f, :]
                        bank = pb[h % 2]
                        nc.tensor.matmul(bank[:, 0:P], q[:, 0:P], kk[:, 0:P], start=True, stop=True)
                        nc.tensor.matmul(bank[:, P:384], q[:, P:T], kk[:, :], start=True, stop=True).then_inc(scored, 1)

                    def turn(h):
                        pe.wait_ge(weighted, h + 1)
                        if h >= 2:
                            pe.wait_ge(p_copied, h - 1)
                        bank = pb[2 + h % 2]
                        for i in range(3):
                            at = [0, P, 2 * P][i]
                            ins = nc.tensor.transpose(bank[:, at:at + P], Pr[:, h % 2, [0, P, 2 * P][i]:[0, P, 2 * P][i] + P], ident)
                        ins.then_inc(p_turned, 1)

                    def mix(h):
                        pe.wait_ge(p_copied, h + 1)
                        if h >= 4 and h % 2 == 0:
                            pe.wait_ge(out_copied, h // 2 - 1)
                        lo, pt = DH * (h % 2), PT[:, h % 2, :]
                        o = pb[4 + h // 2 % 2][lo:lo + DH, 0:T]
                        nc.tensor.matmul(o, V[:, 0, h * DH:(h + 1) * DH], pt[:, 0:T], start=True, stop=False)
                        nc.tensor.matmul(o[:, P:T], V[:, 1, h * DH:(h + 1) * DH], pt[:, T:T + P], start=False,
                                         stop=True).then_inc(head_out, 1)

                    for i in range(HEADS + 2):
                        if i < HEADS:
                            score(i)
                        if 1 <= i <= HEADS:
                            turn(i - 1)
                        if i >= 2:
                            mix(i - 2)

                @block.vector
                def _(dve):
                    def first_half(h):
                        dve.wait_ge(scored, h + 1)
                        if h >= 2:
                            dve.wait_ge(exped, 2 * (h - 1))
                        nc.vector.tensor_tensor(S[:, h % 2, :], pb[h % 2][:, 0:384], const("causal"), ALU.add).then_inc(masked, 1)
                        dve.wait_ge(masked, h + 1)
                        dve_step.mark(nc.vector.reduce_max(st[:, h, 0:1], S[:, h % 2, 0:P], AX))
                        dve_step.link(dve, nc.vector.reduce_max(st[:, h, 1:2], S[:, h % 2, P:384], AX))
                        nc.vector.tensor_scalar(st[:, h, 0:2], st[:, h, 0:2], -sc, None, ALU.mult).then_inc(maxed, 1)

                    def second_half(h):
                        dve.wait_ge(exped, 2 * (h + 1))
                        dve_step.link(dve, nc.vector.reciprocal(st[:, h, 4:6], st[:, h, 2:4]))
                        if h >= 2:
                            dve.wait_ge(p_turned, h - 1)
                        dve_step.mark(nc.vector.tensor_scalar(Pr[:, h % 2, 0:P], S[:, h % 2, 0:P], st[:, h, 4:5], None, ALU.mult))
                        nc.vector.tensor_scalar(Pr[:, h % 2, P:384], S[:, h % 2, P:384], st[:, h, 5:6], None,
                                                ALU.mult).then_inc(weighted, 1)

                    for h in range(HEADS + 1):
                        if h in (2, 4, 6):
                            rest_to(dve, n0 + h // 2)
                        if h >= 1:
                            second_half(h - 1)
                        if h < HEADS:
                            if h >= 2:
                                dve.wait_ge(weighted, h - 1)
                            first_half(h)

                @block.scalar
                def _(act):
                    def copies(h):
                        act.wait_ge(p_turned, h + 1)
                        if h >= 2:
                            act.wait_ge(head_out, h - 1)
                        nc.scalar.copy(PT[:, h % 2, :], pb[2 + h % 2][:, 0:384]).then_inc(p_copied, 1)

                    def outs(f):
                        act.wait_ge(head_out, 2 * f + 2)
                        nc.scalar.copy(AT[:, f, :], pb[4 + f % 2][:, 0:T]).then_inc(out_copied, 1)
                        if f % 2:
                            act.wait_ge(out_copied, f + 1)
                            nc.scalar.copy(acts[0][:, f - 1:f + 1, :], AT[:, f - 1:f + 1, :]).then_inc(at_hi, 1)

                    for i in range(HEADS + 3):
                        if i in (0, 2, 4):
                            round_to(act, n0 + i // 2 + 1)
                        if i < HEADS:
                            act.wait_ge(maxed, i + 1)
                            for t, (lo, hi) in enumerate(((0, P), (P, 384))):
                                nc.scalar.activation(S[:, i % 2, lo:hi], S[:, i % 2, lo:hi], ACT.Exp, scale=sc,
                                                     bias=st[:, i, t:t + 1], accum_out=st[:, i, 2 + t:3 + t]).then_inc(exped, 1)
                        if 1 <= i <= HEADS:
                            copies(i - 1)
                        if i >= 3 and i % 2 == 1:
                            outs((i - 3) // 2)
            after = ffn_plan[0]["gate", 0]
            ahead(after + 2)
            norm = Norm(1, lambda f: v("norm_ffn", f), then=after, look=2, joined=True)
            with nc.Block() as block:
                @block.sync
                def _(sp):
                    feed(sp)

                @block.scalar
                def _(act):
                    round_to(act, after + 2)
                    norm.act(act)

                @block.tensor
                def _(pe):
                    for c in range(4):
                        pe.wait_ge(at_lo, 4 * no + c + 1)
                        project(pe, n0 + c, c, 4, acts)
                    norm.pe(pe)

                @block.vector
                def _(dve):
                    for c in range(4):
                        at_rest(dve, no, c)
                    rest_to(dve, after + 2)
                    add_projected(dve, n0 + 4, joined=True)
                    norm.dve(dve)
        heads_stage.close()

        ffn_no = norm.no
        gate_copied = sem("gate_copied")
        gate_pads = sem("gate_pads")
        convolved = sem("convolved")
        silued = sem("silued")
        hidden = sem("hidden")
        hid_hi = sem("hid_hi")
        hid_lo = sem("hid_lo")
        ada_done = sem("ada_done")
        ada_read = sem("ada_read")
        ada_in = [sem(f"ada_in{i}") for i in range(2)]
        ada_scaled = sem("ada_scaled")
        ada_summed = sem("ada_summed")
        gates = [None, None]
        gates_in = sem("gates_in")
        ada_before, pairs_done_before, conv_before = [0], [0], [0]

        def make_gates(l):
            gates[l] = sb(f"gates{l}", [P, 2, D])
            return gates[l]

        def ffn(name, no, then, conv=None, scale=None, gate_rows=None, finished=None, norm=None):
            at = ffn_plan[name]
            places = at["places"]
            pairs = sum(1 for k in at if k[0] == "gate")
            hb, cb, ab = pairs_done_before[0], conv_before[0], ada_before[0]
            number = {q: ab + i for i, q in enumerate(sorted(places))}
            last = at["down", pairs - 1] + 1
            ahead(then + (2 if norm is None else norm.look))
            with ExitStack() as stage:
                hf = sb("hf", [P, 2, 2 * T], stage=stage)
                hp = [sb(n, [P, 4, T], F32R, stage=stage) for n in ("hid_hi_part", "hid_lo_part")]
                sg = sb("sg", [P, 2, 2 * T], stage=stage)
                asum = sb("asum", [P, 4, 256], stage=stage)
                ada = sb("ada", [P, 2, BLK], stage=stage)
                if conv is not None:
                    gp = sb("gp", [P, 2, 2, T + 2], stage=stage)
                    cv = sb("cv", [P, 2, 2 * T], stage=stage)
                zz = sb("zz", [P, 2, 512], stage=stage) if scale is not None else None
                with nc.Block() as block:
                    @block.sync
                    def _(sp):
                        if gate_rows is not None:
                            for i in range(2):
                                sp.dma_start(gates[gate_rows][:, i, :],
                                             a["ada_b_2"][gate_rows:gate_rows + 1, (3 * i + 2) * D:(3 * i + 3) * D]
                                             .broadcast_to([P, D])).then_inc(gates_in, 16)
                        feed(sp)

                    @block.gpsimd
                    def _(pool):
                        blocks = [places[q] for q in sorted(places)]

                        def load(n):
                            l, i = blocks[n - ab]
                            if n >= 2:
                                pool.wait_ge(ada_summed, n - 1)
                            src = cols_block(a["ada_w_2"][l], i)
                            pool.dma_start(ada[:, n % 2, :].rearrange("p (k n) -> p k n", k=KT), src).then_inc(ada_in[n % 2], 16)

                        for n in range(ab, ab + 2):
                            load(n)
                        for n in range(ab, ab + len(blocks)):
                            pool.wait_ge(ada_scaled, n + 1)
                            if n >= 4:
                                pool.wait_ge(ada_done, n - 3)
                            x, z = ada[:, n % 2, :], asum[:, n % 4, :]
                            for half in (1024, 512):
                                pool_step.link(pool, pool.tensor_tensor(x[:, 0:half], x[:, 0:half], x[:, half:2 * half], ALU.add))
                            pool.tensor_tensor(z, x[:, 0:256], x[:, 256:512], ALU.add).then_inc(ada_summed, 1)
                            if n + 2 < ab + len(blocks):
                                load(n + 2)

                    @block.tensor
                    def _(pe):
                        def modulation(q):
                            if q - 3 not in places:
                                return
                            (l, i), n = places[q - 3], number[q - 3]
                            pe.wait_ge(ada_summed, n + 1)
                            if n:
                                pe.wait_ge(ada_read, n)
                            if i // 4 in (2, 5):
                                ins = nc.tensor.matmul(pb[3][:, 0:256], const("ones"), asum[:, n % 4, :],
                                                       start=True, stop=True)
                            else:
                                for f in range(2):
                                    ins = nc.tensor.matmul(pb[3][:, f:f + 1], asum[:, n % 4, f * P:(f + 1) * P],
                                                           const("ones", 0, 1), start=True, stop=True)
                            ins.then_inc(ada_done, 1)

                        for j in range(pairs + 1):
                            if j < pairs:
                                if j >= 2:
                                    pe.wait_ge(gate_copied, hb + j - 1)
                                to_features(pe, at["gate", j], pb[j % 2], None if j else no)
                                if j:
                                    pe.wait_ge(hidden, hb + j)
                                to_features(pe, at["up", j], pb[2])
                            modulation(2 * j)
                            if j:
                                pe.wait_ge(hid_lo, hb + j)
                                project(pe, at["down", j - 1], j - 1, pairs, hp, 2 * ((j - 1) % 2))
                            modulation(2 * j + 1)
                        if norm is not None:
                            pe.wait_ge(ada_read, ab + len(places))
                            norm.pe(pe)

                    @block.scalar
                    def _(act):
                        for j in range(pairs + 1):
                            if j:
                                act.wait_ge(hidden, hb + j)
                                if j >= 3:
                                    act.wait_ge(used, at["down", j - 3] + 1)
                                h = 2 * ((j - 1) % 2)
                                nc.scalar.copy(hp[0][:, h:h + 2, :].rearrange("p f t -> p (f t)"), hf[:, (j - 1) % 2, :]).then_inc(hid_hi, 1)
                            if j < pairs:
                                round_to(act, at["gate", j] + 3)
                                round_to(act, at["up", j] + 3)
                                act.wait_ge(used, at["gate", j] + 1)
                                if conv is None:
                                    if j >= 2:
                                        act.wait_ge(hidden, hb + j - 1)
                                    nc.scalar.activation(sg[:, j % 2, :], pb[j % 2][:], ACT.Silu).then_inc(gate_copied, 1)
                                else:
                                    if j >= 2:
                                        act.wait_ge(convolved, cb + j - 1)
                                    else:
                                        act.wait_ge(gate_pads, 2 * conv + 2)
                                    nc.scalar.copy(gp[:, j % 2, :, 2:], pb[j % 2][:].rearrange("p (f t) -> p f t", f=2)).then_inc(gate_copied, 1)
                                    act.wait_ge(convolved, cb + j + 1)
                                    if j >= 2:
                                        act.wait_ge(hidden, hb + j - 1)
                                    nc.scalar.activation(sg[:, j % 2, :], cv[:, j % 2, :], ACT.Silu).then_inc(silued, 1)
                            if j:
                                round_to(act, at["down", j - 1] + 3)
                        if norm is not None:
                            norm.act(act)

                    @block.vector
                    def _(dve):
                        if conv is not None:
                            for b in range(2):
                                nc.vector.memset(gp[:, b, :, 0:2], 0.0).then_inc(gate_pads, 1)
                        def convolve(j):
                            dve.wait_ge(gate_copied, hb + j + 1)
                            if j >= 2:
                                dve.wait_ge(silued, cb + j - 1)
                            for i in range(3):
                                for f in range(2):
                                    ft = 2 * j + f
                                    w = v("ffn_conv_w", (conv * 3 + 2 - i) * (F1 // P) + ft)
                                    src, dst = gp[:, j % 2, f, 2 - i:2 - i + T], cv[:, j % 2, f * T:(f + 1) * T]
                                    if i == 0:
                                        ins = nc.vector.tensor_scalar(dst, src, w, v("ffn_conv_b", conv * (F1 // P) + ft), ALU.mult, ALU.add)
                                    else:
                                        ins = nc.vector.scalar_tensor_tensor(dst, src, w, dst, ALU.mult, ALU.add)
                                    if i == 2 and f == 1:
                                        ins.then_inc(convolved, 1)
                                    else:
                                        dve_step.mark(ins)
                                if i < 2:
                                    dve_step.wait(dve)

                        def multiply(j):
                            dve.wait_ge(gate_copied if conv is None else silued, (hb if conv is None else cb) + j + 1)
                            dve.wait_ge(used, at["up", j] + 1)
                            if j >= 2:
                                dve.wait_ge(hid_lo, hb + j - 1)
                            nc.vector.tensor_tensor(hf[:, j % 2, :], sg[:, j % 2, :], pb[2][:], ALU.mult).then_inc(hidden, 1)

                        def rest(j):
                            dve.wait_ge(hid_hi, hb + j + 1)
                            h = 2 * (j % 2)
                            hi, lo = (z[:, h:h + 2, :].rearrange("p f t -> p (f t)") for z in hp)
                            nc.vector.tensor_tensor(lo, hf[:, j % 2, :], hi.bitcast(F32), ALU.subtract).then_inc(hid_lo, 1)

                        def scale_rows(q):
                            if q - 1 not in places:
                                return
                            n = number[q - 1]
                            dve.wait_ge(ada_in[n % 2], 16 * (n // 2 + 1))
                            for r in range(KT):
                                y = ada[:, n % 2, r * 256:(r + 1) * 256]
                                ins = nc.vector.tensor_scalar(y, y, silu_c[:, r:r + 1], None, ALU.mult)
                            ins.then_inc(ada_scaled, 1)

                        def modulation_read(q):
                            if q - 4 not in places:
                                return
                            (l, i), n = places[q - 4], number[q - 4]
                            dve.wait_ge(ada_done, n + 1)
                            seg, c = i // 4, i % 4
                            if seg in (2, 5):
                                dve.wait_ge(gates_in, 32 * (l + 1))
                                g = gates[l][:, seg // 3, c * 256:(c + 1) * 256]
                                ins = nc.vector.tensor_tensor(g, g, pb[3][:, 0:256], ALU.add)
                            else:
                                k = seg * KT + 2 * c
                                ins = nc.vector.tensor_tensor(mods[:, l, k:k + 2], pb[3][:, 0:2],
                                                              v("ada_b_2", l * 48 + k, 2), ALU.add)
                            ins.then_inc(ada_read, 1)

                        for j in range(pairs + 1):
                            if j:
                                multiply(j - 1)
                            if j < pairs:
                                rest_to(dve, at["gate", j] + 3)
                            if j:
                                rest(j - 1)
                            modulation_read(2 * j)
                            if j < pairs and conv is not None:
                                convolve(j)
                            if j < pairs:
                                rest_to(dve, at["up", j] + 3)
                            if j:
                                rest_to(dve, at["down", j - 1] + 3)
                            modulation_read(2 * j + 1)
                            scale_rows(2 * j)
                            scale_rows(2 * j + 1)
                        if finished is not None:
                            dve.wait_ge(ada_read, ab + len(places))
                            for i, gname in enumerate(("ln1_g_2", "ln2_g_2")):
                                seg = 3 * i + 1
                                nc.vector.scalar_tensor_tensor(gain2[:, finished, i, :], mods[:, finished, seg * KT:(seg + 1) * KT],
                                                               1.0, v(gname, finished * KT, KT), ALU.add, ALU.mult)
                        add_projected(dve, last, scale, zz, joined=norm is not None)
                        if norm is not None:
                            norm.dve(dve)
            ada_before[0] += len(places)
            pairs_done_before[0] += pairs
            if conv is not None:
                conv_before[0] += pairs

        norm = Norm(2, lambda f: v("norm_mix", KT + f), then=first["rkv1"], look=SPLITS, parts=False, joined=True)
        ffn(0, ffn_no, first["rkv1"], norm=norm, conv=0)
        region.close()
        nk = first["rkv1"]
        C = P
        rwkv = ExitStack()
        KR = sb("KR", [P, 16, 2, C], stage=rwkv)
        bet = sb("bet", [P, 16, C], stage=rwkv)
        G = sb("G", [P, KT, T], stage=rwkv)
        bonus = sb("bonus", [P, TT, HEADS], stage=rwkv)
        S0 = sb("S0", [P, KT, DH], stage=rwkv)
        fac = sb("fac", [P, KT], stage=rwkv)
        fc = lambda z: z.rearrange("p f (c t) -> p (f c) t", c=2)

        mix_ready = sem("mix_ready")
        lora_in = sem("lora_in")
        lora_first = sem("lora_first")
        lora_act = sem("lora_act")
        lora_out = sem("lora_out")
        lora_read = sem("lora_read")
        rkv_read = sem("rkv_read")
        with ExitStack() as stage:
            xx = xn[:].rearrange("p a b -> p (a b)").rearrange("p (k t) -> p k t", k=KT)
            mix = sb("mix", [P, 2, KT, T], stage=stage)
            w1, a1, g1 = (sb(n, [P, KT, m], stage=stage) for n, m in (("w1", 64), ("a1", 64), ("g1", 128)))
            second = sb("second", [P, 3, D], stage=stage)
            la = sb("la", [P, 3, T], stage=stage)
            with nc.Block() as block:
                @block.sync
                def _(sp):
                    for dst, name in ((w1, "rwkv_w1"), (a1, "rwkv_a1"), (g1, "rwkv_g1")):
                        sp.dma_start(dst[:], a[name][0].rearrange("(k p) n -> p k n", p=P)).then_inc(lora_in, 16)
                    for i, name in enumerate(("rwkv_w2", "rwkv_a2", "rwkv_g2")):
                        m = 64 if i < 2 else P
                        sp.dma_start(second[0:m, i, :], a[name][0]).then_inc(lora_in, 16)

                @block.vector
                def _(dve):
                    dve_step.mark(nc.vector.tensor_tensor(xx[:, :, 1:T], AT[:, :, 0:T - 1], AT[:, :, 1:T], ALU.subtract))
                    dve_step.link(dve, nc.vector.tensor_scalar(xx[:, :, 0:1], AT[:, :, 0:1], -1.0, None, ALU.mult))
                    for i, m in enumerate((1, 4, 5)):
                        if i == 2:
                            dve.wait_ge(lora_first, 1)
                        for k in range(KT):
                            ins = nc.vector.scalar_tensor_tensor(mix[:, i % 2, k, :], xx[:, k, :], v("rwkv_mu", m * KT + k),
                                                                 AT[:, k, :], ALU.mult, ALU.add)
                        ins.then_inc(mix_ready, 1)

                @block.tensor
                def _(pe):
                    pe.wait_ge(lora_in, 96)
                    for i, (w, m) in enumerate(((w1, 64), (a1, 64), (g1, P))):
                        pe.wait_ge(mix_ready, i + 1)
                        for k in range(KT):
                            ins = nc.tensor.matmul(pb[i][0:m, 0:T], w[:, k, :], mix[:, i % 2, k, :],
                                                   start=(k == 0), stop=(k == KT - 1))
                        ins.then_inc(lora_first, 1)
                    for q in range(12):
                        i, m = q // 4, (64, 64, P)[q // 4]
                        if q % 4 == 0:
                            pe.wait_ge(lora_act, i + 1)
                        if q >= 4:
                            pe.wait_ge(lora_read, q - 3)
                        for f in range(2):
                            ft = 2 * (q % 4) + f
                            ins = nc.tensor.matmul(pb[3 + q % 4][:, f * T:(f + 1) * T], second[0:m, i, ft * P:(ft + 1) * P],
                                                   la[0:m, i, :], start=True, stop=True)
                        ins.then_inc(lora_out, 1)

                @block.scalar
                def _(act):
                    for i, func in enumerate((ACT.Tanh, ACT.Copy, ACT.Sigmoid)):
                        m = (64, 64, P)[i]
                        act.wait_ge(lora_first, i + 1)
                        nc.scalar.activation(la[0:m, i, :], pb[i][0:m, 0:T], func).then_inc(lora_act, 1)
                    for q in range(12):
                        act.wait_ge(lora_out, q + 1)
                        bank = pb[3 + q % 4]
                        if q >= 8:
                            nc.scalar.copy(G[:, 2 * (q % 4):2 * (q % 4) + 2, :].rearrange("p f t -> p (f t)"),
                                           bank[:]).then_inc(lora_read, 1)
                            continue
                        for f in range(2):
                            ft = 2 * (q % 4) + f
                            dst = KR[:, 2 * ft:2 * ft + 2, 0, :] if q < 4 else bet[:, 2 * ft:2 * ft + 2, :]
                            ins = nc.scalar.activation(dst, bank[:, f * T:(f + 1) * T].rearrange("p (c t) -> p c t", c=2),
                                                       ACT.Sigmoid, bias=v("rwkv_w0" if q < 4 else "rwkv_a0", ft))
                        ins.then_inc(lora_read, 1)

        CD = -math.exp(-0.5)
        keyed = sem("keyed")
        key_sq = sem("key_sq")
        key_sum = sem("key_sum")
        key_max = sem("key_max")
        key_root = sem("key_root")
        decays = sem("decays")
        exps = sem("exps")
        bonus_in = sem("bonus_in")
        bonus_done = sem("bonus_done")
        beta_done = sem("beta_done")
        kh = sb("kh", [P, 16, C], stage=rwkv)
        V = sb("Vr", [P, TT, D], stage=rwkv)
        with ExitStack() as stage:
            mix = sb("mix", [P, 2, KT, T], stage=stage)
            open_acts(stage)
            numbers = [new_split() for _ in range(3)]
            n0 = first["rwkv_wo"]
            ahead(n0 + 3)
            tall = lambda z: z.rearrange("p k t -> p (k t)").rearrange("p (f t) -> p f t", f=16)
            rn, E1, Lp = tall(AT[:]), tall(mix[:, 0]), tall(mix[:, 1])
            Ls = xn[:].rearrange("p a b -> p (a b)").rearrange("p (f t) -> p f t", f=16)
            rksel = sb("rksel", [P, KT, 2], stage=stage)
            flat = lambda z: z.rearrange("p a b -> p (a b)")
            kap, rho = KR[:, :, 0, :], KR[:, :, 1, :]
            with nc.Block() as block:
                @block.sync
                def _(sp):
                    feed(sp)

                @block.tensor
                def _(pe):
                    for q in range(12):
                        if q >= 4:
                            pe.wait_ge(rkv_read, q - 3)
                        if q >= 8:
                            pe.wait_ge(at_lo, 4 * numbers[2] + 4)
                            to_tokens(pe, nk + q, pb[q % 4])
                        else:
                            to_features(pe, nk + q, pb[q % 4], None if q % 4 else numbers[q // 4])
                        if q == 5:
                            pe.wait_ge(key_sq, 1)
                            for b in range(4):
                                nc.tensor.matmul(pb[4 + b][:], const("headones"), flat(rn)[:, b * 512:(b + 1) * 512],
                                                 start=True, stop=True).then_inc(key_sum, 1)
                        if q == 11:
                            pe.wait_ge(bonus_in, 1)
                            pe.wait_ge(beta_done, 1)
                            for f in range(KT):
                                for t in range(TT):
                                    ins = nc.tensor.matmul(pb[4][:, t * HEADS + 2 * f:t * HEADS + 2 * f + 2], rn[:, 2 * f + t, :],
                                                           rksel[:, f, :], start=True, stop=True)
                            ins.then_inc(bonus_done, 1)

                @block.gpsimd
                def _(pool):
                    for f in range(KT):
                        ins = pool.tensor_scalar(rksel[:, f, :], const("headsel"), v("rwkv_r_k", f), None, ALU.mult)
                    pool_step.link(pool, ins)
                    pool.wait_ge(keyed, 1)
                    pool.tensor_tensor(bet[:], bet[:], kap, ALU.mult).then_inc(beta_done, 1)
                    pool.wait_ge(beta_done, 1)
                    pool.wait_ge(exps, 4)
                    pool.tensor_tensor(bet[:], bet[:], Ls, ALU.mult)

                @block.vector
                def _(dve):
                    def interpolate(i):
                        if i == 2:
                            dve.wait_ge(at_lo, 4 * numbers[1])
                        for k in range(KT):
                            ins = nc.vector.scalar_tensor_tensor(mix[:, i % 2, k, :], xx[:, k, :], v("rwkv_mu", (2, 0, 3)[i] * KT + k),
                                                                 AT[:, k, :], ALU.mult, ALU.add)
                            if k % 2:
                                ins.then_inc(at_ready[k // 2], 1)

                    def rests(i):
                        for c in range(4):
                            at_rest(dve, numbers[i], c, mix[:, i % 2])

                    def running():
                        dve.wait_ge(at_lo, 4 * numbers[1] + 4)
                        for i in range(16):
                            ins = nc.vector.tensor_tensor_scan(Lp[:, i, :], const("ones"), kap[:, i, :], 0.0, ALU.mult, ALU.add)
                        dve_step.link(dve, ins)
                        mid = Lp[:, :, C // 2 - 1:C // 2]
                        dve_step.link(dve, nc.vector.tensor_tensor(Ls, Lp, mid.broadcast_to([P, 16, C]), ALU.subtract))
                        four = lambda z: z.rearrange("p (f c) t -> p f c t", c=2)
                        dve_step.link(dve, nc.vector.tensor_tensor(
                            fac[:].rearrange("p (f a) -> p f a", a=1), four(Ls)[:, :, 0, C - 1:C],
                            four(Lp)[:, :, 1, C // 2 - 1:C // 2], ALU.add))
                        nc.vector.tensor_tensor(Lp, Ls, kap, ALU.subtract).then_inc(decays, 1)

                    def greatest():
                        for b in range(4):
                            dve.wait_ge(key_sum, b + 1)
                            nc.vector.tensor_scalar(flat(rn)[:, b * 512:(b + 1) * 512], pb[4 + b][:], 1e-24, None,
                                                    ALU.max).then_inc(key_max, 1)

                    def keys():
                        dve.wait_ge(decays, 1)
                        dve_step.wait(dve)
                        for f in range(KT):
                            w = slice(2 * f, 2 * f + 2)
                            ins = nc.vector.scalar_tensor_tensor(kap[:, w, :], kh[:, w, :], v("rwkv_k_k", f), rn[:, w, :],
                                                                 ALU.mult, ALU.mult)
                        dve_step.link(dve, ins)
                        for f in range(KT):
                            w = slice(2 * f, 2 * f + 2)
                            ins = nc.vector.tensor_scalar(rn[:, w, :], bet[:, w, :], 1.0, v("rwkv_k_a", f), ALU.subtract, ALU.mult)
                        ins.then_inc(keyed, 1)

                    def keys_more():
                        dve.wait_ge(keyed, 1)
                        dve_step.link(dve, nc.vector.scalar_tensor_tensor(kh[:], rn, 1.0, kh[:], ALU.add, ALU.mult))
                        dve.wait_ge(rkv_read, 8)
                        nc.vector.tensor_tensor(rn, rho, kh[:], ALU.mult).then_inc(bonus_in, 1)

                    interpolate(0)
                    rests(0)
                    interpolate(1)
                    for q in range(12):
                        rest_to(dve, nk + q + 3)
                        if q in (3, 7):
                            rests(q // 4 + 1)
                        if q == 3:
                            interpolate(2)
                        if q == 4:
                            running()
                        if q == 6:
                            greatest()
                        if q in (7, 8):
                            dve.wait_ge(key_root, 1)
                            for i in range(2):
                                w = slice(8 * (q - 7) + 4 * i, 8 * (q - 7) + 4 * i + 4)
                                dve_step.mark(nc.vector.reciprocal(rn[:, w, :], rn[:, w, :]))
                        if q == 9:
                            keys()
                        if q == 10:
                            keys_more()
                        if q == 11:
                            dve.wait_ge(bonus_in, 1)
                            dve.wait_ge(exps, 4)
                            nc.vector.tensor_tensor(rho, rho, E1, ALU.mult)
                            nc.vector.tensor_tensor(kh[:], kh[:], Ls, ALU.mult)
                            dve.wait_ge(beta_done, 1)
                            nc.vector.tensor_tensor(kap, kap, Lp, ALU.mult)
                    rest_to(dve, n0 + 3)
                    dve.wait_ge(bonus_done, 1)
                    nc.vector.tensor_copy(bonus[:].rearrange("p t h -> p (t h)"), pb[4][:, 0:2 * HEADS])

                @block.scalar
                def _(act):
                    for c in range(4):
                        at_round(act, numbers[0], c, mix[:, 0])
                    for q in range(12):
                        round_to(act, nk + q + 3)
                        act.wait_ge(used, nk + q + 1)
                        if q in (3, 7):
                            for c in range(4):
                                at_round(act, numbers[q // 4 + 1], c, mix[:, (q // 4 + 1) % 2])
                        bank, b = pb[q % 4], q % 4
                        if q >= 8:
                            dst, src = V[:, :, b * 256:(b + 1) * 256], bank[:].rearrange("p (t n) -> p t n", t=2)
                        else:
                            dst = (kh[:, 4 * b:4 * b + 4, :] if q < 4 else KR[:, 4 * b:4 * b + 4, 1, :])
                            src = bank[:].rearrange("p (f t) -> p f t", f=4)
                        nc.scalar.copy(dst, src).then_inc(rkv_read, 1)
                        if q == 4:
                            act.wait_ge(rkv_read, 4)
                            act.wait_ge(at_ready[3], numbers[2] + 1 - skipped[0])
                            for f in range(KT):
                                ins = nc.scalar.activation(rn[:, 2 * f:2 * f + 2, :], kh[:, 2 * f:2 * f + 2, :], ACT.Square,
                                                           scale=v("rwkv_k_k", f))
                            ins.then_inc(key_sq, 1)
                        if q == 6:
                            act.wait_ge(key_max, 4)
                            nc.scalar.activation(rn, rn, ACT.Sqrt).then_inc(key_root, 1)
                        if q == 7:
                            act.wait_ge(decays, 1)
                            act.wait_ge(at_lo, 4 * numbers[2] + 4)
                            nc.scalar.activation(E1, Ls, ACT.Exp, scale=CD).then_inc(exps, 1)
                            nc.scalar.activation(Lp, Lp, ACT.Exp, scale=CD).then_inc(exps, 1)
                            nc.scalar.activation(fac[:], fac[:], ACT.Exp, scale=CD).then_inc(exps, 1)
                            act.wait_ge(exps, 1)
                            nc.scalar.activation(Ls, Ls, ACT.Exp, scale=-CD).then_inc(exps, 1)
                    round_to(act, n0 + 3)

        pairs_done = sem("pairs_done")
        pairs_read = sem("pairs_read")
        level_in = sem("level_in")
        y_done = sem("y_done")
        y_copied = sem("y_copied")
        x_done = sem("x_done")
        x_new = sem("x_new")
        w_done, w_copied, u_done, u_copied, o_done, o_copied = (sem(n) for n in (
            "w_done", "w_copied", "u_done", "u_copied", "o_done", "o_copied"))
        tok_done, tok_copied, s_done, s_copied = (sem(n) for n in ("tok_done", "tok_copied", "s_done", "s_copied"))
        Y = xn
        with ExitStack() as stage:
            AD = sb("AD", [P, 2, 4, 256], stage=stage)
            BE = sb("BE", [P, 2, 4, 256], stage=stage)
            N = sb("N", [P, 2, 2, 4, C], stage=stage)
            X, XT = (AT[:, 4 * i:4 * i + 4, :].rearrange("p k t -> p (k t)").rearrange("p (g h c) -> p g h c", g=2, h=4)
                     for i in range(2))
            YS = sb("YS", [P, 2, 4, C], stage=stage)
            W = sb("W", [P, 2, 4, DH], stage=stage)
            U = sb("U", [P, 2, 4, DH], stage=stage)
            BT = sb("BT", [P, 2, 4, C], stage=stage)
            four = lambda z: z.rearrange("p (h n) -> p h n", h=4)
            rounds = [(c, d) for c in range(2) for d in range(2)]
            with nc.Block() as block:
                def heads(d, g):
                    return [(par, i, 4 * d + 2 * g + i) for par in range(2) for i in range(2)]

                @block.tensor
                def _(pe):
                    for r, (c, d) in enumerate(rounds):
                        for g in range(2):
                            if r:
                                pe.wait_ge(o_copied, 2 * (r - 1) + 2)
                                if c == 0 or r == 2:
                                    pe.wait_ge(s_copied, 2 * min(r, 2))
                            for j, (par, i, f) in enumerate(heads(d, g)):
                                rows = slice(DH * par, DH * par + DH)
                                both = KR[rows, 2 * f + c, :, :].rearrange("p a t -> p (a t)")
                                nc.tensor.matmul(pb[4 * g + par][:, i * 256:(i + 1) * 256], bet[rows, 2 * f + c, :], both,
                                                 start=True, stop=True)
                                ins = nc.tensor.matmul(pb[4 * g + 2 + par][:, i * 256:(i + 1) * 256], kh[rows, 2 * f + c, :],
                                                       both, start=True, stop=True)
                            ins.then_inc(pairs_done, 1)
                        for lv in range(7):
                            at = 7 * r + lv
                            for g in range(2):
                                pe.wait_ge(level_in, 2 * at + g + 1)
                                if lv == 0:
                                    pe.wait_ge(pairs_read, 2 * r + 2)
                                else:
                                    pe.wait_ge(x_new, 2 * (at - 1) + g + 1)
                                for j in range(4):
                                    ins = nc.tensor.matmul(pb[g][:, j * C:(j + 1) * C], N[:, at % 2, g, j, :],
                                                           X[:, g, j, :] if lv else ident, start=True, stop=True)
                                ins.then_inc(y_done, 1)
                            if lv:
                                for g in range(2):
                                    pe.wait_ge(y_copied, 2 * (6 * r + lv - 1) + g + 1)
                                    for j in range(4):
                                        if lv < 6:
                                            nc.tensor.matmul(pb[2 + g][:, j * C:(j + 1) * C], XT[:, g, j, :], YS[:, g, j, :],
                                                             start=True, stop=True)
                                        ins = nc.tensor.matmul(pb[4 + g][:, j * C:(j + 1) * C], YS[:, g, j, :], XT[:, g, j, :],
                                                               start=True, stop=True)
                                    ins.then_inc(x_done, 1)
                        for g in range(2):
                            pe.wait_ge(x_new, 2 * (7 * r + 6) + g + 1)
                            for par, i, f in heads(d, g):
                                h = 2 * f + par
                                o = pb[2 * g + par][:, i * DH:(i + 1) * DH]
                                rows = slice(DH * par, DH * par + DH)
                                ins = nc.tensor.matmul(o, BE[:, g, 2 * par + i, 0:C], V[:, c, h * DH:(h + 1) * DH],
                                                       start=True, stop=(c == 0))
                                if c:
                                    ins = nc.tensor.matmul(o, KR[rows, 2 * f + c, 0, :], S0[rows, f, :], start=False, stop=True)
                            ins.then_inc(w_done, 1)
                        for g in range(2):
                            pe.wait_ge(w_copied, 2 * r + g + 1)
                            for j in range(4):
                                ins = nc.tensor.matmul(pb[4 + g][:, j * DH:(j + 1) * DH], XT[:, g, j, :], W[:, g, j, :],
                                                       start=True, stop=True)
                            ins.then_inc(u_done, 1)
                        if c == 0:
                            for g in range(2):
                                for z, src in enumerate((bet, kh)):
                                    for i in range(2):
                                        f = 4 * d + 2 * g + i
                                        ins = nc.tensor.transpose(pb[6 + g][:, (2 * z + i) * C:(2 * z + i + 1) * C],
                                                                  src[:, 2 * f + c, :], ident)
                                ins.then_inc(tok_done, 1)
                        for g in range(2):
                            pe.wait_ge(u_copied, 2 * r + g + 1)
                            for par, i, f in heads(d, g):
                                h, j = 2 * f + par, 2 * par + i
                                o = pb[2 * g + par][:, i * DH:(i + 1) * DH]
                                rows = slice(DH * par, DH * par + DH)
                                nc.tensor.matmul(o, AD[:, g, j, C:2 * C], U[:, g, j, :], start=True, stop=False)
                                ins = nc.tensor.matmul(o, BE[:, g, j, C:2 * C], V[:, c, h * DH:(h + 1) * DH],
                                                       start=False, stop=(c == 0))
                                if c:
                                    ins = nc.tensor.matmul(o, KR[rows, 2 * f + c, 1, :], S0[rows, f, :], start=False, stop=True)
                            ins.then_inc(o_done, 1)
                        if c == 0:
                            for g in range(2):
                                pe.wait_ge(tok_copied, 2 * r + g + 1)
                                for par, i, f in heads(d, g):
                                    h, j = 2 * f + par, 2 * par + i
                                    o = pb[4 + g][DH * par:DH * par + DH, i * DH:(i + 1) * DH]
                                    nc.tensor.matmul(o, BT[:, g, i, DH * par:DH * par + DH], U[:, g, j, :], start=True, stop=False)
                                    ins = nc.tensor.matmul(o, BT[:, g, 2 + i, DH * par:DH * par + DH],
                                                           V[:, c, h * DH:(h + 1) * DH], start=False, stop=True)
                                ins.then_inc(s_done, 1)

                @block.gpsimd
                def _(pool):
                    for r in range(4):
                        for lv in range(7):
                            for g in range(2):
                                at = 7 * r + lv
                                if lv == 0:
                                    pool.wait_ge(pairs_read, 2 * r + g + 1)
                                if at >= 2:
                                    pool.wait_ge(y_done, 2 * (at - 2) + g + 1)
                                if lv == 2:
                                    pool.wait_ge(x_new, 2 * (at - 2) + g + 1)
                                mask = const(f"level{lv}").rearrange("p (a t) -> p a t", a=1).broadcast_to([P, 4, C])
                                pool.tensor_tensor(N[:, at % 2, g, :, :], AD[:, g, :, 0:C], mask, ALU.mult).then_inc(level_in, 1)

                @block.vector
                def _(dve):
                    idb = ident.rearrange("p (a t) -> p a t", a=1).broadcast_to([P, 4, C])
                    for r, (c, d) in enumerate(rounds):
                        for g in range(2):
                            dve.wait_ge(pairs_done, 2 * r + g + 1)
                            for par in range(2):
                                for z, dst in enumerate((AD, BE)):
                                    ins = nc.vector.tensor_tensor(
                                        dst[:, g, 2 * par:2 * par + 2, :].rearrange("p h n -> p (h n)"),
                                        pb[4 * g + 2 * z + par][:], const("pairmask"), ALU.mult)
                            ins.then_inc(pairs_read, 1)
                        for lv in range(7):
                            at = 7 * r + lv
                            for g in range(2):
                                if lv == 0:
                                    dve.wait_ge(y_done, 2 * at + g + 1)
                                    nc.vector.tensor_tensor(X[:, g, :, :], idb, four(pb[g][:]), ALU.subtract)
                                    nc.vector.tensor_tensor(XT[:, g, :, :], idb, N[:, at % 2, g, :, :], ALU.subtract).then_inc(x_new, 1)
                                    continue
                                dve.wait_ge(x_done, 2 * (6 * r + lv - 1) + g + 1)
                                dve.wait_ge(x_new, 2 * at - 2 + g + 1)
                                if lv < 6:
                                    nc.vector.tensor_tensor(X[:, g, :, :], X[:, g, :, :], four(pb[2 + g][:]), ALU.subtract)
                                nc.vector.tensor_tensor(XT[:, g, :, :], XT[:, g, :, :], four(pb[4 + g][:]),
                                                        ALU.subtract).then_inc(x_new, 1)
                        if c == 0:
                            for g in range(2):
                                dve.wait_ge(tok_done, 2 * r + g + 1)
                                nc.vector.tensor_copy(BT[:, g, :, :], four(pb[6 + g][:])).then_inc(tok_copied, 1)
                            for g in range(2):
                                dve.wait_ge(s_done, 2 * r + g + 1)
                                for i in range(2):
                                    f = 4 * d + 2 * g + i
                                    ins = nc.vector.tensor_scalar(S0[:, f, :], pb[4 + g][:, i * DH:(i + 1) * DH],
                                                                  fac[:, f:f + 1], None, ALU.mult)
                                ins.then_inc(s_copied, 1)

                @block.scalar
                def _(act):
                    for r, (c, d) in enumerate(rounds):
                        for lv in range(1, 7):
                            for g in range(2):
                                act.wait_ge(y_done, 2 * (7 * r + lv) + g + 1)
                                nc.scalar.copy(YS[:, g, :, :], four(pb[g][:])).then_inc(y_copied, 1)
                        for g in range(2):
                            act.wait_ge(w_done, 2 * r + g + 1)
                            for par in range(2):
                                ins = nc.scalar.copy(W[:, g, 2 * par:2 * par + 2, :],
                                                     pb[2 * g + par][:, 0:2 * DH].rearrange("p (h n) -> p h n", h=2))
                            ins.then_inc(w_copied, 1)
                        for g in range(2):
                            act.wait_ge(u_done, 2 * r + g + 1)
                            nc.scalar.mul(U[:, g, :, :], four(pb[4 + g][:, 0:4 * DH]), -1.0).then_inc(u_copied, 1)
                        for g in range(2):
                            act.wait_ge(o_done, 2 * r + g + 1)
                            for par in range(2):
                                f = 4 * d + 2 * g
                                dst = Y[:, c, :].rearrange("p (f a n) -> p f a n", a=2, n=DH)[:, f:f + 2, par, :]
                                ins = nc.scalar.copy(dst, pb[2 * g + par][:, 0:2 * DH].rearrange("p (h n) -> p h n", h=2))
                            ins.then_inc(o_copied, 1)

        lnx_in = sem("lnx_in")
        y_sq = sem("y_sq")
        y_centred = sem("y_centred")
        y_var = sem("y_var")
        y_root = sem("y_root")
        y_ready = sem("y_ready")
        y_turned = sem("y_turned")
        with ExitStack() as stage:
            lw = sb("lw", [P, D], stage=stage)
            lb = sb("lb", [P, D], stage=stage)
            sq = sb("sq", [P, TT, D], stage=stage)
            hs = sb("hs", [P, 2, TT * HEADS], stage=stage)
            open_acts(stage)
            no = new_split()
            after = ffn_plan[1]["gate", 0]
            ahead(after + 2)
            hv = lambda z: z.rearrange("p t (h n) -> p (t h) n", n=DH)
            one = lambda z: z.rearrange("p (h a) -> p h a", a=1).broadcast_to([P, TT * HEADS, DH])
            with nc.Block() as block:
                @block.sync
                def _(sp):
                    sp.dma_start(lw[:], a["rwkv_lnx_w"][0:1, :].broadcast_to([P, D])).then_inc(lnx_in, 16)
                    sp.dma_start(lb[:], a["rwkv_lnx_b"][0:1, :].broadcast_to([P, D])).then_inc(lnx_in, 16)
                    feed(sp)

                @block.vector
                def _(dve):
                    L = lambda ins: dve_step.link(dve, ins)
                    L(nc.vector.reduce_sum(hs[:, 0, :], hv(Y[:]), AX))
                    L(nc.vector.tensor_scalar(hs[:, 0, :], hs[:, 0, :], 1.0 / DH, None, ALU.mult))
                    nc.vector.tensor_tensor(hv(Y[:]), hv(Y[:]), one(hs[:, 0, :]), ALU.subtract).then_inc(y_centred, 1)
                    dve.wait_ge(y_sq, 1)
                    nc.vector.reduce_sum(hs[:, 1, :], hv(sq[:]), AX).then_inc(y_var, 1)
                    dve.wait_ge(y_root, 1)
                    L(nc.vector.reciprocal(hs[:, 1, :], hs[:, 1, :]))
                    L(nc.vector.tensor_tensor(hv(Y[:]), hv(Y[:]), one(hs[:, 1, :]), ALU.mult))
                    dve.wait_ge(lnx_in, 32)
                    rowb = lambda z: z.rearrange("p (a n) -> p a n", a=1).broadcast_to([P, TT, D])
                    L(nc.vector.tensor_tensor(Y[:], Y[:], rowb(lw[:]), ALU.mult))
                    dve_step.mark(nc.vector.tensor_tensor(Y[:], Y[:], rowb(lb[:]), ALU.add))
                    L(nc.vector.tensor_tensor(hv(sq[:]), hv(V[:]), one(bonus[:].rearrange("p t h -> p (t h)")), ALU.mult))
                    nc.vector.tensor_tensor(Y[:], Y[:], sq[:], ALU.add).then_inc(y_ready, 1)
                    for b in range(4):
                        dve.wait_ge(y_turned, b + 1)
                        w = slice(2 * b, 2 * b + 2)
                        ins = nc.vector.tensor_tensor(AT[:, w, :].rearrange("p f t -> p (f t)"), pb[b][:],
                                                      G[:, w, :].rearrange("p f t -> p (f t)"), ALU.mult)
                        ins.then_inc(at_ready[b], 1)
                    for c in range(4):
                        at_rest(dve, no, c)
                    rest_to(dve, after + 2)
                    add_projected(dve, n0 + 4)

                @block.scalar
                def _(act):
                    act.wait_ge(y_centred, 1)
                    nc.scalar.activation(sq[:], Y[:], ACT.Square).then_inc(y_sq, 1)
                    act.wait_ge(y_var, 1)
                    nc.scalar.activation(hs[:, 1, :], hs[:, 1, :], ACT.Sqrt, scale=1.0 / DH,
                                         bias=const("lnx_eps")).then_inc(y_root, 1)
                    for c in range(4):
                        at_round(act, no, c)
                    round_to(act, after + 2)

                @block.tensor
                def _(pe):
                    pe.wait_ge(y_ready, 1)
                    for b in range(4):
                        for i in range(2):
                            for t in range(TT):
                                f = 2 * b + i
                                ins = nc.tensor.transpose(pb[b][:, i * T + t * P:i * T + (t + 1) * P],
                                                          Y[:, t, f * P:(f + 1) * P], ident)
                        ins.then_inc(y_turned, 1)
                    for c in range(4):
                        pe.wait_ge(at_lo, 4 * no + c + 1)
                        project(pe, n0 + c, c, 4, acts)
        rwkv.close()
        cos2, sin2 = sb("cos2", [P, T]), sb("sin2", [P, T])
        seen = sb("seen", [P, TT, T])
        nlam = sb("nlam", [P, 2])
        decay8 = sb("decay8", [P, 8])
        two_in = sem("two_in")
        two_exp = sem("two_exp")
        two_ready = sem("two_ready")
        lam0 = [0.8 - 0.6 * math.exp(-0.3 * l) for l in range(2)]
        TWO_PI = 2.0 * math.pi
        C1 = 6.28125
        C2 = float(np.round((TWO_PI - C1) * 2 ** 21) / 2 ** 21)
        C3 = TWO_PI - C1 - C2
        MAGIC = 1.5 * 2.0 ** 23
        with ExitStack() as stage:
            posb = sb("posb", [P, T], I32, stage=stage)
            posq = sb("posq", [P, TT], I32, stage=stage)
            fl = sb("fl", [P, 4, T], stage=stage)
            cq = sb("cq", [P, TT], stage=stage)
            lams = sb("lams", [P, 4, 2, DH], stage=stage)
            dots = sb("dots", [P, 2, 2], stage=stage)
            sp8 = sb("sp8", [P, 6, 8], stage=stage)
            with nc.Block() as block:
                @block.sync
                def _(sp):
                    sp.dma_start(posb[:], a["positions_2"][0:1, :].broadcast_to([P, T])).then_inc(two_in, 16)
                    sp.dma_start(posq[:], a["positions_2"][0].rearrange("(t p) -> p t", p=P), allow_slow_non_contiguous=True).then_inc(two_in, 16)
                    for i, n in enumerate(("lam_q1_2", "lam_k1_2", "lam_q2_2", "lam_k2_2")):
                        sp.dma_start(lams[:, i, :, :].rearrange("p l d -> p (l d)"),
                                     a[n].rearrange("(a l) d -> a (l d)", a=1).broadcast_to([P, 2 * DH])).then_inc(two_in, 16)

                @block.vector
                def _(dve):
                    L = lambda ins: dve_step.link(dve, ins)
                    ts, tt = nc.vector.tensor_scalar, nc.vector.tensor_tensor
                    dve.wait_ge(two_in, 96)
                    L(nc.vector.tensor_copy(fl[:, 0, :], posb[:]))
                    L(ts(fl[:, 0, :], fl[:, 0, :], const("inv"), None, ALU.mult))
                    L(ts(fl[:, 1, :], fl[:, 0, :], 1.0 / TWO_PI, MAGIC, ALU.mult, ALU.add))
                    L(ts(fl[:, 1, :], fl[:, 1, :], MAGIC, None, ALU.subtract))
                    for part in (C1, C2, C3):
                        L(nc.vector.scalar_tensor_tensor(fl[:, 0, :], fl[:, 1, :], -part, fl[:, 0, :], ALU.mult, ALU.add))
                    L(ts(fl[:, 2, :], fl[:, 0, :], math.pi / 2, None, ALU.add))
                    L(ts(fl[:, 3, :], fl[:, 2, :], math.pi, -TWO_PI, ALU.is_gt, ALU.mult))
                    L(tt(fl[:, 2, :], fl[:, 2, :], fl[:, 3, :], ALU.add))
                    PI = 3.1415925
                    L(ts(fl[:, 2, :], fl[:, 2, :], PI, -PI, ALU.min, ALU.max))
                    ts(fl[:, 0, :], fl[:, 0, :], PI, -PI, ALU.min, ALU.max).then_inc(two_ready, 1)
                    dve_step.mark(nc.vector.tensor_scalar(posq[:], posq[:], 6, None, ALU.arith_shift_right))
                    L(nc.vector.tensor_scalar(posb[:], posb[:], 6, None, ALU.arith_shift_right))
                    dve_step.mark(nc.vector.tensor_copy(cq[:], posq[:]))
                    L(nc.vector.tensor_copy(fl[:, 3, :], posb[:]))
                    for t in range(TT):
                        dve_step.mark(ts(seen[:, t, :], fl[:, 3, :], cq[:, t:t + 1], 1.0, ALU.is_le, ALU.subtract))
                    dve_step.wait(dve)
                    dve_step.mark(ts(seen[:], seen[:], BIG, None, ALU.mult))
                    for i in range(2):
                        dve_step.mark(tt(lams[:, 2 * i, :, :], lams[:, 2 * i, :, :], lams[:, 2 * i + 1, :, :], ALU.mult))
                    dve_step.wait(dve)
                    for i in range(2):
                        ins = nc.vector.reduce_sum(dots[:, i, :], lams[:, 2 * i, :, :], AX)
                    ins.then_inc(two_ready, 1)
                    lam = v("lru_lambda_2", 0, 8)
                    L(ts(sp8[:, 0, :], lam, -1.0, None, ALU.mult))
                    L(tt(sp8[:, 1, :], sp8[:, 0, :], lam, ALU.min))
                    ts(sp8[:, 0, :], sp8[:, 0, :], 0.0, None, ALU.max).then_inc(two_ready, 1)
                    dve.wait_ge(two_exp, 1)
                    ts(sp8[:, 2, :], sp8[:, 1, :], 1.0, None, ALU.add).then_inc(two_ready, 1)
                    dve.wait_ge(two_ready, 4)
                    L(ts(sp8[:, 3, :], sp8[:, 2, :], 1.0, None, ALU.subtract))
                    L(ts(sp8[:, 4, :], sp8[:, 3, :], 0.0, None, ALU.is_equal))
                    L(tt(sp8[:, 3, :], sp8[:, 3, :], sp8[:, 4, :], ALU.add))
                    L(nc.vector.reciprocal(sp8[:, 3, :], sp8[:, 3, :]))
                    dve.wait_ge(two_exp, 2)
                    L(tt(sp8[:, 5, :], sp8[:, 5, :], sp8[:, 3, :], ALU.mult))
                    L(tt(sp8[:, 5, :], sp8[:, 5, :], sp8[:, 4, :], ALU.add))
                    L(tt(sp8[:, 5, :], sp8[:, 5, :], sp8[:, 1, :], ALU.mult))
                    L(tt(sp8[:, 5, :], sp8[:, 5, :], sp8[:, 0, :], ALU.add))
                    dve_step.mark(ts(decay8[:], sp8[:, 5, :], -8.0, None, ALU.mult))
                    dve.wait_ge(two_exp, 3)
                    for l in range(2):
                        L(tt(nlam[:, l:l + 1], dots[:, 1, l:l + 1], dots[:, 0, l:l + 1], ALU.subtract))
                        L(ts(nlam[:, l:l + 1], nlam[:, l:l + 1], -lam0[l], None, ALU.add))

                @block.scalar
                def _(act):
                    act.wait_ge(two_ready, 1)
                    nc.scalar.activation(sin2[:], fl[:, 0, :], ACT.Sin)
                    nc.scalar.activation(cos2[:], fl[:, 2, :], ACT.Sin)
                    act.wait_ge(two_ready, 3)
                    nc.scalar.activation(sp8[:, 1, :], sp8[:, 1, :], ACT.Exp).then_inc(two_exp, 1)
                    act.wait_ge(two_ready, 4)
                    nc.scalar.activation(sp8[:, 5, :], sp8[:, 2, :], ACT.Ln).then_inc(two_exp, 1)
                    nc.scalar.activation(dots[:], dots[:], ACT.Exp).then_inc(two_exp, 1)

        make_gates(0)
        open_acts(ctx)
        no = norm_turn(3, lambda f: v("norm_ffn", KT + f), then=ffn_plan[1]["gate", 0], look=2)
        ffn(1, no, first["win0"], conv=1, gate_rows=0, finished=0)
        norm_rows(4, a["norm_final"].rearrange("(a d) -> a d", a=1))
        lru_in = sem("lru_in")
        pads_clear = sem("pads_clear")
        win_read = sem("win_read")
        rot2 = sem("rot2")
        rotated2 = sem("rotated2")
        lru_conv = sem("lru_conv")
        lru_gate = sem("lru_gate")
        lru_gate_read = sem("lru_gate_read")
        lru_log = sem("lru_log")
        lru_exp = sem("lru_exp")
        lru_mult = sem("lru_mult")
        d_scored, d_masked, d_maxed, d_exped, d_mixed = (sem("d_" + n) for n in ("scored", "masked", "maxed", "exped", "mixed"))
        d_turned, d_copied, d_out, d_read = (sem("d_" + n) for n in ("turned", "copied", "out", "read"))
        o_sq, o_var, o_root, o_norm, o_turned = (sem("o_" + n) for n in ("sq", "var", "root", "norm", "turned"))

        def mixer(l, no, then, norm):
            n0, n1 = first[f"win{l}"], first[f"wout{l}"]
            ahead(n1 + 3)
            own = new_split()
            with ExitStack() as stage:
                QK = sb(f"QK{l}", [P, 8, T], stage=stage)
                V = sb(f"V{l}", [P, TT, 512], stage=stage)
                lru = ExitStack()
                xp = sb(f"xp{l}", [P, 4, T + 3], stage=lru)
                xc = sb(f"xc{l}", [P, 4, T], stage=lru)
                yr = sb(f"yr{l}", [P, 4, T], stage=lru)
                rg = sb(f"rg{l}", [P, 4, T], stage=lru)
                ig = sb(f"ig{l}", [P, 4, T], stage=lru)
                e2, th = (xn[:, i, :].rearrange("p (f t) -> p f t", f=4) for i in range(2))
                raw = sb(f"raw{l}", [P, 2, 2 * T], stage=lru)
                rc = sb(f"rc{l}", [P, 2, 2 * T], stage=lru)
                rs = sb(f"rs{l}", [P, 2, 2 * T], stage=lru)
                bd = [sb(f"bd{i}{l}", [P, 4, P], stage=lru) for i in range(2)]
                with nc.Block() as block:
                    @block.sync
                    def _(sp):
                        feed(sp)

                    @block.gpsimd
                    def _(pool):
                        for b in bd:
                            ins = pool.memset(b[:], 0.0)
                            ins.then_inc(pads_clear, 1)
                        pool.memset(xp[:, :, 0:3], 0.0).then_inc(pads_clear, 1)
                        pool.wait_ge(pads_clear, 3 * l + 3)
                        for b, name in zip(bd, ("gate_a_w_2", "gate_x_w_2")):
                            for par in range(2):
                                pool.dma_start(b[DH * par:DH * par + DH, :, DH * par:DH * par + DH],
                                               a[name][l, par::2].rearrange("n h k -> h n k")).then_inc(lru_in, 16)

                    @block.tensor
                    def _(pe):
                        for i in range(10):
                            if i >= 3:
                                pe.wait_ge(win_read, 10 * l + i - 2)
                            if i >= 8:
                                to_tokens(pe, n0 + i, pb[i % 3])
                            else:
                                to_features(pe, n0 + i, pb[i % 3], None if i else no)
                            if 5 <= i <= 8:
                                b = i - 5
                                pe.wait_ge(win_read, 10 * l + i)
                                if b >= 2:
                                    pe.wait_ge(rotated2, 4 * l + b - 1)
                                nc.tensor.matmul(pb[4 + b % 2][:], const("rot"), raw[:, b % 2, :], start=True,
                                                 stop=True).then_inc(rot2, 1)
                            if i == 4:
                                pe.wait_ge(lru_in, 64 * (l + 1))
                                pe.wait_ge(lru_conv, l + 1)
                                for q in range(4):
                                    if q == 3:
                                        pe.wait_ge(lru_gate_read, 4 * l + 1)
                                    for f in range(2):
                                        ft = 2 * (q % 2) + f
                                        ins = nc.tensor.matmul(pb[(6, 7, 3, 6)[q]][:, f * T:(f + 1) * T], bd[q // 2][:, ft, :],
                                                               xc[:, ft, :], start=True, stop=True)
                                    ins.then_inc(lru_gate, 1)

                    @block.scalar
                    def _(act):
                        def read(i):
                            round_to(act, n0 + i + 3)
                            act.wait_ge(used, n0 + i + 1)
                            two = pb[i % 3][:].rearrange("p (f t) -> p f t", f=2)
                            if i < 2:
                                dst = xp[:, 2 * i:2 * i + 2, 3:]
                            elif i < 4:
                                dst = yr[:, 2 * i - 4:2 * i - 2, :]
                            elif i < 8:
                                if i >= 6:
                                    act.wait_ge(rotated2, 4 * l + i - 5)
                                dst = raw[:, i % 2, :].rearrange("p (f t) -> p f t", f=2)
                            else:
                                dst = V[:, :, (i - 8) * 256:(i - 7) * 256]
                            nc.scalar.copy(dst, two).then_inc(win_read, 1)

                        for i in range(5):
                            read(i)
                        for q in range(4):
                            act.wait_ge(lru_gate, 4 * l + q + 1)
                            for f in range(2):
                                ft = 2 * (q % 2) + f
                                ins = nc.scalar.activation((rg, ig)[q // 2][:, ft, :], pb[(6, 7, 3, 6)[q]][:, f * T:(f + 1) * T],
                                                           ACT.Sigmoid, bias=v(("gate_a_b_2", "gate_x_b_2")[q // 2], 4 * l + ft))
                            ins.then_inc(lru_gate_read, 1)
                        read(5)
                        read(6)
                        act.wait_ge(lru_log, l + 1)
                        nc.scalar.activation(e2, rg[:], ACT.Exp, scale=2.0)
                        nc.scalar.activation(th, rg[:], ACT.Tanh, scale=-1.0).then_inc(act_step.sem, 1)
                        act_step.n += 1
                        act_step.wait(act)
                        nc.scalar.activation(rg[:], rg[:], ACT.Exp).then_inc(lru_exp, 1)
                        read(7)
                        act.wait_ge(lru_mult, l + 1)
                        nc.scalar.activation(th, th, ACT.Sqrt).then_inc(lru_exp, 1)
                        nc.scalar.activation(yr[:], yr[:], ACT.Gelu_apprx_tanh).then_inc(lru_exp, 1)
                        read(8)
                        read(9)
                        round_to(act, n1 + 3)

                    @block.vector
                    def _(dve):
                        L = lambda ins: dve_step.link(dve, ins)

                        def rotate(b):
                            three = lambda z: z.rearrange("p (f t) -> p f t", f=2)
                            cos = cos2[:].rearrange("p (a t) -> p a t", a=1).broadcast_to([P, 2, T])
                            sin = sin2[:].rearrange("p (a t) -> p a t", a=1).broadcast_to([P, 2, T])
                            rest_to(dve, n0 + 4 + b + 3)
                            dve.wait_ge(win_read, 10 * l + 5 + b)
                            dve_step.mark(nc.vector.tensor_tensor(three(rc[:, b % 2, :]), three(raw[:, b % 2, :]), cos, ALU.mult))
                            dve.wait_ge(rot2, 4 * l + b + 1)
                            L(nc.vector.tensor_tensor(three(rs[:, b % 2, :]), three(pb[4 + b % 2][:]), sin, ALU.mult))
                            nc.vector.tensor_tensor(QK[:, 2 * b:2 * b + 2, :].rearrange("p f t -> p (f t)"), rc[:, b % 2, :],
                                                    rs[:, b % 2, :], ALU.add).then_inc(rotated2, 1)

                        rest_to(dve, n0 + 4)
                        dve.wait_ge(pads_clear, 3 * l + 3)
                        dve.wait_ge(win_read, 10 * l + 2)
                        for i in range(4):
                            for ft in range(4):
                                w = v("conv_w_2", (l * 4 + 3 - i) * 4 + ft)
                                src, dst = xp[:, ft, 3 - i:3 - i + T], xc[:, ft, :]
                                if i == 0:
                                    ins = nc.vector.tensor_scalar(dst, src, w, v("conv_b_2", 4 * l + ft), ALU.mult, ALU.add)
                                else:
                                    ins = nc.vector.scalar_tensor_tensor(dst, src, w, dst, ALU.mult, ALU.add)
                                if i == 3 and ft == 3:
                                    ins.then_inc(lru_conv, 1)
                                else:
                                    dve_step.mark(ins)
                            if i < 3:
                                dve_step.wait(dve)
                            if i == 0:
                                rest_to(dve, n0 + 5)
                            if i == 2:
                                rest_to(dve, n0 + 6)
                        rest_to(dve, n0 + 7)
                        dve.wait_ge(lru_gate_read, 4 * l + 4)
                        for ft in range(4):
                            ins = nc.vector.tensor_scalar(rg[:, ft, :], rg[:, ft, :], decay8[:, 4 * l + ft:4 * l + ft + 1], None, ALU.mult)
                        ins.then_inc(lru_log, 1)
                        dve.wait_ge(lru_conv, l + 1)
                        L(nc.vector.tensor_tensor(ig[:], ig[:], xc[:], ALU.mult))
                        rotate(0)
                        rotate(1)
                        dve.wait_ge(lru_exp, 3 * l + 1)
                        nc.vector.scalar_tensor_tensor(th, e2, 1.0, th, ALU.add, ALU.mult).then_inc(lru_mult, 1)
                        rotate(2)
                        dve.wait_ge(lru_exp, 3 * l + 2)
                        L(nc.vector.tensor_tensor(ig[:], ig[:], th, ALU.mult))
                        for ft in range(4):
                            ins = nc.vector.tensor_tensor_scan(xc[:, ft, :], rg[:, ft, :], ig[:, ft, :], 0.0, ALU.mult, ALU.add)
                        L(ins)
                        rotate(3)
                        rest_to(dve, n0 + 12)
                        dve.wait_ge(lru_exp, 3 * l + 3)
                        for c in range(2):
                            w = slice(2 * c, 2 * c + 2)
                            nc.vector.tensor_tensor(AT[:, w, :], xc[:, w, :], yr[:, w, :], ALU.mult).then_inc(at_ready[c], 1)
                        rest_to(dve, n1 + 3)
                lru.close()

                S = sb(f"S{l}", [P, 2, 2, 2 * T], stage=stage)
                st = sb(f"st{l}", [P, 4, 2, 3, TT], stage=stage)
                Pd = sb(f"Pd{l}", [P, 2, 2 * T], stage=stage)
                PT = sb(f"PT{l}", [P, 2, 2 * T], stage=stage)
                O = sb(f"O{l}", [P, TT, 4, P], stage=stage)
                osq = sb(f"osq{l}", [P, TT, 4, P], stage=stage)
                ov = sb(f"ov{l}", [P, 8], stage=stage)
                zz = sb(f"zz{l}", [P, 2, 512], stage=stage)
                sc = DH ** -0.5
                ahead(then + 2)
                norm = norm()
                with nc.Block() as block:
                    @block.tensor
                    def _(pe):
                        def score(h):
                            if h >= 2:
                                pe.wait_ge(d_masked, 8 * l + 2 * (h - 1))
                            for c in range(2):
                                rows = slice(DH * c, DH * c + DH)
                                for t in range(TT):
                                    ins = nc.tensor.matmul(pb[2 * (h % 2) + c][:, t * T:(t + 1) * T],
                                                           QK[rows, h, t * P:(t + 1) * P], QK[rows, 4 + h, :], start=True, stop=True)
                                ins.then_inc(d_scored, 1)

                        def turn(h):
                            pe.wait_ge(d_mixed, 4 * l + h + 1)
                            if h >= 2:
                                pe.wait_ge(d_copied, 4 * l + h - 1)
                            for t in range(TT):
                                for kt in range(2):
                                    ins = nc.tensor.transpose(pb[4 + h % 2][:, kt * T + t * P:kt * T + (t + 1) * P],
                                                              Pd[:, h % 2, t * T + kt * P:t * T + (kt + 1) * P], ident)
                            ins.then_inc(d_turned, 1)

                        def out(h):
                            pe.wait_ge(d_copied, 4 * l + h + 1)
                            if h >= 2:
                                pe.wait_ge(d_read, 4 * l + h - 1)
                            for t in range(TT):
                                for kt in range(2):
                                    ins = nc.tensor.matmul(pb[6 + h % 2][:, t * P:(t + 1) * P],
                                                           PT[:, h % 2, kt * T + t * P:kt * T + (t + 1) * P],
                                                           V[:, kt, h * P:(h + 1) * P], start=(kt == 0), stop=(kt == 1))
                            ins.then_inc(d_out, 1)

                        for i in range(6):
                            if i < 4:
                                score(i)
                            if 1 <= i <= 4:
                                turn(i - 1)
                            if i >= 2:
                                out(i - 2)
                        pe.wait_ge(o_norm, l + 1)
                        for h in range(4):
                            for t in range(TT):
                                ins = nc.tensor.transpose(pb[h // 2][:, (h % 2) * T + t * P:(h % 2) * T + (t + 1) * P], O[:, t, h, :], ident)
                        ins.then_inc(o_turned, 1)
                        pe.wait_ge(d_read, 4 * l + 4)
                        for c in range(4):
                            pe.wait_ge(at_lo, 4 * own + c + 1)
                            project(pe, n1 + c, c, 4, acts)
                        norm.pe(pe)

                    @block.sync
                    def _(sp):
                        feed(sp)

                    @block.vector
                    def _(dve):
                        def first_half(h):
                            for c in range(2):
                                dve.wait_ge(d_scored, 8 * l + 2 * h + c + 1)
                                nc.vector.tensor_tensor(S[:, h % 2, c, :], pb[2 * (h % 2) + c][:], seen[:].rearrange("p t k -> p (t k)"),
                                                        ALU.add).then_inc(d_masked, 1)
                            for c in range(2):
                                dve.wait_ge(d_masked, 8 * l + 2 * h + c + 1)
                                dve_step.mark(nc.vector.reduce_max(st[:, h, c, 0, :], S[:, h % 2, c, :].rearrange("p (t k) -> p t k", t=2), AX))
                            dve_step.wait(dve)
                            nc.vector.tensor_scalar(st[:, h, :, 0, :], st[:, h, :, 0, :], -sc, None, ALU.mult).then_inc(d_maxed, 1)

                        def second_half(h):
                            dve.wait_ge(d_exped, 16 * l + 4 * (h + 1))
                            dve_step.link(dve, nc.vector.reciprocal(st[:, h, :, 2, :], st[:, h, :, 1, :]))
                            dve_step.link(dve, nc.vector.tensor_scalar(st[:, h, 1, 2, :], st[:, h, 1, 2, :], nlam[:, l:l + 1], None, ALU.mult))
                            if h >= 2:
                                dve.wait_ge(d_turned, 4 * l + h - 1)
                            for t in range(TT):
                                w = slice(t * T, (t + 1) * T)
                                dve_step.mark(nc.vector.tensor_scalar(Pd[:, h % 2, w], S[:, h % 2, 0, w], st[:, h, 0, 2, t:t + 1], None, ALU.mult))
                            dve_step.wait(dve)
                            for t in range(TT):
                                w = slice(t * T, (t + 1) * T)
                                ins = nc.vector.scalar_tensor_tensor(Pd[:, h % 2, w], S[:, h % 2, 1, w], st[:, h, 1, 2, t:t + 1],
                                                                     Pd[:, h % 2, w], ALU.mult, ALU.add)
                            ins.then_inc(d_mixed, 1)

                        for h in range(5):
                            if h == 2:
                                for c in range(2):
                                    at_rest(dve, own, c)
                            if h >= 1:
                                second_half(h - 1)
                            if h < 4:
                                if h >= 2:
                                    dve.wait_ge(d_mixed, 4 * l + h - 1)
                                first_half(h)
                        dve.wait_ge(o_sq, l + 1)
                        nc.vector.reduce_sum(ov[:], osq[:].rearrange("p t h n -> p (t h) n"), AX).then_inc(o_var, 1)
                        dve.wait_ge(o_root, l + 1)
                        dve_step.link(dve, nc.vector.reciprocal(ov[:], ov[:]))
                        nc.vector.tensor_tensor(O[:].rearrange("p t h n -> p (t h) n"), O[:].rearrange("p t h n -> p (t h) n"),
                                                ov[:].rearrange("p (h a) -> p h a", a=1).broadcast_to([P, 8, P]), ALU.mult).then_inc(o_norm, 1)
                        dve.wait_ge(o_turned, l + 1)
                        for b in range(2):
                            nc.vector.tensor_scalar(AT[:, 4 + 2 * b:6 + 2 * b, :].rearrange("p f t -> p (f t)"), pb[b][:],
                                                    v("subln_g_2", l), 1.0 - lam0[l], ALU.mult, ALU.mult).then_inc(at_ready[2 + b], 1)
                        for c in range(2, 4):
                            at_rest(dve, own, c)
                        rest_to(dve, then + 2)
                        add_projected(dve, n1 + 4, gates[l][:, 0, :], zz, joined=True)
                        norm.dve(dve)

                    @block.scalar
                    def _(act):
                        for c in range(2):
                            at_round(act, own, c)
                        for i in range(6):
                            if i < 4:
                                act.wait_ge(d_maxed, 4 * l + i + 1)
                                for c in range(2):
                                    for t in range(TT):
                                        w = slice(t * T, (t + 1) * T)
                                        nc.scalar.activation(S[:, i % 2, c, w], S[:, i % 2, c, w], ACT.Exp, scale=sc,
                                                             bias=st[:, i, c, 0, t:t + 1],
                                                             accum_out=st[:, i, c, 1, t:t + 1]).then_inc(d_exped, 1)
                            if 1 <= i <= 4:
                                h = i - 1
                                act.wait_ge(d_turned, 4 * l + h + 1)
                                if h >= 2:
                                    act.wait_ge(d_out, 4 * l + h - 1)
                                nc.scalar.copy(PT[:, h % 2, :], pb[4 + h % 2][:]).then_inc(d_copied, 1)
                            if i >= 2:
                                h = i - 2
                                act.wait_ge(d_out, 4 * l + h + 1)
                                nc.scalar.copy(O[:, :, h, :], pb[6 + h % 2][:, 0:2 * P].rearrange("p (t n) -> p t n", t=2)).then_inc(d_read, 1)
                        act.wait_ge(d_read, 4 * l + 4)
                        nc.scalar.activation(osq[:], O[:], ACT.Square).then_inc(o_sq, 1)
                        act.wait_ge(o_var, l + 1)
                        nc.scalar.activation(ov[:], ov[:], ACT.Sqrt, scale=1.0 / P, bias=const("rms_eps")).then_inc(o_root, 1)
                        for c in range(2, 4):
                            at_round(act, own, c)
                        round_to(act, then + 2)
                        norm.act(act)
            return norm.no

        def shift(l, i):
            return lambda f: mods[:, l, 3 * i * KT + f:3 * i * KT + f + 1]

        def gain_of(l, i):
            return lambda f: gain2[:, l, i, f:f + 1]

        no = norm_turn(5, gain_of(0, 0), shift(0, 0), turns=4, then=first["win0"])
        no = mixer(0, no, ffn_plan[2]["gate", 0], lambda: Norm(6, gain_of(0, 1), shift(0, 1), turns=5,
                                                               then=ffn_plan[2]["gate", 0], look=2, joined=True))
        make_gates(1)
        norm = Norm(7, gain_of(1, 0), shift(1, 0), turns=6, then=first["win1"], look=2, joined=True)
        ffn(2, no, first["win1"], scale=gates[0][:, 1, :], gate_rows=1, finished=1, norm=norm)
        mixer(1, norm.no, moe_first - 2, lambda: Norm(8, gain_of(1, 1), shift(1, 1), turns=7, parts=False, joined=True))
        m_sel, m_gath, m_xg, m_gt, m_gtc, m_sg, m_h = (sem("m_" + n) for n in ("sel", "gath", "xg", "gt", "gtc", "sg", "h"))
        m_t, m_ht, m_oe, m_sc, m_y = (sem("m_" + n) for n in ("t", "ht", "oe", "sc", "y"))
        m_xhi, m_xlo, m_hlo = (sem("m_" + n) for n in ("xhi", "xlo", "hlo"))
        router_in = sem("router_in")
        routed = sem("routed")
        ranked = sem("ranked")
        r_exp = sem("r_exp")
        r_top = sem("r_top")
        slot_no = sb("slot_no", [P, 2, TT, EXPERTS])
        gate_w = sb("gate_w", [P, TT, EXPERTS])
        info = sb("info", [1, 3 * EXPERTS], I32)
        yacc = sb("yacc", [P, TT, D])
        E = EXPERTS
        with ExitStack() as stage:
            router = sb("router", [P, KT, E], stage=stage)
            lg = sb("lg", [P, TT, E], stage=stage)
            w3 = [sb(f"w3_{i}", [P, TT, E], stage=stage) for i in range(6)]
            m = sb("m", [P, 8, TT], stage=stage)
            cn = sb("cn", [P, 4, E], stage=stage)

            def moe_hi(act, n, j):
                slot = (moe_first + j) % RING
                act.wait_ge(arrived[slot], n * (16 * EXPERT_BLOCKS // RING) + 16 * ((moe_first + j) // RING + 1))
                act.wait_ge(used, n * EXPERT_BLOCKS + (moe_first + j - SPLITS + 1))
                nc.scalar.copy(split[0][:, (moe_first + j) % SPLITS, :], ring[:, slot, :]).then_inc(hi_ready, 1)

            def moe_lo(dve, n, j):
                at = (moe_first + j) % SPLITS
                dve.wait_ge(hi_ready, n * EXPERT_BLOCKS + (moe_first + j + 1))
                nc.vector.tensor_tensor(split[1][:, at, :], ring[:, (moe_first + j) % RING, :],
                                        split[0][:, at, :].bitcast(F32), ALU.subtract).then_inc(taken, 1)

            with nc.Block() as block:
                @block.sync
                def _(sp):
                    sp.dma_start(router[:], a["moe_router_2"][0].rearrange("(k p) n -> p k n", p=P)).then_inc(router_in, 16)

                @block.gpsimd
                def _(pool):
                    pool.memset(yacc[:], 0.0).then_inc(m_y, 4)

                @block.tensor
                def _(pe):
                    pe.wait_ge(router_in, 16)
                    for t in range(TT):
                        for k in range(KT):
                            ins = nc.tensor.matmul(pb[0][:, t * E:(t + 1) * E], AT[:, k, t * P:(t + 1) * P], router[:, k, :],
                                                   start=(k == 0), stop=(k == KT - 1))
                    ins.then_inc(routed, 1)
                    sel = w3[2]
                    pe.wait_ge(r_top, 2)
                    nc.tensor.matmul(pb[1][:, 0:E], const("before"), sel[:, 0, :], start=True, stop=True)
                    nc.tensor.matmul(pb[1][:, E:2 * E], const("before"), sel[:, 1, :], start=True, stop=False)
                    nc.tensor.matmul(pb[1][:, E:2 * E], const("ones"), sel[:, 0, :], start=False, stop=True)
                    nc.tensor.matmul(pb[1][:, 2 * E:3 * E], const("ones"), sel[:, 0, :], start=True, stop=False)
                    nc.tensor.matmul(pb[1][:, 2 * E:3 * E], const("ones"), sel[:, 1, :], start=False, stop=True).then_inc(ranked, 1)

                @block.scalar
                def _(act):
                    for j in range(SPLITS):
                        moe_hi(act, 0, j)
                    act.wait_ge(r_top, 1)
                    nc.scalar.activation(m[:, 4, :], m[:, 4, :], ACT.Exp).then_inc(r_exp, 1)

                @block.vector
                def _(dve):
                    L = lambda ins: dve_step.link(dve, ins)
                    ts, tt = nc.vector.tensor_scalar, nc.vector.tensor_tensor
                    wide = lambda z: z.rearrange("p (t a) -> p t a", a=1).broadcast_to([P, TT, E])
                    iota8 = const("iota8").rearrange("p (t e) -> p t e", t=TT)
                    dve.wait_ge(routed, 1)
                    L(nc.vector.tensor_copy(lg[:].rearrange("p t e -> p (t e)"), pb[0][:, 0:TT * E]))
                    for n in range(2):
                        s1, eq = w3[n], w3[3]
                        L(nc.vector.reduce_max(m[:, n, :], lg[:], AX))
                        L(tt(eq[:], lg[:], wide(m[:, n, :]), ALU.is_equal))
                        L(ts(eq[:], eq[:], -100.0, 100.0, ALU.mult, ALU.add))
                        L(tt(eq[:], eq[:], iota8, ALU.add))
                        L(nc.vector.tensor_reduce(m[:, 2 + n, :], eq[:], AX, ALU.min))
                        L(tt(s1[:], iota8, wide(m[:, 2 + n, :]), ALU.is_equal))
                        if n == 0:
                            L(nc.vector.scalar_tensor_tensor(lg[:], s1[:], -BIG, lg[:], ALU.mult, ALU.add))
                    tt(m[:, 4, :], m[:, 1, :], m[:, 0, :], ALU.subtract).then_inc(r_top, 1)
                    tt(w3[2][:], w3[0][:], w3[1][:], ALU.add).then_inc(r_top, 1)
                    for j in range(SPLITS):
                        moe_lo(dve, 0, j)
                    dve.wait_ge(r_exp, 1)
                    L(ts(m[:, 5, :], m[:, 4, :], 1.0, None, ALU.add))
                    L(nc.vector.reciprocal(m[:, 5, :], m[:, 5, :]))
                    L(tt(m[:, 6, :], m[:, 5, :], m[:, 4, :], ALU.mult))
                    dve_step.mark(tt(w3[0][:], w3[0][:], wide(m[:, 5, :]), ALU.mult))
                    L(tt(w3[1][:], w3[1][:], wide(m[:, 6, :]), ALU.mult))
                    L(tt(gate_w[:], w3[0][:], w3[1][:], ALU.add))
                    dve.wait_ge(ranked, 1)
                    L(ts(w3[4][:].rearrange("p t e -> p (t e)"), pb[1][:, 0:TT * E], 1.0, None, ALU.add))
                    L(tt(w3[4][:], w3[4][:], w3[2][:], ALU.mult))
                    for n in range(2):
                        dve_step.mark(ts(slot_no[:, n, :, :], w3[4][:], 1.0 + P * n, None, ALU.subtract))
                    L(ts(cn[:, 0, :], pb[1][:, 2 * E:3 * E], float(P), None, ALU.is_gt))
                    L(nc.vector.tensor_tensor_scan(cn[:, 1, :], const("ones", 0, E), cn[:, 0, :], 0.0, ALU.mult, ALU.add))
                    L(tt(cn[:, 2, :], cn[:, 1, :], cn[:, 0, :], ALU.subtract))
                    dve_step.mark(nc.vector.tensor_copy(info[0:1, 0:E], cn[0:1, 0, :]))
                    dve_step.mark(nc.vector.tensor_copy(info[0:1, E:2 * E], cn[0:1, 2, :]))
                    dve_step.mark(nc.vector.tensor_copy(info[0:1, 2 * E:3 * E], cn[0:1, 1, :]))

        with ExitStack() as stage:
            xg = sb("xg", [P, KT, P], stage=stage)
            Sel = sb("Sel", [P, TT, P], stage=stage)
            Gs = sb("Gs", [P, TT, P], stage=stage)
            GT = sb("GT", [P, T], stage=stage)
            sg = sb("msg", [P, 2, 512], stage=stage)
            hh = sb("mhh", [P, 2, 512], stage=stage)
            xp = [sb(z, [P, KT, P], F32R, stage) for z in ("xg_hi", "xg_lo")]
            hT = [sb(z, [P, 2, 512], F32R, stage) for z in ("hT_hi", "hT_lo")]
            oe = sb("moe", [P, D], stage=stage)
            first_use = {key: j for j, key in enumerate(order)}
            CH = CHUNKS

            def after(n, key):
                return n * EXPERT_BLOCKS + (moe_first + first_use[key] + 1)

            def arrival(eng, n, key):
                eng.wait_ge(taken, n * EXPERT_BLOCKS + (moe_first + first_use[key] + 1))

            def load(sp, e, n, j):
                src = expert_block(e, j)
                slot = (moe_first + j) % RING
                sp.wait_ge(taken, n * EXPERT_BLOCKS + (moe_first + j - RING + 1))
                sp.dma_start(slot_view(slot, src), src).then_inc(arrived[slot], 16)

            def gather(pe, n):
                pe.wait_ge(m_sel, n + 1)
                for b in range(2):
                    for k in range(4):
                        f = 4 * b + k
                        for t in range(TT):
                            ins = nc.tensor.matmul(pb[2 * b][:, k * P:(k + 1) * P], xn[:, t, f * P:(f + 1) * P], Sel[:, t, :],
                                                   start=(t == 0), stop=(t == 1))
                    ins.then_inc(m_gath, 1)

            def scatter(pe, s, t):
                if t == 0:
                    pe.wait_ge(m_oe, s * 2 + 2)
                for b in range(2):
                    if t:
                        pe.wait_ge(m_y, s * 4 + (5 + b))
                    nc.tensor.matmul(pb[6 + b][:], GT[:, t * P:(t + 1) * P], oe[:, b * 512:(b + 1) * 512],
                                     start=True, stop=True).then_inc(m_sc, 1)

            def pe_pass(pe, e, n, second, span, kind):
                if kind == "extra":
                    gather(pe, n)
                pe.wait_ge(m_xlo, n + 1)

                def up(name, c, bank):
                    for half in range(2):
                        arrival(pe, n, (name, c, half))
                        slot = slot_of[name, c, half]
                        for k in range(4):
                            for x, w in PARTS:
                                ins = nc.tensor.matmul(bank[:], xp[x][:, 4 * half + k, :], split[w][:, slot, k * 512:(k + 1) * 512],
                                                       start=(half == 0 and k == 0 and w + x == 0),
                                                       stop=(half == 1 and k == 3 and x == 1))
                        ins.then_inc(used, 1)

                for i in range(CH + 1):
                    if i < CH:
                        if i >= 2:
                            pe.wait_ge(m_sg, n * CH + (i - 1))
                        up("gate", i, pb[i % 2])
                    if i == 0 and kind != "extra":
                        scatter(pe, n, 0)
                    if i:
                        c = i - 1
                        pe.wait_ge(m_h, n * CH + i)
                        if c == 1:
                            pe.wait_ge(m_gtc, n + 1)
                        for q in range(4):
                            ins = nc.tensor.transpose(pb[4 + c % 2][:, q * P:(q + 1) * P], hh[:, c % 2, q * P:(q + 1) * P], ident)
                        ins.then_inc(m_t, 1)
                    if i < CH:
                        if i >= 2:
                            pe.wait_ge(m_h, n * CH + (i - 1))
                        up("up", i, pb[2 + i % 2])
                    if i == 0:
                        if kind != "extra":
                            scatter(pe, n, 1)
                        for t in range(TT):
                            ins = nc.tensor.transpose(pb[5][:, t * P:(t + 1) * P], Gs[:, t, :], ident)
                        ins.then_inc(m_gt, 1)
                    if i == CH and kind == "main":
                        gather(pe, n + 1)
                    if i:
                        if c == 0:
                            pe.wait_ge(m_y, n * 4 + 8)
                        pe.wait_ge(m_hlo, n * CH + i)
                        for half in range(2):
                            arrival(pe, n, ("down", c, half))
                            slot = slot_of["down", c, half]
                            for f in range(2):
                                q = 2 * half + f
                                for x, w in PARTS:
                                    for b in range(2):
                                        ins = nc.tensor.matmul(pb[6 + b][:], hT[x][:, c % 2, q * P:(q + 1) * P],
                                                               split[w][:, slot, f * D + b * 512:f * D + (b + 1) * 512],
                                                               start=(c == 0 and q == 0 and w + x == 0),
                                                               stop=(c == CH - 1 and q == 3 and x == 1))
                            ins.then_inc(used, 1)
                if kind != "main":
                    scatter(pe, n + 1, 0)
                    scatter(pe, n + 1, 1)

            def up_to(part, eng, n, span):
                left = list(range(*span))

                def go(j):
                    while left and left[0] < j:
                        part(eng, n, left.pop(0))
                return go

            def act_gathered(act, n):
                act.wait_ge(m_gath, n * 2 + 1)
                for k in range(4):
                    ins = nc.scalar.activation(xg[:, k, :], pb[0][:, k * P:(k + 1) * P], ACT.Identity,
                                               scale=gain_of(1, 1)(k), bias=shift(1, 1)(k))
                ins.then_inc(m_xg, 1)
                act.wait_ge(m_xg, n * 2 + 2)
                nc.scalar.copy(xp[0][:], xg[:]).then_inc(m_xhi, 1)

            def act_pass(act, e, n, second, span, kind):
                hi_to = up_to(moe_hi, act, n, span)
                if kind == "extra":
                    hi_to(SPLITS)
                    act_gathered(act, n)
                for i in range(CH + 1):
                    if i < CH:
                        hi_to(first_use["gate", i, 1] + 3)
                        act.wait_ge(used, after(n, ("gate", i, 1)))
                        if i >= 2:
                            act.wait_ge(m_h, n * CH + (i - 1))
                        nc.scalar.activation(sg[:, i % 2, :], pb[i % 2][:], ACT.Silu).then_inc(m_sg, 1)
                    if i:
                        c = i - 1
                        act.wait_ge(m_t, n * CH + i)
                        if c >= 2:
                            act.wait_ge(used, after(n, ("down", c - 2, 1)))
                        nc.scalar.copy(hT[0][:, c % 2, :], pb[4 + c % 2][:]).then_inc(m_ht, 1)
                    if i < CH:
                        hi_to(first_use["up", i, 1] + 3)
                    if i == 0:
                        act.wait_ge(m_gt, n + 1)
                        nc.scalar.copy(GT[:], pb[5][:, 0:T]).then_inc(m_gtc, 1)
                    if 0 < i < CH:
                        hi_to(first_use["down", i - 1, 1] + 3)
                hi_to(first_use["down", CH - 1, 1] + 2)
                if kind == "main":
                    act_gathered(act, n + 1)
                hi_to(first_use["down", CH - 1, 1] + 3)
                act.wait_ge(used, after(n, ("down", CH - 1, 1)))
                act.wait_ge(m_sc, n * 4 + 4)
                nc.scalar.copy(oe[:, 0:512], pb[6][:]).then_inc(m_oe, 1)
                hi_to(span[1])

            def select(dve, e, n, second):
                for t in range(TT):
                    s = slot_no[:, int(second), t, bass.ds(e, 1)]
                    nc.vector.tensor_scalar(Sel[:, t, :], const("iota"), s, None, ALU.is_equal)
                    ins = nc.vector.tensor_scalar(Gs[:, t, :], const("iota"), s, gate_w[:, t, bass.ds(e, 1)],
                                                  ALU.is_equal, ALU.mult)
                ins.then_inc(m_sel, 1)

            def dve_gathered(dve, n):
                dve.wait_ge(m_gath, n * 2 + 2)
                for k in range(4):
                    ins = nc.vector.tensor_scalar(xg[:, 4 + k, :], pb[2][:, k * P:(k + 1) * P], gain_of(1, 1)(4 + k),
                                                  shift(1, 1)(4 + k), ALU.mult, ALU.add)
                ins.then_inc(m_xg, 1)
                dve.wait_ge(m_xhi, n + 1)
                nc.vector.tensor_tensor(xp[1][:], xg[:], xp[0][:].bitcast(F32), ALU.subtract).then_inc(m_xlo, 1)

            def add_results(dve, s, t):
                if t == 0:
                    dve.wait_ge(m_y, s * 4 + 4)
                for b in range(2):
                    dve.wait_ge(m_sc, s * 4 + (2 * t + b + 1))
                    y = yacc[:, t, b * 512:(b + 1) * 512]
                    nc.vector.tensor_tensor(y, y, pb[6 + b][:], ALU.add).then_inc(m_y, 1)

            def dve_pass(dve, e, n, second, span, kind):
                lo_to = up_to(moe_lo, dve, n, span)
                if kind == "extra":
                    select(dve, e, n, second)
                    lo_to(SPLITS)
                    dve_gathered(dve, n)
                for i in range(CH + 1):
                    if i < CH:
                        lo_to(first_use["gate", i, 1] + 3)
                    if i == 0 and kind != "extra":
                        add_results(dve, n, 0)
                    if i:
                        c = i - 1
                        dve.wait_ge(m_ht, n * CH + i)
                        nc.vector.tensor_tensor(hT[1][:, c % 2, :], pb[4 + c % 2][:], hT[0][:, c % 2, :].bitcast(F32),
                                                ALU.subtract).then_inc(m_hlo, 1)
                    if i < CH:
                        lo_to(first_use["up", i, 1] + 3)
                        dve.wait_ge(m_sg, n * CH + (i + 1))
                        dve.wait_ge(used, after(n, ("up", i, 1)))
                        if i >= 2:
                            dve.wait_ge(m_t, n * CH + (i - 1))
                        nc.vector.tensor_tensor(hh[:, i % 2, :], sg[:, i % 2, :], pb[2 + i % 2][:], ALU.mult).then_inc(m_h, 1)
                    if i == 0 and kind != "extra":
                        add_results(dve, n, 1)
                    if i == 2 and kind == "main":
                        dve.wait_ge(m_gt, n + 1)
                        select(dve, e + 1, n + 1, False)
                    if 0 < i < CH:
                        lo_to(first_use["down", i - 1, 1] + 3)
                lo_to(first_use["down", CH - 1, 1] + 2)
                if kind == "main":
                    dve_gathered(dve, n + 1)
                lo_to(first_use["down", CH - 1, 1] + 3)
                dve.wait_ge(used, after(n, ("down", CH - 1, 1)))
                nc.vector.tensor_copy(oe[:, 512:D], pb[7][:]).then_inc(m_oe, 1)
                lo_to(span[1])
                if kind != "main":
                    add_results(dve, n + 1, 0)
                    add_results(dve, n + 1, 1)

            def second_passes(eng, one_pass):
                total = eng.value_load(info[0:1, 3 * E - 1:3 * E], min_val=0, max_val=E)
                with eng.If(total > 0):
                    with eng.Fori(0, E) as e:
                        over = eng.value_load(info[0:1, bass.ds(e, 1)], min_val=0, max_val=1)
                        with eng.If(over > 0):
                            rank = eng.value_load(info[0:1, bass.ds(e + E, 1)], min_val=0, max_val=E - 1)
                            one_pass(eng, e, rank + E, True, (0, EXPERT_BLOCKS), "extra")

            def sp_second(sp, e, n, second, span, kind):
                for j in range(EXPERT_BLOCKS):
                    load(sp, e, n, j)

            with nc.Block() as block:
                @block.sync
                def _(sp):
                    with sp.Fori(0, E - 1) as e:
                        for j in range(RING, EXPERT_BLOCKS):
                            load(sp, e, e, j)
                        for j in range(RING):
                            sp.wait_ge(taken, e * EXPERT_BLOCKS + (EXPERT_BLOCKS + moe_first + j - RING + 1))
                            src = expert_block(e + 1, j)
                            slot = (moe_first + j) % RING
                            sp.dma_start(slot_view(slot, src), src).then_inc(arrived[slot], 16)
                    for j in range(RING, EXPERT_BLOCKS):
                        load(sp, E - 1, E - 1, j)
                    second_passes(sp, sp_second)

                @block.gpsimd
                def _(pool):
                    pool.memset(oe[:], 0.0).then_inc(m_oe, 1)
                    pool.memset(GT[:], 0.0).then_inc(m_oe, 1)

                def all_passes(eng, one_pass):
                    with eng.Fori(0, E - 1) as e:
                        one_pass(eng, e, e, False, (SPLITS, EXPERT_BLOCKS + SPLITS), "main")
                    one_pass(eng, E - 1, E - 1, False, (SPLITS, EXPERT_BLOCKS), "last")
                    second_passes(eng, one_pass)

                @block.tensor
                def _(pe):
                    gather(pe, 0)
                    all_passes(pe, pe_pass)

                @block.scalar
                def _(act):
                    act_gathered(act, 0)
                    all_passes(act, act_pass)

                @block.vector
                def _(dve):
                    select(dve, 0, 0, False)
                    dve_gathered(dve, 0)
                    all_passes(dve, dve_pass)

            with nc.Block() as block:
                @block.vector
                def _(dve):
                    for t in range(TT):
                        dve_step.mark(nc.vector.tensor_tensor(yacc[:, t, :], yacc[:, t, :], gates[1][:, 1, :], ALU.mult))
                    dve_step.wait(dve)
                    nc.vector.tensor_tensor(resid[:], resid[:], yacc[:], ALU.add)
        norm_rows(9, a["final_g_2"].rearrange("(a d) -> a d", a=1))
        return finish()


_OUT = (1, T, D)


def kernel(**inputs):
    from concourse import bacc
    from concourse.bass_utils import run_bass_kernel_spmd

    nc = bacc.Bacc("TRN2", target_bir_lowering=False, num_devices=1)
    arrays, args = {}, {}
    for name, x in {**inputs, "consts": CONSTS}.items():
        x = np.ascontiguousarray(x)
        arrays[f"in_{name}"] = x
        args[name] = nc.dram_tensor(f"in_{name}", x.shape, mybir.dt.from_np(x.dtype), kind="ExternalInput").ap()
    out = nc.dram_tensor("out", _OUT, F32, kind="ExternalOutput").ap()
    build(nc, args, out)
    return run_bass_kernel_spmd(nc, [arrays], core_ids=[0]).results[0]["out"]
```
